# Optimizing a Trainium2 kernel written in Bass

```python
import jax, jax.numpy as jnp
from jax import lax
import numpy as np

D_MODEL = 1024
BATCH = 1
SEQ = 512
DEPTH = 1

GDN_HEADS = 8
GDN_DK = 128
GDN_DV = 128
GDN_CONV = 4
GDN_CHUNK = 64
FOX_HEADS = 8
FOX_DH = 128
FOX_BLOCK = 128
D_FF = 4 * D_MODEL
EPS = 1e-6

GDN_QK_W = GDN_HEADS * GDN_DK
GDN_V_W = GDN_HEADS * GDN_DV
FOX_W = FOX_HEADS * FOX_DH
IN_SPLITS = (GDN_QK_W, GDN_QK_W, GDN_V_W, GDN_V_W, GDN_HEADS, GDN_HEADS,
             FOX_W, FOX_W, FOX_W, FOX_HEADS, D_MODEL, D_MODEL)
N_IN = sum(IN_SPLITS)


def rmsnorm(x, g):
    xf = x.astype(jnp.float32)
    y = xf * lax.rsqrt(jnp.mean(xf * xf, axis=-1, keepdims=True) + EPS)
    return (y * g.astype(jnp.float32)).astype(x.dtype)

def l2norm(x):
    xf = x.astype(jnp.float32)
    return xf * lax.rsqrt(jnp.sum(xf * xf, axis=-1, keepdims=True) + EPS)

def to_heads(x, n_heads):
    b, t, w = x.shape
    return x.reshape(b, t, n_heads, w // n_heads).transpose(0, 2, 1, 3)

def causal_depthwise_conv(x, w):
    k_width = w.shape[0]
    t = x.shape[1]
    xp = jnp.pad(x, ((0, 0), (k_width - 1, 0), (0, 0)))
    y = xp[:, 0:t] * w[0]
    for i in range(1, k_width):
        y = y + xp[:, i:i + t] * w[i]
    return y

def gated_delta_rule_chunked(q, k, v, g, beta):
    b, h, t, dk = q.shape
    dv = v.shape[-1]
    c = GDN_CHUNK
    n = t // c
    q = q.reshape(b, h, n, c, dk)
    k = k.reshape(b, h, n, c, dk)
    v = v.reshape(b, h, n, c, dv)
    g = g.reshape(b, h, n, c)
    beta = beta.reshape(b, h, n, c)

    G = jnp.cumsum(g, axis=-1)
    diff = G[..., :, None] - G[..., None, :]
    tri_incl = jnp.tril(jnp.ones((c, c), dtype=bool))
    tri_strict = jnp.tril(jnp.ones((c, c), dtype=bool), -1)
    decay = jnp.where(tri_incl, jnp.exp(jnp.where(tri_incl, diff, 0.0)), 0.0)

    kk = jnp.einsum('bhncd,bhnsd->bhncs', k, k)
    a_mat = jnp.where(tri_strict, beta[..., None] * kk * decay, 0.0)
    eye = jnp.eye(c, dtype=jnp.float32)
    rhs = jnp.concatenate([v * beta[..., None], k * (beta * jnp.exp(G))[..., None]], axis=-1)
    a_full = jnp.broadcast_to(a_mat + eye, (b, h, n, c, c))
    sol = lax.linalg.triangular_solve(a_full, rhs, left_side=True, lower=True,
                                      unit_diagonal=True)
    value, k_cum = sol[..., :dv], sol[..., dv:]

    attn_intra = jnp.einsum('bhncd,bhnsd->bhncs', q, k) * decay
    q_dec = q * jnp.exp(G)[..., None]
    g_last = G[..., -1:]
    k_dec = k * jnp.exp(g_last - G)[..., None]
    chunk_decay = jnp.exp(g_last[..., 0])

    def step(s, inp):
        value_c, kcum_c, attn_c, qdec_c, kdec_c, dec_c = inp
        v_new = value_c - jnp.einsum('bhcd,bhde->bhce', kcum_c, s)
        o = (jnp.einsum('bhcd,bhde->bhce', qdec_c, s)
             + jnp.einsum('bhcs,bhse->bhce', attn_c, v_new))
        s = s * dec_c[..., None, None] + jnp.einsum('bhcd,bhce->bhde', kdec_c, v_new)
        return s, o

    xs = tuple(jnp.moveaxis(a, 2, 0) for a in (value, k_cum, attn_intra, q_dec, k_dec, chunk_decay))
    s0 = jnp.zeros((b, h, dk, dv), jnp.float32)
    _, o = lax.scan(step, s0, xs)
    return jnp.moveaxis(o, 0, 2).reshape(b, h, t, dv)

def forgetting_attention(q, k, v, log_f):
    t = q.shape[2]
    cum = jnp.cumsum(log_f, axis=-1)
    scale = FOX_DH ** -0.5
    outs = []
    for i in range(t // FOX_BLOCK):
        q0 = i * FOX_BLOCK
        q1 = q0 + FOX_BLOCK
        s = (jnp.einsum('bhqd,bhkd->bhqk', q[:, :, q0:q1], k[:, :, :q1]) * scale
             + cum[:, :, q0:q1, None] - cum[:, :, None, :q1])
        mask = (q0 + jnp.arange(FOX_BLOCK))[:, None] >= jnp.arange(q1)[None, :]
        p = jax.nn.softmax(jnp.where(mask, s, -jnp.inf), axis=-1)
        outs.append(jnp.einsum('bhqk,bhkd->bhqd', p, v[:, :, :q1]))
    return jnp.concatenate(outs, axis=2)

def first_inputs(seed: int = 0) -> dict:
    key = jax.random.key(seed)
    ks = jax.random.split(key, 20)
    f32 = jnp.float32

    def nrm(k, shape, fan_in):
        return jax.random.normal(k, shape, f32) * (fan_in ** -0.5)

    def gain(k, shape):
        return 1.0 + 0.02 * jax.random.normal(k, shape, f32)

    dt = jnp.exp(jax.random.uniform(ks[5], (DEPTH, GDN_HEADS), f32,
                                    minval=float(np.log(1e-3)), maxval=float(np.log(1e-1))))
    return {
        "x": jax.random.normal(ks[0], (BATCH, SEQ, D_MODEL), f32),
        "norm_mix_g": gain(ks[1], (DEPTH, D_MODEL)),
        "w_in": nrm(ks[2], (DEPTH, D_MODEL, N_IN), D_MODEL),
        "gdn_conv_w": nrm(ks[3], (DEPTH, GDN_CONV, 2 * GDN_QK_W + GDN_V_W), GDN_CONV),
        "gdn_a_log": jnp.log(jax.random.uniform(ks[4], (DEPTH, GDN_HEADS), f32, minval=1.0, maxval=16.0)),
        "gdn_dt_bias": dt + jnp.log(-jnp.expm1(-dt)),
        "gdn_norm_g": gain(ks[6], (DEPTH, GDN_DV)),
        "fox_q_norm_g": gain(ks[7], (DEPTH, FOX_DH)),
        "fox_k_norm_g": gain(ks[8], (DEPTH, FOX_DH)),
        "fox_f_bias": jax.random.uniform(ks[9], (DEPTH, FOX_HEADS), f32, minval=2.0, maxval=6.0),
        "w_proj_gdn": nrm(ks[10], (DEPTH, GDN_V_W, D_MODEL), GDN_V_W),
        "w_proj_fox": nrm(ks[11], (DEPTH, FOX_W, D_MODEL), FOX_W),
        "w_out": nrm(ks[12], (DEPTH, D_MODEL, D_MODEL), D_MODEL),
        "norm_mlp_g": gain(ks[13], (DEPTH, D_MODEL)),
        "w_up": nrm(ks[14], (DEPTH, D_MODEL, D_FF), D_MODEL),
        "w_down": nrm(ks[15], (DEPTH, D_FF, D_MODEL), D_FF),
    }

def first_block(x, norm_mix_g, w_in, gdn_conv_w, gdn_a_log, gdn_dt_bias, gdn_norm_g,
              fox_q_norm_g, fox_k_norm_g, fox_f_bias, w_proj_gdn, w_proj_fox, w_out,
              norm_mlp_g, w_up, w_down):
    f32 = jnp.float32
    b, t, _ = x.shape
    split_idx = [int(i) for i in np.cumsum(IN_SPLITS)[:-1]]
    for l in range(DEPTH):
        u = rmsnorm(x, norm_mix_g[l])
        proj = u @ w_in[l]
        (gq, gk, gv, gz, ga, gb, fq, fk, fv, ff, gate_a, gate_b) = jnp.split(proj, split_idx, axis=-1)

        qkv = jax.nn.silu(causal_depthwise_conv(jnp.concatenate([gq, gk, gv], axis=-1), gdn_conv_w[l]))
        cq, ck, cv = jnp.split(qkv, [GDN_QK_W, 2 * GDN_QK_W], axis=-1)
        qh = l2norm(to_heads(cq, GDN_HEADS)) * (GDN_DK ** -0.5)
        kh = l2norm(to_heads(ck, GDN_HEADS))
        vh = to_heads(cv, GDN_HEADS).astype(f32)
        beta = jax.nn.sigmoid(gb.astype(f32)).transpose(0, 2, 1)
        g = (-jnp.exp(gdn_a_log[l].astype(f32))
             * jax.nn.softplus(ga.astype(f32) + gdn_dt_bias[l].astype(f32))).transpose(0, 2, 1)
        o_a = gated_delta_rule_chunked(qh, kh, vh, g, beta).transpose(0, 2, 1, 3)
        z = gz.reshape(b, t, GDN_HEADS, GDN_DV).astype(f32)
        o_a = rmsnorm(o_a, gdn_norm_g[l]) * jax.nn.silu(z)
        y_a = o_a.reshape(b, t, GDN_V_W).astype(x.dtype) @ w_proj_gdn[l]

        fqh = rmsnorm(to_heads(fq, FOX_HEADS), fox_q_norm_g[l]).astype(f32)
        fkh = rmsnorm(to_heads(fk, FOX_HEADS), fox_k_norm_g[l]).astype(f32)
        fvh = to_heads(fv, FOX_HEADS).astype(f32)
        log_f = jax.nn.log_sigmoid(ff.astype(f32) + fox_f_bias[l].astype(f32)).transpose(0, 2, 1)
        o_b = forgetting_attention(fqh, fkh, fvh, log_f).transpose(0, 2, 1, 3)
        y_b = o_b.reshape(b, t, FOX_W).astype(x.dtype) @ w_proj_fox[l]

        merged = jax.nn.sigmoid(gate_a) * y_a + jax.nn.sigmoid(gate_b) * y_b
        h = x + merged @ w_out[l]

        hn = rmsnorm(h, norm_mlp_g[l])
        x = h + jnp.square(jax.nn.relu(hn @ w_up[l])) @ w_down[l]
    return x


RET_HEADS = 4
RET_QK_DIM = 128
RET_V_DIM = 256
RET_CHUNK = 128
ATTN_Q_HEADS = 16
ATTN_KV_HEADS = 2
ATTN_HEAD_DIM = 64
WINDOW = 128
ATTN_BLOCK = 128
D_FF_2 = -(-8 * D_MODEL // (3 * 256)) * 256
ROPE_THETA = 10000.0

RET_QK = RET_HEADS * RET_QK_DIM
RET_V = RET_HEADS * RET_V_DIM
ATTN_Q = ATTN_Q_HEADS * ATTN_HEAD_DIM
ATTN_KV = ATTN_KV_HEADS * ATTN_HEAD_DIM
SPLITS = [RET_QK, RET_QK, RET_V, RET_V, ATTN_Q, ATTN_KV, ATTN_KV, D_MODEL, D_MODEL]
D_IN = sum(SPLITS)
SPLIT_IDX = [int(v) for v in np.cumsum(SPLITS)[:-1]]


def rms_norm(x, g):
    xf = x.astype(jnp.float32)
    y = xf * lax.rsqrt(jnp.mean(xf * xf, axis=-1, keepdims=True) + EPS)
    return (y * g.astype(jnp.float32)).astype(x.dtype)

def rotary(x, pos):
    d = x.shape[-1]
    half = d // 2
    inv_freq = ROPE_THETA ** (-jnp.arange(half, dtype=jnp.float32) / half)
    ang = pos.astype(jnp.float32)[:, None] * inv_freq[None, :]
    cos = jnp.cos(ang)[None, :, None, :]
    sin = jnp.sin(ang)[None, :, None, :]
    xf = x.astype(jnp.float32)
    x1, x2 = xf[..., :half], xf[..., half:]
    out = jnp.concatenate([x1 * cos - x2 * sin, x2 * cos + x1 * sin], axis=-1)
    return out.astype(x.dtype)

def retention_chunkwise(q, k, v):
    B, S, H, dk = q.shape
    dv = v.shape[-1]
    C = RET_CHUNK
    N = S // C
    log_gamma = jnp.log1p(-jnp.exp2(-5.0 - jnp.arange(H, dtype=jnp.float32)))
    idx = jnp.arange(C, dtype=jnp.float32)
    rel = idx[:, None] - idx[None, :]
    intra_decay = jnp.where(rel[None] >= 0,
                            jnp.exp(log_gamma[:, None, None] * jnp.maximum(rel, 0.0)[None]), 0.0)
    q_decay = jnp.exp(log_gamma[:, None] * (idx + 1.0))[None, :, :, None]
    k_decay = jnp.exp(log_gamma[:, None] * (C - 1.0 - idx))[None, :, :, None]
    chunk_decay = jnp.exp(log_gamma * C)[None, :, None, None]

    qf = q.astype(jnp.float32) * (dk ** -0.5)
    kf = k.astype(jnp.float32)
    vf = v.astype(jnp.float32)
    to_chunks = lambda t: t.reshape(B, N, C, H, t.shape[-1]).transpose(1, 0, 3, 2, 4)
    qc, kc, vc = to_chunks(qf), to_chunks(kf), to_chunks(vf)

    def step(state, inp):
        qn, kn, vn = inp
        scores = jnp.einsum('bhcd,bhsd->bhcs', qn, kn) * intra_decay
        inner = jnp.einsum('bhcs,bhse->bhce', scores, vn)
        cross = jnp.einsum('bhcd,bhde->bhce', qn, state) * q_decay
        new_state = state * chunk_decay + jnp.einsum('bhsd,bhse->bhde', kn * k_decay, vn)
        return new_state, inner + cross

    state0 = jnp.zeros((B, H, dk, dv), jnp.float32)
    _, out = lax.scan(step, state0, (qc, kc, vc))
    return out.transpose(1, 0, 3, 2, 4).reshape(B, S, H, dv)

def head_group_norm(y, g):
    B, S, H, dv = y.shape
    mu = jnp.mean(y, axis=-1, keepdims=True)
    yc = y - mu
    var = jnp.mean(yc * yc, axis=-1, keepdims=True)
    yn = (yc * lax.rsqrt(var + EPS)).reshape(B, S, H * dv)
    return yn * g.astype(jnp.float32)

def sliding_window_sink_attention(q, k, v, sinks):
    B, S, Hq, d = q.shape
    Hkv = k.shape[2]
    G = Hq // Hkv
    C = ATTN_BLOCK
    N = S // C
    qb = q.reshape(B, N, C, Hkv, G, d)
    pad = ((0, 0), (C, 0), (0, 0), (0, 0))
    kp = jnp.pad(k, pad).reshape(B, N + 1, C, Hkv, d)
    vp = jnp.pad(v, pad).reshape(B, N + 1, C, Hkv, d)
    kb = jnp.concatenate([kp[:, :-1], kp[:, 1:]], axis=2)
    vb = jnp.concatenate([vp[:, :-1], vp[:, 1:]], axis=2)
    scores = jnp.einsum('bnqhgd,bnkhd->bnhgqk', qb, kb).astype(jnp.float32) * (d ** -0.5)
    qi = jnp.arange(C)[:, None]
    kj = jnp.arange(2 * C)[None, :]
    rel = C + qi - kj
    key_pos = jnp.arange(N)[:, None, None] * C + kj[None] - C
    mask = (rel[None] >= 0) & (rel[None] < WINDOW) & (key_pos >= 0)
    scores = jnp.where(mask[None, :, None, None], scores, -1e30)
    sink = sinks.astype(jnp.float32).reshape(1, 1, Hkv, G, 1, 1)
    m = jnp.maximum(jnp.max(scores, axis=-1, keepdims=True), sink)
    e = jnp.exp(scores - m)
    probs = e / (jnp.sum(e, axis=-1, keepdims=True) + jnp.exp(sink - m))
    out = jnp.einsum('bnhgqk,bnkhd->bnqhgd', probs.astype(v.dtype), vb)
    return out.reshape(B, S, Hq, d)

def second_inputs(seed: int = 0) -> dict:
    key = jax.random.key(seed)
    ks = jax.random.split(key, 16)
    nrm = lambda k, shape, fan_in: jax.random.normal(k, shape, jnp.float32) * (fan_in ** -0.5)
    gain = lambda k, shape: 1.0 + 0.02 * jax.random.normal(k, shape, jnp.float32)
    return {
        "x": jax.random.normal(ks[0], (BATCH, SEQ, D_MODEL), jnp.float32),
        "ln1_g": gain(ks[1], (DEPTH, D_MODEL)),
        "w_in": nrm(ks[2], (DEPTH, D_MODEL, D_IN), D_MODEL),
        "b_in": 0.02 * jax.random.normal(ks[3], (DEPTH, D_IN), jnp.float32),
        "ret_norm_g": gain(ks[4], (DEPTH, RET_V)),
        "w_ret_out": nrm(ks[5], (DEPTH, RET_V, D_MODEL), RET_V),
        "attn_sinks": 0.5 * jax.random.normal(ks[6], (DEPTH, ATTN_Q_HEADS), jnp.float32),
        "w_attn_out": nrm(ks[7], (DEPTH, ATTN_Q, D_MODEL), ATTN_Q),
        "w_out": nrm(ks[8], (DEPTH, D_MODEL, D_MODEL), D_MODEL),
        "ln2_g": gain(ks[9], (DEPTH, D_MODEL)),
        "w_ffn_gate": nrm(ks[10], (DEPTH, D_MODEL, D_FF_2), D_MODEL),
        "w_ffn_up": nrm(ks[11], (DEPTH, D_MODEL, D_FF_2), D_MODEL),
        "w_ffn_down": nrm(ks[12], (DEPTH, D_FF_2, D_MODEL), D_FF_2),
        "lnf_g": gain(ks[13], (D_MODEL,)),
    }

def second_block(x, ln1_g, w_in, b_in, ret_norm_g, w_ret_out, attn_sinks, w_attn_out, w_out,
              ln2_g, w_ffn_gate, w_ffn_up, w_ffn_down, lnf_g):
    B, S, _ = x.shape
    pos = jnp.arange(S, dtype=jnp.int32)
    for l in range(DEPTH):
        h = rms_norm(x, ln1_g[l])
        proj = h @ w_in[l] + b_in[l]
        rq, rk, rv, rg, aq, ak, av, gate_a, gate_b = jnp.split(proj, SPLIT_IDX, axis=-1)

        rq = rotary(rq.reshape(B, S, RET_HEADS, RET_QK_DIM), pos)
        rk = rotary(rk.reshape(B, S, RET_HEADS, RET_QK_DIM), pos)
        ry = retention_chunkwise(rq, rk, rv.reshape(B, S, RET_HEADS, RET_V_DIM))
        ry = head_group_norm(ry, ret_norm_g[l]).astype(x.dtype)
        branch_a = (jax.nn.silu(rg) * ry) @ w_ret_out[l]

        aq = rotary(aq.reshape(B, S, ATTN_Q_HEADS, ATTN_HEAD_DIM), pos)
        ak = rotary(ak.reshape(B, S, ATTN_KV_HEADS, ATTN_HEAD_DIM), pos)
        ay = sliding_window_sink_attention(aq, ak, av.reshape(B, S, ATTN_KV_HEADS, ATTN_HEAD_DIM),
                                           attn_sinks[l])
        branch_b = ay.reshape(B, S, ATTN_Q) @ w_attn_out[l]

        merged = jax.nn.sigmoid(gate_a) * branch_a + jax.nn.sigmoid(gate_b) * branch_b
        x = x + merged @ w_out[l]

        h2 = rms_norm(x, ln2_g[l])
        x = x + (jax.nn.silu(h2 @ w_ffn_gate[l]) * (h2 @ w_ffn_up[l])) @ w_ffn_down[l]
    return rms_norm(x, lnf_g)


def setup_inputs(seed=0):
    out = dict(first_inputs(seed))
    for name, value in second_inputs(seed + 1).items():
        if name != "x":
            out[name + "_2"] = value
    return out


def reference(
    x, norm_mix_g, w_in, gdn_conv_w, gdn_a_log, gdn_dt_bias, gdn_norm_g, fox_q_norm_g,
    fox_k_norm_g, fox_f_bias, w_proj_gdn, w_proj_fox, w_out, norm_mlp_g, w_up, w_down, ln1_g_2,
    w_in_2, b_in_2, ret_norm_g_2, w_ret_out_2, attn_sinks_2, w_attn_out_2, w_out_2, ln2_g_2,
    w_ffn_gate_2, w_ffn_up_2, w_ffn_down_2, lnf_g_2,
):
    x = first_block(
        x, norm_mix_g, w_in, gdn_conv_w, gdn_a_log, gdn_dt_bias, gdn_norm_g, fox_q_norm_g,
        fox_k_norm_g, fox_f_bias, w_proj_gdn, w_proj_fox, w_out, norm_mlp_g, w_up, w_down,
    )
    return second_block(
        x, ln1_g_2, w_in_2, b_in_2, ret_norm_g_2, w_ret_out_2, attn_sinks_2, w_attn_out_2,
        w_out_2, ln2_g_2, w_ffn_gate_2, w_ffn_up_2, w_ffn_down_2, lnf_g_2,
    )


_drawn_inputs = setup_inputs


def setup_inputs(seed=0):
    import zlib

    import numpy as np

    out = dict(_drawn_inputs(seed))
    spreads = {}
    factors = {'norm_mix_g': 3.9,
     'gdn_norm_g': 7.448,
     'fox_q_norm_g': 8.0,
     'fox_k_norm_g': 8.0,
     'norm_mlp_g': 2.804,
     'ln1_g_2': 5.96,
     'b_in_2': 3.689,
     'ret_norm_g_2': 24.643,
     'attn_sinks_2': 200.0,
     'ln2_g_2': 17.281,
     'lnf_g_2': 21.591}
    for name, (base, spread) in spreads.items():
        noise = np.random.default_rng([zlib.crc32(name.encode()), seed]).standard_normal(out[name].shape)
        drawn = base * np.exp(spread * noise) if base else spread * noise
        out[name] = __import__('jax').numpy.asarray(drawn.astype(out[name].dtype))
    for name, factor in factors.items():
        out[name] = (out[name] * factor).astype(out[name].dtype)
    return out
```

```python
from contextlib import ExitStack

import numpy as np

import concourse.bass as bass
from concourse import mybir
from concourse.alu_op_type import AluOpType as ALU

ACT = mybir.ActivationFunctionType
AX = mybir.AxisListType
F32 = mybir.dt.float32
F32R = mybir.dt.float32r

P = 128
T = 512
NT = T // P
D = 1024
KT = D // P
EPS = 1e-6
HEADS = 8
LEVELS = 7
SCALE = float(P) ** -0.5
SLOTS = 4
DVE_STEPS = 28
LEAD = 2

RET_HEADS = 4
FF2_TILES = 22
KiB = 1024


def slab_order():
    order = []
    q, k, v, z = 0, D, 2 * D, 3 * D
    fq = 4 * D + 16
    fk, fv = fq + D, fq + 2 * D
    gate_a = fq + 3 * D + 8
    gate_b = gate_a + D
    for h in range(HEADS):
        order += [("w_in", 0, KT, base + h * P) for base in (q, k, v, z, fq, fk, fv)]
    for m in range(KT):
        order += [("w_in", 0, KT, gate_a + m * P), ("w_in", 0, KT, gate_b + m * P),
                  ("w_proj_gdn", 0, KT, m * P), ("w_proj_fox", 0, KT, m * P)]
    order += [("w_out", 0, KT, m * P) for m in range(KT)]
    for part in range(4):
        order += [("w_up", 0, KT, (8 * part + j) * P) for j in range(8)]
        order += [("w_down", 8 * part, KT, m * P) for m in range(KT)]
    rq, rk, rv, rg, aq, ak, av, ga = 0, 512, 1024, 2048, 3072, 4096, 4224, 4352
    order += [("w_in_2", 0, KT, ak), ("w_in_2", 0, KT, av)]
    for r in range(RET_HEADS):
        order += [("w_in_2", 0, KT, c) for c in (
            rq + r * P, rk + r * P, rv + 2 * r * P, rv + (2 * r + 1) * P,
            aq + 2 * r * P, aq + (2 * r + 1) * P, rg + 2 * r * P, rg + (2 * r + 1) * P)]
    for m in range(KT):
        order += [("w_in_2", 0, KT, ga + m * P), ("w_in_2", 0, KT, ga + D + m * P),
                  ("w_ret_out_2", 0, KT, m * P), ("w_attn_out_2", 0, KT, m * P)]
    order += [("w_out_2", 0, KT, m * P) for m in range(KT)]
    for part in range(3):
        n = min(8, FF2_TILES - 8 * part)
        for j in range(n):
            order += [("w_ffn_gate_2", 0, KT, (8 * part + j) * P), ("w_ffn_up_2", 0, KT, (8 * part + j) * P)]
        order += [("w_ffn_down_2", 8 * part, n, m * P) for m in range(KT)]
    return order


N_SLABS = len(slab_order()) + LEAD


class Phase:

    def __init__(self, n, iters, before=None):
        self.n, self.iters = n, iters
        self.first = before.end if before else 0
        self.uses0 = before.uses_end if before else [0] * SLOTS
        self.last0 = before.last_end if before else [None] * SLOTS
        self.per = [len([j for j in range(n) if j % SLOTS == s]) for s in range(SLOTS)]
        self.end = self.first + n * iters
        self.uses_end = [u + p * iters for u, p in zip(self.uses0, self.per)]
        self.last_end = [self.first + n * (iters - 1) + max(j for j in range(n) if j % SLOTS == s)
                         if p else self.last0[s] for s, p in zip(range(SLOTS), self.per)]

    def slot(self, j):
        return (j % self.n) % SLOTS

    def index(self, i, j):
        return self.first + i * self.n + j

    def landed(self, i, j):
        wrap, j = divmod(j, self.n)
        s = j % SLOTS
        return ((i + wrap) * self.per[s] + (self.uses0[s] + j // SLOTS + 1)) * 16

    def back(self, j):
        wrap, j0 = divmod(j, self.n)
        s = j0 % SLOTS
        dist = []
        if j0 >= SLOTS:
            return SLOTS
        if self.iters > 1 or wrap:
            dist.append(self.n + j0 - max(x for x in range(self.n) if x % SLOTS == s))
        if not wrap and self.last0[s] is not None:
            dist.append(self.first + j0 - self.last0[s])
        return min(dist) if dist else None


def program(nc, dram, out):
    order = slab_order()
    ph_heads = Phase(7, HEADS)
    ph_merge1 = Phase(4, KT, ph_heads)
    ph_out1 = Phase(8, 1, ph_merge1)
    ph_mlp = Phase(16, 4, ph_out1)
    ph_kv = Phase(10, 1, ph_mlp)
    ph_ret = Phase(8, RET_HEADS - 1, ph_kv)
    ph_merge2 = Phase(4, KT, ph_ret)
    ph_out2 = Phase(8, 1, ph_merge2)
    ph_ffn = Phase(24, 2, ph_out2)
    ph_ffn_end = Phase(20, 1, ph_ffn)
    phases = [ph_heads, ph_merge1, ph_out1, ph_mlp, ph_kv, ph_ret, ph_merge2, ph_out2, ph_ffn, ph_ffn_end]
    assert ph_ffn_end.end == len(order)

    with ExitStack() as ctx:
        def at(name, shape, offset, dt=F32):
            n = 4
            for s in shape[1:]:
                n *= s
            assert offset + n <= LIMIT, name
            return nc.alloc_sbuf_tensor_at(name, shape, dt, offset=BASE + offset)

        BASE, LIMIT = 16 * KiB + 256, 207 * KiB
        ctx.enter_context(nc.sbuf_tensor("arena", [P, (128 + LIMIT) // 4], F32))

        class Bump:

            def __init__(self, start, end):
                self.at, self.end = start, end

            def __call__(self, name, shape, dt=F32):
                n = 4
                for s in shape[1:]:
                    n *= s
                t = at(name, shape, self.at, dt)
                self.at += (n + 31) // 32 * 32
                assert self.at <= self.end, (name, self.at, self.end)
                return t

        raw = [at(f"slab_raw{s}", [P, KT, P], s * 4 * KiB) for s in range(SLOTS)]
        w_hi = [at(f"slab_hi{s}", [P, KT, P], (16 + 4 * s) * KiB, F32R) for s in range(SLOTS)]
        w_lo = [at(f"slab_lo{s}", [P, KT, P], (32 + 4 * s) * KiB, F32R) for s in range(SLOTS)]
        u_hi = at("u_hi", [P, KT, T], 48 * KiB, F32R)
        u_lo = at("u_lo", [P, KT, T], 64 * KiB, F32R)
        br_a = at("branch_a", [P, KT, T], 80 * KiB)
        br_b = at("branch_b", [P, KT, T], 96 * KiB)
        m_hi = at("merged_hi", [P, KT, T], 80 * KiB, F32R)
        m_lo = at("merged_lo", [P, KT, T], 96 * KiB, F32R)
        a_hi = at("branch_a_hi", [P, KT, T], 112 * KiB, F32R)
        a_lo = at("branch_a_lo", [P, KT, T], 128 * KiB, F32R)
        b_hi = at("branch_b_hi", [P, KT, T], 144 * KiB, F32R)
        b_lo = at("branch_b_lo", [P, KT, T], 160 * KiB, F32R)
        y_hi = at("hidden_hi", [P, 8, T], 112 * KiB, F32R)
        y_lo = at("hidden_lo", [P, 8, T], 128 * KiB, F32R)
        tmp = [at(f"tmp{n}", [P, T], (144 + 2 * n) * KiB) for n in range(8)]
        mtmp = [at(f"mtmp{n}", [P, T], (192 + 2 * n) * KiB) for n in range(2)]
        h_res = at("residual", [P, KT, T], 176 * KiB)

        small = Bump(196 * KiB, LIMIT)
        ident = small("ident", [P, P])
        ones = small("ones", [P, P])
        mhalf = small("minus_half", [P, 16])
        gains = small("gains", [P, 5, KT])
        sq_sum = small("sq_sum", [P, T])
        r_row = small("r_row", [P, T])
        r_diag = small("r_diag", [P, NT, P])
        ms_col = small("ms_col", [P, NT])
        r_col = small("r_col", [P, NT])
        head_gain = small("head_gain", [P, 3])

        ps = [ctx.enter_context(nc.psum_tensor(f"bank{n}", [P, T], F32)) for n in range(8)]
        bank_slab = ps[0:2]
        bA, bB, bC, bD, bE, bF = ps[2:8]

        sems = {}

        def sem(name):
            if name not in sems:
                sems[name] = ctx.enter_context(nc.semaphore(name))
            return sems[name]

        s_raw = [sem(f"slab_landed{s}") for s in range(SLOTS)]
        s_hi, s_lo, s_used = sem("slab_hi"), sem("slab_lo"), sem("slab_used")
        s_taken = sem("slab_taken")

        def c4(ap):
            return ap.rearrange("p (n c) -> p n c", n=NT)

        def over_cols(ap):
            return ap.unsqueeze(2).to_broadcast([P, NT, P])

        def over_tiles(ap):
            return ap.unsqueeze(1).to_broadcast([P, NT, P])

        def wait_slab(eng, s, ph, i, j):
            back = ph.back(j)
            value = None if back is None else ph.index(i, j) - back + 1
            if value is not None and not (isinstance(value, int) and value <= 0):
                eng.wait_ge(s, value)

        def load_slab(sp, ph, i, j):
            wait_slab(sp, s_lo, ph, i, j)
            s = ph.slot(j)
            src = dram["slabs"][bass.ds(ph.index(i, j), 1), :, :].rearrange("a p n -> (a p) n")
            sp.dma_start(raw[s][:].rearrange("p k c -> p (k c)"), src).then_inc(s_raw[s], 16)

        def split_hi(act, ph, i, j):
            s = ph.slot(j)
            wait_slab(act, s_used, ph, i, j)
            act.wait_ge(s_raw[s], ph.landed(i, j))
            act.copy(w_hi[s][:], raw[s][:]).then_inc(s_hi, 1)

        def split_lo(pool, ph, i, j):
            s = ph.slot(j)
            pool.wait_ge(s_hi, ph.index(i, j) + 1)
            pool.tensor_tensor(w_lo[s][:], raw[s][:], w_hi[s][:].bitcast(F32),
                               ALU.subtract).then_inc(s_lo, 1)

        def slab_products(pe, ph, i, j, bank, x_hi, x_lo, ks=range(KT), n_k=KT):
            s = ph.slot(j)
            if ks[0] == 0:
                pe.wait_ge(s_lo, ph.index(i, j) + 1)
            for k in ks:
                first, last = k == 0, k == n_k - 1
                pe.matmul(bank, w_hi[s][:, k, :], x_hi[:, k, :], start=first, stop=False)
                pe.matmul(bank, w_hi[s][:, k, :], x_lo[:, k, :], start=False, stop=False)
                mm = pe.matmul(bank, w_lo[s][:, k, :], x_hi[:, k, :], start=False, stop=last)
            if ks[-1] == n_k - 1:
                mm.then_inc(s_used, 1)

        Q_G, Q_LF, Q_LFPREV, Q_GCUM, Q_BETA, Q_BEG, Q_EGL = range(7)
        NQ = 7
        head = Bump(112 * KiB, 196 * KiB)
        table = head("table", [P, HEADS, NQ, NT])
        conv_w = head("conv_w", [P, HEADS, 12])
        upper = head("upper", [P, P])
        level_mask = head("level_mask", [P, LEVELS, P])
        neg_mask = head("neg_mask", [P, P])
        h_small = head("h_small", [P, NQ, NT])
        h_conv = head("h_conv", [P, 12])
        rawq = [head(f"raw_qkv{n}", [P, 3 + T]) for n in range(3)]
        raw_z, raw_fq, raw_fk, raw_fv = [head(f"raw_{n}", [P, T]) for n in ("z", "fq", "fk", "fv")]
        cq, ck, cv, sz = [head(n, [P, T]) for n in ("cq", "ck", "cv", "silu_z")]
        ssc, rsc = head("ssc", [P, 16]), head("rsc", [P, 16])
        cols = head("cols", [P, 6, NT])
        C_BK, C_KB, C_KD, C_RQ, C_RFQ, C_VB = range(6)
        dec = head("chunk_decay", [P, NT])
        d_g = head("diag_g", [P, T])
        d_b, d_q, d_rk, d_cum = [head(f"diag_{n}", [P, T]) for n in ("b", "q", "rk", "cum")]
        e_g, qdec = head("exp_g", [P, T]), head("q_dec", [P, T])
        dt_, bdt, adt = head("decay", [P, T]), head("decay_b", [P, T]), head("decay_q", [P, T])
        a_t, att = d_g, head("attn_t", [P, T])
        kp, kd, vp = head("k_rhs", [P, T]), head("k_dec", [P, T]), head("v_rhs", [P, T])
        atm = [head(f"a_level{n}", [P, T]) for n in range(2)]
        xi, zi, yi = head("inv", [P, T]), head("inv_t", [P, T]), head("level_prod", [P, T])
        th = [xi, yi]
        sq = [atm[1], zi]
        st, vn = head("state", [P, P]), head("v_new", [P, P])
        on = dt_
        fqt, fkt, fvt = [head(f"fox_{n}", [P, T]) for n in ("q", "k", "v")]
        cumr = head("cum_row", [P, T])
        sb_, pr, pt = head("logits", [P, T]), head("probs", [P, T]), head("probs_t", [P, T])
        nmax, lsum, rsum = [head(n, [P, NT]) for n in ("neg_max", "row_sum", "inv_sum")]
        osc, ors = head("osc", [P, NT]), head("ors", [P, NT])
        pre = Bump(80 * KiB, 112 * KiB)
        w_gates = pre("w_gates", [P, KT, 24])
        gate_rows = pre("gate_rows", [P, 3, HEADS])
        gt = pre("gates_tok", [P, NT, 24])
        y2, sp2, e2 = [pre(f"tok_{n}", [P, 2 * HEADS, NT]) for n in ("y", "softplus", "e")]
        t8, gtot = [pre(f"tok_{n}", [P, HEADS, NT]) for n in ("tanh", "gtot")]

        ORDER = """cv0 th0 cv1 th1 s0.0 sl0 cv2 th2 s0.1 sl1 th3 s0.2 sq0 sl2 sl3 sq1 s0.3
                   fvt s1.0 e0 ssq s1.1 cols s1.2 s1.3 diag rows s2.0 e1 dif frows s2.1 dt s2.2 s2.3
                   tkv s3.0 e2 S0 kkqk s3.1 z0 T0 s3.2 xt Y1 s3.3 O0 X1 s4.0 e3 S1 Y2 s4.1
                   X2 T1 s4.2 Y3 s4.3 O1 X3 s5.0 e4 S2 Y4 s5.1 X4 T2 s5.2 Y5 s5.3 O2 X5
                   S3 s6.0 e5 Y6 T3 X6 s6.1 vk O3 r0 s6.2 r1 r2 r3 s6.3 e6 osq orow""".split()
        FINE = [t for t in ORDER if not (t[0] == "s" and t[1].isdigit()) and not (t[0] == "e" and t[1].isdigit())]
        SLAB_ONLY = [t for t in ORDER if (t[0] == "s" and t[1].isdigit()) or (t[0] == "e" and t[1].isdigit())]

        def quarter(tok):
            j, t = tok[1:].split(".")
            return int(j), int(t)

        def is_slab(tok):
            return tok[0] == "s" and tok[1].isdigit()

        def is_evac(tok):
            return tok[0] == "e" and tok[1].isdigit()

        def run(tokens, stages, slab, evac):
            for tok in tokens:
                if is_slab(tok):
                    if slab:
                        slab(*quarter(tok))
                elif is_evac(tok):
                    if evac:
                        evac(int(tok[1:]))
                elif tok in stages:
                    stages[tok]()

        HEAD_BANK = [0, 1, 0, 1, 0, 1, 0]

        def head_rounds(eng, per_round):
            per_round(SLAB_ONLY, 0, None)
            with eng.Fori(1, HEADS) as i:
                per_round(ORDER, i, i - 1)
            per_round(FINE, None, HEADS - 1)

        class Steps:

            def __init__(self, eng, s):
                self.eng, self.sem, self.n, self.base = eng, s, 0, None

            def value(self):
                return self.n if self.base is None else self.base + self.n

            def __call__(self, ins):
                self.n += 1
                ins.then_inc(self.sem, 1)
                self.eng.wait_ge(self.sem, self.value())

            def rounds(self, start, per, c):
                self.base, self.n = start + c * per, 0

            def straight(self, value):
                self.base, self.n = None, value

        def norm_pool_square(pool, n, m):
            if n > 0:
                pool.wait_ge(sem("h_new"), (n - 1) * KT + m + 1)
            if m == 0:
                pool.tensor_tensor(sq_sum[:], h_res[:, 0, :], h_res[:, 0, :], ALU.mult).then_inc(sem("norm_sum"), 1)
                return
            pool.wait_ge(sem("norm_sum"), n * KT + m)
            pool.tensor_tensor(r_diag[:].rearrange("p n c -> p (n c)"), h_res[:, m, :], h_res[:, m, :],
                               ALU.mult).then_inc(sem("norm_sq"), 1)
            pool.wait_ge(sem("norm_sq"), n * (KT - 1) + m)
            pool.tensor_tensor(sq_sum[:], sq_sum[:], r_diag[:].rearrange("p n c -> p (n c)"), ALU.add)\
                .then_inc(sem("norm_sum"), 1)

        def part_hi(act, n, m):
            if n > 0:
                act.wait_ge(sem("h_new"), (n - 1) * KT + m + 1)
            act.activation(u_hi[:, m, :], h_res[:, m, :], ACT.Copy, scale=gains[:, n, m:m + 1])\
                .then_inc(sem("u_hi"), 1)

        def part_lo(dve, n, m):
            dve.wait_ge(sem("u_hi"), n * KT + m + 1)
            dve.scalar_tensor_tensor(out=u_lo[:, m, :], in0=h_res[:, m, :], scalar=gains[:, n, m:m + 1],
                                     in1=u_hi[:, m, :].bitcast(F32), op0=ALU.mult, op1=ALU.subtract)\
                .then_inc(sem("u_lo"), 1)

        def residual_add(dve, bank, m, count=True):
            ins = dve.tensor_tensor(h_res[:, m, :], h_res[:, m, :], bank[:], ALU.add)
            ins.then_inc(sem("h_new") if count else sem("h_part"), 1)

        def norm_pool_scale(pool, n):
            pool.wait_ge(sem("norm_ms"), n + 1)
            pool.tensor_tensor(r_col[:], ms_col[:], mhalf[:, 0:NT], ALU.pow).then_inc(sem("norm_pool"), 1)
            pool.wait_ge(sem("norm_pool"), 2 * n + 1)
            pool.tensor_tensor(r_diag[:], over_tiles(ident[:]), over_cols(r_col[:]), ALU.mult)\
                .then_inc(sem("norm_pool"), 1)

        def norm_pe(pe, n):
            pe.wait_ge(sem("norm_sum"), (n + 1) * KT)
            for t in range(NT):
                mm = pe.matmul(bF[:, t:t + 1], sq_sum[:, t * P:(t + 1) * P], ones[:, 0:1], start=True, stop=True)
            mm.then_inc(sem("norm_ps"), 1)

        def norm_pe_row(pe, n):
            pe.wait_ge(sem("norm_pool"), 2 * n + 2)
            pe.matmul(bF[:], ones[:], r_diag[:].rearrange("p n c -> p (n c)"), start=True, stop=True)\
                .then_inc(sem("norm_ps"), 1)

        def norm_dve(dve, n):
            dve.wait_ge(sem("norm_ps"), 2 * n + 1)
            dve.tensor_scalar(ms_col[:], bF[:, 0:NT], 1.0 / D, EPS, ALU.mult, ALU.add).then_inc(sem("norm_ms"), 1)

        def norm_dve_row(dve, n):
            dve.wait_ge(sem("norm_ps"), 2 * n + 2)
            dve.tensor_copy(r_row[:], bF[:]).then_inc(sem("norm_row"), 1)
            dve.wait_ge(sem("norm_row"), n + 1)

        merge_g = mtmp

        def branches_hi(act, rnd):
            act.wait_ge(sem("branches_done"), rnd + 1)
            for k in range(KT):
                for hi, br in ((a_hi, br_a), (b_hi, br_b)):
                    act.copy(hi[:, k, :], br[:, k, :]).then_inc(sem("br_hi"), 1)

        def branches_lo(dve, rnd):
            for k in range(KT):
                for n, (hi, lo, br) in enumerate(((a_hi, a_lo, br_a), (b_hi, b_lo, br_b))):
                    dve.wait_ge(sem("br_hi"), (rnd * KT + k) * 2 + n + 1)
                    dve.tensor_tensor(lo[:, k, :], br[:, k, :], hi[:, k, :].bitcast(F32), ALU.subtract)\
                        .then_inc(sem("br_lo"), 1)

        def merge_pe(pe, ph, rnd):
            with pe.Fori(0, KT) as m:
                q = rnd * KT + m
                for j in range(4):
                    if j < 2:
                        pe.wait_ge(sem("gate_taken"), 2 * q + 1)
                        slab_products(pe, ph, m, j, bank_slab[j][:], u_hi, u_lo)
                        continue
                    if j == 2:
                        pe.wait_ge(sem("br_lo"), 2 * KT * (rnd + 1))
                    pe.wait_ge(sem("branch_taken"), 2 * q + 1)
                    slab_products(pe, ph, m, j, (bA, bB)[j - 2][:], (a_hi, b_hi)[j - 2], (a_lo, b_lo)[j - 2])

        def merge_act(act, ph, rnd):
            branches_hi(act, rnd)
            with act.Fori(0, KT) as m:
                q = rnd * KT + m
                for j in range(4):
                    split_hi(act, ph, m, j + LEAD)
                    if j < 2:
                        act.wait_ge(sem("gate_taken"), 2 * q + j + 2)
                        act.activation(merge_g[j][:], merge_g[j][:], ACT.Tanh, scale=0.5).then_inc(sem("gate_tanh"), 1)

        def merge_pool(pool, ph):
            with pool.Fori(0, KT) as m:
                for j in range(4):
                    split_lo(pool, ph, m, j + LEAD)

        def merge_dve(dve, ph, rnd, bias=None):
            with dve.Fori(0, KT) as m:
                q = rnd * KT + m
                dve.wait_ge(sem("merged"), 3 * q + 1)
                for j in range(2):
                    dve.wait_ge(s_used, ph.index(m, j) + 1)
                    if bias is None:
                        dve.tensor_tensor(merge_g[j][:], bank_slab[j][:], r_row[:], ALU.mult)\
                            .then_inc(sem("gate_taken"), 1)
                    else:
                        dve.tensor_tensor(merge_g[j][:], bank_slab[j][:], r_row[:], ALU.mult)\
                            .then_inc(sem("gate_scaled"), 1)
                        dve.wait_ge(sem("gate_scaled"), 2 * m + j + 1)
                        dve.tensor_scalar(merge_g[j][:], merge_g[j][:], bias[:, bass.ds(m + KT * j, 1)], None, ALU.add)\
                            .then_inc(sem("gate_taken"), 1)
                for j in range(2):
                    dve.wait_ge(s_used, ph.index(m, 2 + j) + 1)
                    dve.wait_ge(sem("gate_tanh"), 2 * q + j + 1)
                    dve.scalar_tensor_tensor(out=merge_g[j][:], in0=merge_g[j][:], scalar=1.0, in1=(bA, bB)[j][:],
                                             op0=ALU.add, op1=ALU.mult).then_inc(sem("branch_taken"), 1)
                dve.wait_ge(sem("branch_taken"), 2 * q + 3)
                dve.tensor_tensor(merge_g[0][:], merge_g[0][:], merge_g[1][:], ALU.add).then_inc(sem("merged"), 1)
                dve.wait_ge(sem("merged"), 3 * q + 2)
                dst_hi = m_hi[:, bass.ds(m, 1), :].rearrange("p a t -> p (a t)")
                dst_lo = m_lo[:, bass.ds(m, 1), :].rearrange("p a t -> p (a t)")
                dve.tensor_scalar(dst_hi, merge_g[0][:], 0.5, None, ALU.mult).then_inc(sem("merged"), 1)
                dve.wait_ge(sem("merged"), 3 * q + 3)
                dve.scalar_tensor_tensor(out=dst_lo, in0=merge_g[0][:], scalar=0.5, in1=dst_hi.bitcast(F32),
                                         op0=ALU.mult, op1=ALU.subtract).then_inc(sem("merged"), 1)

        def out_pe(pe, ph, rnd, n):
            for m in range(KT):
                if m == 0:
                    pe.wait_ge(sem("merged"), 3 * KT * (rnd + 1) + 1)
                    pe.wait_ge(sem("branch_taken"), 2 * KT * (rnd + 1) + 1)
                if m >= 2:
                    pe.wait_ge(sem("h_new"), (n - 1) * KT + m - 1)
                slab_products(pe, ph, 0, m, bank_slab[m % 2][:], m_hi, m_lo)

        def out_act(act, ph, n):
            for m in range(KT):
                split_hi(act, ph, 0, m + LEAD)
                if m >= 1:
                    part_hi(act, n, m - 1)
            part_hi(act, n, KT - 1)

        def out_pool(pool, ph, n):
            for m in range(KT):
                split_lo(pool, ph, 0, m + LEAD)
                if m >= 1:
                    norm_pool_square(pool, n, m - 1)
            norm_pool_square(pool, n, KT - 1)
            norm_pool_scale(pool, n)

        def out_dve(dve, ph, n):
            for m in range(KT):
                dve.wait_ge(s_used, ph.index(0, m) + 1)
                if m == 0:
                    dve.wait_ge(sem("ld_x"), 32)
                residual_add(dve, bank_slab[m % 2], m)
                if m >= 1:
                    part_lo(dve, n, m - 1)
            part_lo(dve, n, KT - 1)
            norm_dve(dve, n)
            norm_dve_row(dve, n)

        MLP_PARTS = 4

        def mlp_parts(eng, part):
            part(0)
            with eng.Fori(1, MLP_PARTS - 1) as i:
                part(i)
            part(MLP_PARTS - 1)

        def is_last(i):
            return isinstance(i, int) and i == MLP_PARTS - 1

        def mlp_pe(pe):
            def part(i):
                first = isinstance(i, int) and i == 0
                for j in range(16):
                    if j < 2 and not first:
                        pe.wait_ge(sem("h_part"), 8 * i + j - 1)
                    elif 2 <= j < 10:
                        pe.wait_ge(sem("relu"), 8 * i + j - 1)
                    elif j >= 10:
                        pe.wait_ge(sem("h_new"), KT + j - 9) if is_last(i) else \
                            pe.wait_ge(sem("h_part"), 8 * i + j - 9)
                    if j < 8:
                        if first and j == 0:
                            pe.wait_ge(sem("u_lo"), 2 * KT)
                            pe.wait_ge(sem("h_new"), KT)
                        slab_products(pe, ph_mlp, i, j, bank_slab[j % 2][:], u_hi, u_lo)
                        if first and j == 0:
                            norm_pe(pe, 1)
                        if first and j == 1:
                            norm_pe_row(pe, 1)
                        continue
                    for k in range(KT):
                        if j == 8:
                            pe.wait_ge(sem("hid_lo"), 8 * i + k + 1)
                        slab_products(pe, ph_mlp, i, j, bank_slab[j % 2][:], y_hi, y_lo, ks=(k,))
            mlp_parts(pe, part)

        def mlp_act(act):
            def part(i):
                for j in range(16):
                    split_hi(act, ph_mlp, i, j + LEAD)
                    if 1 <= j <= 8:
                        hidden(i, j - 1)
                    if isinstance(i, int) and i == MLP_PARTS - 1 and j >= 9:
                        part_hi(act, 2, j - 9)

            def hidden(i, t):
                act.wait_ge(sem("relu"), 8 * i + t + 1)
                act.activation(tmp[2 + t % 2][:], tmp[t % 2][:], ACT.Square).then_inc(sem("hid_sq"), 1)
                act.wait_ge(sem("hid_sq"), 8 * i + t + 1)
                act.copy(y_hi[:, t, :], tmp[2 + t % 2][:]).then_inc(sem("hid_hi"), 1)
            mlp_parts(act, part)
            part_hi(act, 2, KT - 1)

        def mlp_pool(pool):
            def part(i):
                for j in range(16):
                    split_lo(pool, ph_mlp, i, j + LEAD)
                    if is_last(i) and j >= 9:
                        norm_pool_square(pool, 2, j - 9)
            mlp_parts(pool, part)
            norm_pool_square(pool, 2, KT - 1)
            norm_pool_scale(pool, 2)

        def mlp_dve(dve):
            def part(i):
                for j in range(16):
                    if 1 <= j <= 8:
                        t = j - 1
                        dve.wait_ge(sem("hid_hi"), 8 * i + t + 1)
                        dve.tensor_tensor(y_lo[:, t, :], tmp[2 + t % 2][:], y_hi[:, t, :].bitcast(F32), ALU.subtract)\
                            .then_inc(sem("hid_lo"), 1)
                    dve.wait_ge(s_used, ph_mlp.index(i, j) + 1)
                    if j < 8:
                        if j >= 2:
                            dve.wait_ge(sem("hid_sq"), 8 * i + j - 1)
                        dve.scalar_tensor_tensor(out=tmp[j % 2][:], in0=bank_slab[j % 2][:], scalar=0.0, in1=r_row[:],
                                                 op0=ALU.max, op1=ALU.mult).then_inc(sem("relu"), 1)
                    else:
                        residual_add(dve, bank_slab[j % 2], j - 8, count=is_last(i))
                    if is_last(i) and j >= 9:
                        part_lo(dve, 2, j - 9)
            mlp_parts(dve, part)
            part_lo(dve, 2, KT - 1)
            norm_dve(dve, 2)
            norm_dve_row(dve, 2)

        tab = Bump(152 * KiB, 168 * KiB)
        cos_r, sin_r, cos_a, sin_a = [tab(n, [P, T]) for n in ("cos_ret", "sin_ret", "cos_att", "sin_att")]
        swap_r, swap_a, dup0, dup1 = [tab(n, [P, P]) for n in ("swap_ret", "swap_att", "dup_kv0", "dup_kv1")]
        decay_t = tab("ret_decay_t", [P, RET_HEADS, P])
        q_decay = tab("ret_q_decay", [P, RET_HEADS, P])
        band = tab("band_mask", [P, 2, P])
        small2 = Bump(small.at, LIMIT)
        k_decay = small2("ret_k_decay", [P, RET_HEADS, 2])
        bias_cols = small2("bias_cols", [P, 2 + 8 * RET_HEADS])
        bias_gate = small2("bias_gate", [P, 2 * KT])
        ret_gain = small2("ret_gain", [P, RET_HEADS, 2])
        sink_cols = small2("sink_cols", [P, RET_HEADS, 4])
        hb = small2("round_bias", [P, 8])
        hg, hd, hs = [small2(n, [P, w]) for n, w in (("round_gain", 2), ("round_decay", 2), ("round_sinks", 4))]
        gsc, grs = small2("gn_ms", [P, NT]), small2("gn_rs", [P, NT])
        nm2, ls2, es2, rd2 = [small2(n, [P, NT]) for n in ("att_neg_max", "att_sum", "att_sink", "att_inv")]
        TAB2 = [("cos_r", cos_r), ("sin_r", sin_r), ("cos_a", cos_a), ("sin_a", sin_a), ("swap_r", swap_r),
                ("swap_a", swap_a), ("dup0", dup0), ("dup1", dup1), ("decay_t", decay_t), ("q_decay", q_decay),
                ("band", band), ("k_decay", k_decay), ("bias_cols", bias_cols), ("bias_gate", bias_gate),
                ("ret_gain", ret_gain), ("sink_cols", sink_cols)]
        N_TAB2 = len(TAB2)
        w2 = Bump(112 * KiB, 152 * KiB)
        r_q, r_k = w2("ret_q_raw", [P, T]), w2("ret_k_raw", [P, T])
        r_v = [w2(f"ret_v_raw{n}", [P, T]) for n in range(2)]
        r_g = [w2(f"ret_g_raw{n}", [P, T]) for n in range(2)]
        a_q = [w2(f"att_q_raw{n}", [P, T]) for n in range(2)]
        q_r, k_r = w2("ret_q", [P, T]), w2("ret_k", [P, T])
        kdec2, v_tok = w2("ret_k_dec", [P, T]), w2("ret_v_tok", [P, NT, 2 * P])
        sc_t, q_dec2 = w2("ret_scores_t", [P, T]), w2("ret_q_dec", [P, T])
        y2_at = w2.at
        y_r = [w2(f"ret_y{n}", [P, T]) for n in range(2)]
        k_cur = w2("att_k", [P, T])
        lg = w2("att_logits", [P, NT, 2 * P])
        x2 = Bump(168 * KiB, 176 * KiB)
        v_cur = x2("att_v", [P, NT, 64])
        st2 = [x2(f"ret_state{n}", [P, 2 * P]) for n in range(3)]
        pr2 = [x2("att_probs0", [P, NT, 2 * P]), at("att_probs1", [P, NT, 2 * P], y2_at)]
        kv_dup = at("att_kv_dup", [P, 2, T], 192 * KiB)
        av_tok = small2("att_v_tok", [P, NT, P])
        aq_r, pt2 = [q_r, k_r], v_tok
        gn_sq = [kdec2, q_dec2]
        gn_th = [sc_t[:], pt2[:, 0:2, :].rearrange("p n c -> p (n c)")]

        R_DEST = [r_q, r_k, r_v[0], r_v[1], a_q[0], a_q[1], r_g[0], r_g[1]]
        ORDER2 = """rb s0.0 sw kcur s0.1 rot tv s0.2 s0.3 tk sc s1.0 e0 s1.1 qd sp0 s1.2 sp1 s1.3 sp2 s2.0 e1 ro
                    s2.1 s2.2 sa y2 s2.3 rm rota s3.0 e2 yc L0 s3.1 rs s3.2 rr s3.3 yo L1 s4.0 e3 T0 s4.1 O0 L2
                    s4.2 s4.3 T1 s5.0 e4 O1 ev0 L3 s5.1 s5.2 T2 s5.3 O2 s6.0 e5 s6.1 s6.2 T3 s6.3 s7.0 e6 O3 ev1
                    s7.1 s7.2 s7.3 e7""".split()
        FINE2 = [t for t in ORDER2 if not is_slab(t) and not is_evac(t)]
        ORDER2_FIRST = """s0.0 s0.1 s0.2 s0.3 s1.0 e0 s1.1 s1.2 s1.3 s2.0 e1 s2.1 s2.2 kva s2.3 s3.0 e2 s3.1 s3.2 kvb
                          s3.3 s4.0 e3 s4.1 s4.2 s4.3 s5.0 e4 s5.1 s5.2 s5.3 s6.0 e5 s6.1 s6.2 s6.3 s7.0 e6 s7.1 s7.2
                          s7.3 s8.0 e7 s8.1 s8.2 s8.3 s9.0 e8 s9.1 s9.2 s9.3 e9""".split()

        def ret_rounds(eng, per_round):
            per_round(ORDER2_FIRST, ph_kv, 0, None)
            with eng.Fori(0, RET_HEADS - 1) as i:
                per_round(ORDER2, ph_ret, i, i)
            per_round(FINE2, None, None, RET_HEADS - 1)

        L_BANKS = [(bC, bD), (bE, bF), (bE, bF), (bC, bD)]
        O_BANK = [bC, bC, bE, bE]

        def ret_pe(pe, tiles, transposes):
            def per_round(tokens, ph, i, c):
                def slab(j, t):
                    if t == 0:
                        q = ph.index(i, j) - ph_kv.first
                        if not (isinstance(q, int) and q < 2):
                            pe.wait_ge(sem("taken2"), q - 1)
                        else:
                            pe.wait_ge(sem("u_lo"), 3 * KT)
                            pe.wait_ge(sem("h_new"), 2 * KT)
                    slab_products(pe, ph, i, j, bank_slab[j % 2][:], u_hi, u_lo, ks=(2 * t, 2 * t + 1))
                    if ph is ph_kv and j == 0 and t == 3:
                        norm_pe(pe, 2)
                        norm_pe_row(pe, 2)

                def kva():
                    pe.wait_ge(sem("taken2"), 2)
                    pe.wait_ge(sem("ld_tab2"), 16 * N_TAB2)
                    pe.matmul(bA[:], swap_a[:], q_r[:], start=True, stop=True).then_inc(sem("kv_ps"), 1)
                    transposes(bD, k_r).then_inc(sem("kv_ps"), 1)

                def kvb():
                    pe.wait_ge(sem("kv_rot"), 1)
                    pe.matmul(bB[:], dup0[:], sc_t[:], start=True, stop=True)
                    pe.matmul(bC[:], dup1[:], sc_t[:], start=True, stop=True).then_inc(sem("kv_ps"), 1)

                def sw():
                    pe.wait_ge(sem("taken2"), 8 * c + 10)
                    pe.matmul(bA[:], swap_r[:], r_q[:], start=True, stop=True).then_inc(sem("sw_ps"), 1)
                    pe.matmul(bB[:], swap_r[:], r_k[:], start=True, stop=True).then_inc(sem("sw_ps"), 1)

                def tv():
                    transposes(bC, r_v[0]).then_inc(sem("tv2_ps"), 1)
                    transposes(bD, r_v[1]).then_inc(sem("tv2_ps"), 1)

                def tk():
                    pe.wait_ge(sem("rot"), 2 * c + 2)
                    transposes(bA, k_r).then_inc(sem("tk2_ps"), 1)

                def sc():
                    tiles(bB, k_r, q_r).then_inc(sem("sc_ps"), 1)

                def sp(n):
                    if n == 0:
                        pe.wait_ge(sem("kdec2"), c + 1)
                        pe.wait_ge(sem("v_tok"), 2 * c + 2)
                    if n == 2:
                        pe.wait_ge(sem("state2"), 3 * c + 1)
                    pe.matmul((bE, bF, bE)[n][:, 0:2 * P], kdec2[:, n * P:(n + 1) * P], v_tok[:, n, :],
                              start=True, stop=True).then_inc(sem("sp_ps"), 1)

                def ro():
                    pe.wait_ge(sem("sc_t"), c + 1)
                    pe.wait_ge(sem("q_dec2"), c + 1)
                    pe.wait_ge(sem("state2"), 3 * c + 3)
                    for e, bank in enumerate((bC, bD)):
                        cols = slice(e * P, (e + 1) * P)
                        for n in range(NT):
                            q = slice(n * P, (n + 1) * P)
                            mm = pe.matmul(bank[:, q], v_tok[:, n, cols], sc_t[:, q], start=True, stop=n == 0)
                            if n > 0:
                                mm = pe.matmul(bank[:, q], st2[n - 1][:, cols], q_dec2[:, q], start=False, stop=True)
                        mm.then_inc(sem("ro_ps"), 1)

                def rm():
                    pe.wait_ge(sem("ret_y"), 2 * c + 2)
                    pe.matmul(bA[:], ones[:], y_r[0][:], start=True, stop=False)
                    pe.matmul(bA[:], ones[:], y_r[1][:], start=False, stop=True).then_inc(sem("gn_ps"), 1)

                def rs():
                    pe.wait_ge(sem("gn_sq"), 2 * c + 2)
                    for n in range(NT):
                        q = slice(n * P, (n + 1) * P)
                        pe.matmul(bB[:, n:n + 1], gn_sq[0][:, q], ones[:, 0:1], start=True, stop=False)
                        mm = pe.matmul(bB[:, n:n + 1], gn_sq[1][:, q], ones[:, 0:1], start=False, stop=True)
                    mm.then_inc(sem("gn_ps"), 1)

                def rr():
                    pe.wait_ge(sem("gn_scale"), 2 * c + 2)
                    pe.matmul(bA[:], ones[:], r_diag[:].rearrange("p n c -> p (n c)"), start=True, stop=True)\
                        .then_inc(sem("gn_ps"), 1)

                def sa():
                    pe.matmul(bE[:], swap_a[:], a_q[0][:], start=True, stop=True).then_inc(sem("sa_ps"), 1)
                    pe.matmul(bF[:], swap_a[:], a_q[1][:], start=True, stop=True).then_inc(sem("sa_ps"), 1)

                def logits(u):
                    half = slice(64 * (u % 2), 64 * (u % 2) + 64)
                    if u == 0:
                        pe.wait_ge(sem("kv_cur"), c + 1)
                        pe.wait_ge(sem("rot_a"), 2 * c + 1)
                        pe.wait_ge(sem("ret_y"), 2 * c + 2)
                    if u == 1:
                        pe.wait_ge(sem("rot_a"), 2 * c + 2)
                    if u == 2:
                        pe.wait_ge(sem("lg"), 4 * c + 2)
                    if u == 3:
                        pe.wait_ge(sem("att_out"), 2 * c + 1)
                    for b in range(NT):
                        bank, at_ = L_BANKS[u][b // 2], 2 * P * (b % 2)
                        k0 = max(b - 1, 0) * P
                        mm = pe.matmul(bank[:, at_ + (P if b == 0 else 0):at_ + 2 * P],
                                       aq_r[u // 2][half, b * P:(b + 1) * P], k_cur[half, k0:(b + 1) * P],
                                       start=True, stop=True)
                    mm.then_inc(sem("lg_ps"), 1)

                def probs_t(u):
                    pe.wait_ge(sem("probs2"), 4 * c + u + 1)
                    if u == 0:
                        pe.wait_ge(sem("ret_out"), 2 * c + 2)
                    else:
                        pe.wait_ge(sem("pt2"), 2 * (4 * c + u))
                    for b in range(NT):
                        for w in range(1 if b == 0 else 0, 2):
                            mm = pe.transpose((bA, bB)[b // 2][:, (2 * (b % 2) + w) * P:(2 * (b % 2) + w + 1) * P],
                                              pr2[u % 2][:, b, w * P:(w + 1) * P], ident[:])
                        if b % 2:
                            mm.then_inc(sem("pt2_ps"), 1)

                def outs(u):
                    half = slice(64 * (u % 2), 64 * (u % 2) + 64)
                    pe.wait_ge(sem("pt2"), 2 * (4 * c + u + 1))
                    for b in range(NT):
                        for w in range(1 if b == 0 else 0, 2):
                            mm = pe.matmul(O_BANK[u][half, b * P:(b + 1) * P], v_cur[:, b - 1 + w, :],
                                           pt2[:, b, w * P:(w + 1) * P], start=w == 0 or b == 0, stop=w == 1)
                    if u % 2:
                        mm.then_inc(sem("att_ps"), 1)

                stages = {"kva": kva, "kvb": kvb, "sw": sw, "tv": tv, "tk": tk, "sc": sc, "ro": ro, "rm": rm, "rs": rs,
                          "rr": rr, "sa": sa}
                for n in range(3):
                    stages[f"sp{n}"] = lambda n=n: sp(n)
                for u in range(4):
                    stages[f"L{u}"] = lambda u=u: logits(u)
                    stages[f"T{u}"] = lambda u=u: probs_t(u)
                    stages[f"O{u}"] = lambda u=u: outs(u)
                run(tokens, stages, slab, None)
            ret_rounds(pe, per_round)

        def ret_act(act):
            def per_round(tokens, ph, i, c):
                def slab(j, t):
                    if t == 0:
                        split_hi(act, ph, i, j + LEAD)

                def kvb():
                    act.wait_ge(sem("kv_ps"), 2)
                    act.copy(av_tok[:].rearrange("p n d -> p (n d)"), bD[:]).then_inc(sem("kv_act"), 1)
                    act.wait_ge(sem("kv_ps"), 3)
                    act.copy(kv_dup[:, 0, :], bB[:]).then_inc(sem("kv_act"), 1)
                    act.copy(kv_dup[:, 1, :], bC[:]).then_inc(sem("kv_act"), 1)

                def tv():
                    for e, bank in enumerate((bC, bD)):
                        act.wait_ge(sem("tv2_ps"), 2 * c + e + 1)
                        act.copy(v_tok[:, :, e * P:(e + 1) * P], c4(bank[:])).then_inc(sem("v_tok"), 1)

                def tk():
                    act.wait_ge(sem("tk2_ps"), c + 1)
                    act.activation(kdec2[:], bA[:], ACT.Copy, scale=hd[:, 0:1]).then_inc(sem("kdec2"), 1)

                def y2_():
                    for e, bank in enumerate((bC, bD)):
                        act.wait_ge(sem("ro_ps"), 2 * c + e + 1)
                        act.copy(y_r[e][:], bank[:]).then_inc(sem("ret_y"), 1)

                def rs():
                    for e in range(2):
                        act.wait_ge(sem("gn_c"), 2 * c + e + 1)
                        act.activation(gn_sq[e][:], y_r[e][:], ACT.Square).then_inc(sem("gn_sq"), 1)
                    for e in range(2):
                        if e == 1:
                            act.wait_ge(sem("gn_c"), 2 * c + 2)
                        act.activation(gn_th[e], r_g[e][:], ACT.Tanh, scale=0.5).then_inc(sem("gn_tanh"), 1)

                def softmax(u):
                    act.wait_ge(sem("lg_max"), 4 * c + u + 1)
                    if u == 1:
                        act.wait_ge(sem("ret_out"), 2 * c + 2)
                    if u >= 2:
                        act.wait_ge(sem("pt2_ps"), 2 * (4 * c + u - 1))
                    act.activation(es2[:], nm2[:], ACT.Exp, bias=hs[:, u:u + 1])
                    for b in range(NT):
                        ins = act.activation(pr2[u % 2][:, b, :], lg[:, b, :], ACT.Exp, bias=nm2[:, b:b + 1],
                                             accum_out=ls2[:, b:b + 1])
                    ins.then_inc(sem("exp2"), 1)

                def probs_t(u):
                    for h, bank in enumerate((bA, bB)):
                        act.wait_ge(sem("pt2_ps"), 2 * (4 * c + u) + h + 1)
                        lo = P if h == 0 else 0
                        act.copy(pt2[:, 2 * h:2 * h + 2, :].rearrange("p b c -> p (b c)")[:, lo:], bank[:, lo:])\
                            .then_inc(sem("pt2"), 1)

                stages = {"kvb": kvb, "tv": tv, "tk": tk, "y2": y2_, "rs": rs}
                for u in range(4):
                    stages[f"L{u}"] = lambda u=u: softmax(u)
                    stages[f"T{u}"] = lambda u=u: probs_t(u)
                run(tokens, stages, slab, None)
            ret_rounds(act, per_round)

        RET_STEPS = 20

        def ret_dve(dve, step):
            start = [0]

            def dyn(ap):
                return ap.rearrange("p a c -> p (a c)")

            def rotate(bank, src, dst, cos, sin, done):
                step(dve.tensor_tensor(rot_buf[0][:], bank[:], sin[:], ALU.mult))
                step(dve.tensor_tensor(dst[:], src[:], cos[:], ALU.mult))
                dve.tensor_tensor(dst[:], dst[:], rot_buf[0][:], ALU.add).then_inc(sem(done), 1)

            rot_buf = [None]

            def per_round(tokens, ph, i, c):
                if c is not None:
                    step.rounds(start[0], RET_STEPS, c)

                def evac(j):
                    if ph is ph_kv:
                        dst = (q_r, k_r)[j] if j < 2 else R_DEST[j - 2]
                        bias = bias_cols[:, j:j + 1]
                    else:
                        dst, bias = R_DEST[j], hb[:, j:j + 1]
                        if j == 2:
                            dve.wait_ge(sem("tv2_ps"), 2 * c + 2)
                        if j == 6:
                            dve.wait_ge(sem("gn_tanh"), 2 * c + 2)
                    dve.wait_ge(s_used, ph.index(i, j) + 1)
                    dve.tensor_tensor(dst[:], bank_slab[j % 2][:], r_row[:], ALU.mult).then_inc(sem("scaled2"), 1)
                    dve.wait_ge(sem("scaled2"), ph.index(i, j) - ph_kv.first + 1)
                    dve.tensor_scalar(dst[:], dst[:], bias, None, ALU.add).then_inc(sem("taken2"), 1)

                def kva():
                    dve.wait_ge(sem("kv_ps"), 1)
                    dve.wait_ge(sem("taken2"), 2)
                    rot_buf[0] = q_dec2
                    rotate(bA, q_r, sc_t, cos_a, sin_a, "kv_rot")

                def rb():
                    dve.wait_ge(sem("taken2"), 8 * c + 10)
                    if ph is not None:
                        step(dve.tensor_scalar(hb[:], bias_cols[:, bass.ds(8 * i + 10, 8)], 1.0, None, ALU.mult))
                    else:
                        step(dve.tensor_scalar(hb[:], hb[:], 1.0, None, ALU.mult))
                    step(dve.tensor_scalar(hg[:], dyn(ret_gain[:, bass.ds(c, 1), :]), 0.5, None, ALU.mult))
                    step(dve.tensor_scalar(hs[:], dyn(sink_cols[:, bass.ds(c, 1), :]), 1.0, None, ALU.mult))
                    step(dve.tensor_scalar(hd[:], dyn(k_decay[:, bass.ds(c, 1), :]), 1.0, None, ALU.mult))

                def kcur():
                    dve.wait_ge(sem("kv_act"), 3)
                    step(dve.tensor_scalar(k_cur[:], dyn(kv_dup[:, bass.ds(c // 2, 1), :]), 1.0, None, ALU.mult))
                    av = av_tok[:].rearrange("p n (v d) -> p v n d", v=2)[:, bass.ds(c // 2, 1), :, :]
                    dve.tensor_scalar(v_cur[:], av.rearrange("p a n d -> p (a n) d"), 1.0, None, ALU.mult)\
                        .then_inc(sem("kv_cur"), 1)

                def rot():
                    rot_buf[0] = sc_t
                    for n, (bank, src, dst) in enumerate(((bA, r_q, q_r), (bB, r_k, k_r))):
                        dve.wait_ge(sem("sw_ps"), 2 * c + n + 1)
                        if n == 1:
                            dve.wait_ge(sem("rot"), 2 * c + 1)
                        rotate(bank, src, dst, cos_r, sin_r, "rot")

                def sc():
                    dve.wait_ge(sem("sc_ps"), c + 1)
                    dve.wait_ge(sem("rot"), 2 * c + 2)
                    dt = decay_t[:, bass.ds(c, 1), :].to_broadcast([P, NT, P])
                    dve.tensor_tensor(c4(sc_t[:]), c4(bB[:]), dt, ALU.mult).then_inc(sem("sc_t"), 1)

                def qd():
                    qd_ = q_decay[:, bass.ds(c, 1), :].to_broadcast([P, NT, P])
                    dve.tensor_tensor(c4(q_dec2[:]), c4(q_r[:]), qd_, ALU.mult).then_inc(sem("q_dec2"), 1)

                def sp(n):
                    dve.wait_ge(sem("sp_ps"), 3 * c + n + 1)
                    bank = (bE, bF, bE)[n]
                    if n == 0:
                        dve.tensor_copy(st2[0][:], bank[:, 0:2 * P]).then_inc(sem("state2"), 1)
                    else:
                        dve.wait_ge(sem("state2"), 3 * c + n)
                        dve.scalar_tensor_tensor(out=st2[n][:], in0=st2[n - 1][:], scalar=hd[:, 1:2],
                                                 in1=bank[:, 0:2 * P], op0=ALU.mult, op1=ALU.add)\
                            .then_inc(sem("state2"), 1)

                def rota():
                    dve.wait_ge(sem("ro_ps"), 2 * c + 2)
                    rot_buf[0] = sc_t
                    for n in range(2):
                        dve.wait_ge(sem("sa_ps"), 2 * c + n + 1)
                        if n == 1:
                            dve.wait_ge(sem("rot_a"), 2 * c + 1)
                        rotate((bE, bF)[n], a_q[n], aq_r[n], cos_a, sin_a, "rot_a")

                def yc():
                    dve.wait_ge(sem("gn_ps"), 3 * c + 1)
                    dve.wait_ge(sem("rot_a"), 2 * c + 2)
                    for e in range(2):
                        dve.scalar_tensor_tensor(out=y_r[e][:], in0=bA[:], scalar=-1.0 / (2 * P), in1=y_r[e][:],
                                                 op0=ALU.mult, op1=ALU.add).then_inc(sem("gn_c"), 1)

                def rs():
                    dve.wait_ge(sem("gn_ps"), 3 * c + 2)
                    dve.tensor_scalar(gsc[:], bB[:, 0:NT], 1.0 / (2 * P), EPS, ALU.mult, ALU.add)\
                        .then_inc(sem("gn_ms"), 1)
                    for e in range(2):
                        dve.wait_ge(sem("gn_tanh"), 2 * c + e + 1)
                        step(dve.scalar_tensor_tensor(out=gn_th[e], in0=gn_th[e], scalar=1.0, in1=r_g[e][:],
                                                      op0=ALU.add, op1=ALU.mult))

                def yo():
                    dve.wait_ge(sem("gn_ps"), 3 * c + 3)
                    for e in range(2):
                        ins = dve.scalar_tensor_tensor(out=y_r[e][:], in0=y_r[e][:], scalar=hg[:, e:e + 1], in1=bA[:],
                                                       op0=ALU.mult, op1=ALU.mult)
                        if e:
                            ins.then_inc(sem("gn_out"), 1)
                        else:
                            step(ins)
                    dve.wait_ge(sem("gn_out"), c + 1)
                    for e in range(2):
                        dst = br_a[:, bass.ds(2 * c + e, 1), :].rearrange("p a t -> p (a t)")
                        dve.tensor_tensor(dst, y_r[e][:], gn_th[e], ALU.mult).then_inc(sem("ret_out"), 1)

                def logits(u):
                    dve.wait_ge(sem("lg_ps"), 4 * c + u + 1)
                    if u > 0:
                        dve.wait_ge(sem("exp2"), 4 * c + u)
                    flat = lg[:].rearrange("p b c -> p (b c)")
                    bd = band[:].rearrange("p w c -> p (w c)")
                    x_, y_ = L_BANKS[u]
                    for lo, hi, bank in ((P, 2 * P, x_), (2 * P, 4 * P, x_), (4 * P, 6 * P, y_), (6 * P, 8 * P, y_)):
                        ins = dve.scalar_tensor_tensor(out=flat[:, lo:hi], in0=bank[:, lo % 512:lo % 512 + hi - lo],
                                                       scalar=0.125, in1=bd[:, lo % 256:], op0=ALU.mult, op1=ALU.add)
                    ins.then_inc(sem("lg"), 1)
                    dve.wait_ge(sem("lg"), 4 * c + u + 1)
                    step(dve.tensor_reduce(nm2[:], lg[:], AX.X, ALU.max))
                    dve.tensor_scalar(nm2[:], nm2[:], hs[:, u:u + 1], -1.0, ALU.max, ALU.mult)\
                        .then_inc(sem("lg_max"), 1)
                    dve.wait_ge(sem("exp2"), 4 * c + u + 1)
                    if u > 0:
                        dve.wait_ge(sem("probs2"), 4 * c + u)
                    dve.tensor_tensor(rd2[:], ls2[:], es2[:], ALU.add).then_inc(sem("att_sum"), 1)
                    dve.wait_ge(sem("att_sum"), 4 * c + u + 1)
                    dve.reciprocal(rd2[:], rd2[:]).then_inc(sem("att_inv"), 1)

                def ev(a_):
                    dve.wait_ge(sem("att_ps"), 2 * c + a_ + 1)
                    dst = br_b[:, bass.ds(2 * c + a_, 1), :].rearrange("p a t -> p (a t)")
                    dve.tensor_scalar(dst, O_BANK[2 * a_][:], 1.0, None, ALU.mult).then_inc(sem("att_out"), 1)

                stages = {"kva": kva, "rb": rb, "kcur": kcur, "rot": rot, "sc": sc, "qd": qd, "rota": rota, "yc": yc,
                          "rs": rs, "yo": yo, "ev0": lambda: ev(0), "ev1": lambda: ev(1)}
                for n in range(3):
                    stages[f"sp{n}"] = lambda n=n: sp(n)
                for u in range(4):
                    stages[f"L{u}"] = lambda u=u: logits(u)
                if c is None:
                    dve.wait_ge(sem("norm_row"), 3)
                    step(dve.memset(lg[:, 0, 0:P], -1e30))
                run(tokens, stages, None, evac)
                if c is None:
                    start[0] = step.value()
                else:
                    assert step.n == RET_STEPS, step.n
            ret_rounds(dve, per_round)
            step.straight(start[0] + RET_HEADS * RET_STEPS)
            dve.wait_ge(sem("ret_out"), 2 * RET_HEADS)
            dve.wait_ge(sem("att_out"), 2 * RET_HEADS)
            dve.tensor_scalar(ms_col[:], ms_col[:], 1.0, None, ALU.mult).then_inc(sem("branches_done"), 1)

        def ret_pool(pool):
            def per_round(tokens, ph, i, c):
                def slab(j, t):
                    if t == 0:
                        split_lo(pool, ph, i, j + LEAD)

                def rs():
                    pool.wait_ge(sem("gn_ms"), c + 1)
                    pool.tensor_tensor(grs[:], gsc[:], mhalf[:, 0:NT], ALU.pow).then_inc(sem("gn_scale"), 1)
                    pool.wait_ge(sem("gn_scale"), 2 * c + 1)
                    pool.tensor_tensor(r_diag[:], over_tiles(ident[:]), over_cols(grs[:]), ALU.mult)\
                        .then_inc(sem("gn_scale"), 1)

                def probs(u):
                    pool.wait_ge(sem("att_inv"), 4 * c + u + 1)
                    pool.tensor_tensor(pr2[u % 2][:], pr2[u % 2][:],
                                       rd2[:].unsqueeze(2).to_broadcast([P, NT, 2 * P]), ALU.mult)\
                        .then_inc(sem("probs2"), 1)
                stages = {"rs": rs}
                for u in range(4):
                    stages[f"L{u}"] = lambda u=u: probs(u)
                run(tokens, stages, slab, None)
            ret_rounds(pool, per_round)

        FFN_PARTS = [(ph_ffn, 0, 8), (ph_ffn, 1, 8), (ph_ffn_end, 0, FF2_TILES - 16)]

        def ffn_part_sem(p, m):
            return (sem("h_new"), 3 * KT + m + 1) if p == 2 else (sem("ffn_part"), 8 * p + m + 1)

        def ffn_pe(pe):
            for p, (ph, i, n) in enumerate(FFN_PARTS):
                for t in range(n):
                    for g in range(2):
                        if p == 0 and t == 0 and g == 0:
                            pe.wait_ge(sem("u_lo"), 4 * KT)
                            pe.wait_ge(sem("h_new"), 3 * KT)
                        if t > 0:
                            pe.wait_ge(sem("ffn_scaled"), 2 * (8 * p + t - 1) + g + 1)
                        elif p > 0:
                            pe.wait_ge(*ffn_part_sem(p - 1, 6 + g))
                        slab_products(pe, ph, i, 2 * t + g, bank_slab[g][:], u_hi, u_lo)
                        if p == 0 and t == 0 and g == 0:
                            norm_pe(pe, 3)
                        if p == 0 and t == 0 and g == 1:
                            norm_pe_row(pe, 3)
                for m in range(KT):
                    if m < 2:
                        pe.wait_ge(sem("ffn_scaled"), 2 * (8 * p + n - 1) + m + 1)
                    else:
                        pe.wait_ge(*ffn_part_sem(p, m - 2))
                    for k in range(n):
                        if m == 0:
                            pe.wait_ge(sem("ffn_lo"), 8 * p + k + 1)
                        slab_products(pe, ph, i, 2 * n + m, bank_slab[m % 2][:], y_hi, y_lo, ks=(k,), n_k=n)
            norm_pe(pe, 4)
            norm_pe_row(pe, 4)

        def ffn_act(act):
            for p, (ph, i, n) in enumerate(FFN_PARTS):
                for j in range(2 * n + KT):
                    split_hi(act, ph, i, j + LEAD)
                    if j % 2 == 0 and j < 2 * n:
                        t = j // 2
                        act.wait_ge(sem("ffn_scaled"), 2 * (8 * p + t) + 1)
                        act.activation(tmp[4 + t % 2][:], tmp[t % 2][:], ACT.Tanh, scale=0.5)\
                            .then_inc(sem("ffn_tanh"), 1)
                    if j % 2 == 1 and 3 <= j <= 2 * n + 1:
                        t = (j - 3) // 2
                        act.wait_ge(sem("ffn_act"), 8 * p + t + 1)
                        act.activation(y_hi[:, t, :], tmp[2 + t % 2][:], ACT.Copy, scale=0.5).then_inc(sem("ffn_hi"), 1)

        def ffn_dve(dve):
            for p, (ph, i, n) in enumerate(FFN_PARTS):
                def lo(t):
                    dve.wait_ge(sem("ffn_hi"), 8 * p + t + 1)
                    dve.scalar_tensor_tensor(out=y_lo[:, t, :], in0=tmp[2 + t % 2][:], scalar=0.5,
                                             in1=y_hi[:, t, :].bitcast(F32), op0=ALU.mult, op1=ALU.subtract)\
                        .then_inc(sem("ffn_lo"), 1)
                for t in range(n):
                    g, u, th_ = tmp[t % 2], tmp[2 + t % 2], tmp[4 + t % 2]
                    q = 8 * p + t
                    dve.wait_ge(s_used, ph.index(i, 2 * t) + 1)
                    dve.tensor_tensor(g[:], bank_slab[0][:], r_row[:], ALU.mult).then_inc(sem("ffn_scaled"), 1)
                    if t >= 1:
                        lo(t - 1)
                    dve.wait_ge(sem("ffn_tanh"), q + 1)
                    dve.scalar_tensor_tensor(out=g[:], in0=th_[:], scalar=1.0, in1=g[:], op0=ALU.add, op1=ALU.mult)\
                        .then_inc(sem("ffn_silu"), 1)
                    dve.wait_ge(s_used, ph.index(i, 2 * t + 1) + 1)
                    dve.tensor_tensor(u[:], bank_slab[1][:], r_row[:], ALU.mult).then_inc(sem("ffn_scaled"), 1)
                    dve.wait_ge(sem("ffn_scaled"), 2 * q + 2)
                    dve.wait_ge(sem("ffn_silu"), q + 1)
                    dve.tensor_tensor(u[:], u[:], g[:], ALU.mult).then_inc(sem("ffn_act"), 1)
                lo(n - 1)
                for m in range(KT):
                    dve.wait_ge(s_used, ph.index(i, 2 * n + m) + 1)
                    dve.tensor_tensor(h_res[:, m, :], h_res[:, m, :], bank_slab[m % 2][:], ALU.add)\
                        .then_inc(ffn_part_sem(p, m)[0], 1)
            norm_dve(dve, 4)
            norm_dve_row(dve, 4)
            for m in range(KT):
                dve.scalar_tensor_tensor(out=h_res[:, m, :], in0=h_res[:, m, :], scalar=gains[:, 4, m:m + 1],
                                         in1=r_row[:], op0=ALU.mult, op1=ALU.mult).then_inc(sem("result"), 1)

        def ffn_pool(pool):
            for p, (ph, i, n) in enumerate(FFN_PARTS):
                for j in range(2 * n + KT):
                    split_lo(pool, ph, i, j + LEAD)
                    if p == 2 and j > 2 * n:
                        norm_pool_square(pool, 4, j - 2 * n - 1)
            norm_pool_square(pool, 4, KT - 1)
            norm_pool_scale(pool, 4)

        def after_heads_pe(pe, tiles, transposes):
            merge_pe(pe, ph_merge1, 0)
            out_pe(pe, ph_out1, 0, 1)
            mlp_pe(pe)
            ret_pe(pe, tiles, transposes)
            merge_pe(pe, ph_merge2, 1)
            out_pe(pe, ph_out2, 1, 3)
            ffn_pe(pe)

        def after_heads_act(act):
            merge_act(act, ph_merge1, 0)
            out_act(act, ph_out1, 1)
            mlp_act(act)
            ret_act(act)
            merge_act(act, ph_merge2, 1)
            out_act(act, ph_out2, 3)
            ffn_act(act)

        def after_heads_pool(pool):
            merge_pool(pool, ph_merge1)
            out_pool(pool, ph_out1, 1)
            mlp_pool(pool)
            ret_pool(pool)
            merge_pool(pool, ph_merge2)
            out_pool(pool, ph_out2, 3)
            ffn_pool(pool)

        def after_heads_dve(dve, step):
            dve.wait_ge(sem("oa"), HEADS)
            dve.wait_ge(sem("ob"), HEADS)
            dve.tensor_scalar(ms_col[:, 0:1], ms_col[:, 0:1], 1.0, None, ALU.mult).then_inc(sem("branches_done"), 1)
            branches_lo(dve, 0)
            merge_dve(dve, ph_merge1, 0)
            out_dve(dve, ph_out1, 1)
            mlp_dve(dve)
            ret_dve(dve, step)
            branches_lo(dve, 1)
            merge_dve(dve, ph_merge2, 1, bias_gate)
            out_dve(dve, ph_out2, 3)
            ffn_dve(dve)

        block = ctx.enter_context(nc.Block())

        @block.sync
        def _(sp):
            h_view = dram["x_t"].rearrange("(k p) t -> p k t", p=P)
            for name, dst, src in (
                ("ld_x", h_res[:], h_view),
                ("ld_small", gains[:], dram["gains"]), ("ld_small", head_gain[:], dram["head_gain"]),
                ("ld_small", ident[:], dram["ident"]), ("ld_small", w_gates[:], dram["w_gates"]),
                ("ld_small", gate_rows[:], dram["gate_rows"].to_broadcast([P, 3, HEADS])),
                ("ld_head", upper[:], dram["upper"]), ("ld_head", level_mask[:], dram["level_mask"]),
                ("ld_head", neg_mask[:], dram["neg_mask"]), ("ld_head", conv_w[:], dram["conv_w"])):
                sp.dma_start(dst, src).then_inc(sem(name), 16)
            for j in range(ph_heads.n):
                s = ph_heads.slot(j)
                if j >= SLOTS:
                    sp.wait_ge(s_lo, j - SLOTS + 1)
                sp.dma_start(raw[s][:].rearrange("p k c -> p (k c)"), dram["slabs"][j, :, :]).then_inc(s_raw[s], 16)
            for ph in phases:
                if ph is ph_mlp:
                    sp.wait_ge(sem("branch_taken"), 2 * KT + 1)
                    for name, dst in TAB2:
                        sp.dma_start(dst[:], dram[name]).then_inc(sem("ld_tab2"), 16)
                if ph is ph_out1:
                    sp.wait_ge(sem("branches_done"), 1)
                    sp.dma_start(h_res[:], h_view).then_inc(sem("ld_x"), 16)
                start = 1 if ph is ph_heads else 0
                if ph.iters - start > 1:
                    with sp.Fori(start, ph.iters) as i:
                        for j in range(ph.n):
                            load_slab(sp, ph, i, j)
                else:
                    for j in range(ph.n):
                        load_slab(sp, ph, start, j)
            last = phases[-1]
            for j in range(LEAD):
                load_slab(sp, last, last.iters, j)

            for m in range(KT):
                sp.wait_ge(sem("result"), m + 1)
                sp.dma_start(out[m * P:(m + 1) * P, :], h_res[:, m, :]).then_inc(sem("stored"), 16)
            sp.wait_ge(sem("stored"), 16 * KT)

        @block.tensor
        def _(pe):
            pe.wait_ge(sem("ld_x"), 16)
            pe.wait_ge(sem("setup_dve"), 1)
            for n in range(NT):
                for k in range(KT):
                    mm = pe.matmul(bA[:, 24 * n:24 * n + 24], h_res[:, k, n * P:(n + 1) * P], w_gates[:, k, :],
                                   start=k == 0, stop=k == KT - 1)
            mm.then_inc(sem("setup_ps"), 1)
            norm_pe(pe, 0)
            norm_pe_row(pe, 0)
            pe.wait_ge(sem("setup_dve"), 3)
            pe.wait_ge(sem("ld_head"), 64)
            g_all = table[:, :, Q_G, :]
            pe.matmul(bB[:, 0:HEADS * NT].rearrange("p (h n) -> p h n", n=NT), upper[:], g_all, start=True, stop=True)
            pe.matmul(bC[:, 0:HEADS * NT].rearrange("p (h n) -> p h n", n=NT), ones[:], g_all, start=True, stop=True)\
                .then_inc(sem("setup_ps"), 1)

            def tiles(out_, lhs, rhs, start=True, stop=True):
                for n in range(NT):
                    c = slice(n * P, (n + 1) * P)
                    mm = pe.matmul(out_[:, c], lhs[:, c], rhs[:, c], start=start, stop=stop)
                return mm

            def transposes(out_, in_, n=NT):
                for k in range(n):
                    c = slice(k * P, (k + 1) * P)
                    mm = pe.transpose(out_[:, c], in_[:, c], ident[:])
                return mm

            def head_round(tokens, i, c):
                def slab(j, t):
                    bank = bank_slab[HEAD_BANK[j]]
                    if t == 0:
                        if i is not None and not (isinstance(i, int) and i == 0 and j < 2):
                            pe.wait_ge(s_taken, ph_heads.index(i, j) - (1 if j == 0 else 2) + 1)
                        if isinstance(i, int) and i == 0 and j == 0:
                            pe.wait_ge(sem("u_lo"), KT)
                    slab_products(pe, ph_heads, i, j, bank[:], u_hi, u_lo, ks=(2 * t, 2 * t + 1))

                def ssq():
                    for x in range(4):
                        pe.wait_ge(sem("sq"), 4 * c + x + 1)
                        for n in range(NT):
                            mm = pe.matmul(bA[:, 4 * x + n:4 * x + n + 1], sq[x % 2][:, n * P:(n + 1) * P],
                                           ones[:, 0:1], start=True, stop=True)
                        mm.then_inc(sem("ssq_ps"), 1)

                def fvt_():
                    pe.wait_ge(s_taken, 7 * c + 7)
                    transposes(bD, raw_fv).then_inc(sem("fvt_ps"), 1)

                def rows():
                    pe.wait_ge(sem("diag"), 5 * c + 1)
                    pe.matmul(bB[:], ones[:], d_g[:], start=True, stop=True).then_inc(sem("row_ps"), 1)
                    pe.wait_ge(sem("diag"), 5 * c + 2)
                    pe.matmul(bC[:], ones[:], d_b[:], start=True, stop=True).then_inc(sem("row_ps"), 1)
                    pe.wait_ge(sem("diag"), 5 * c + 3)
                    pe.matmul(bA[:], ones[:], d_q[:], start=True, stop=True).then_inc(sem("row_ps"), 1)

                def frows():
                    pe.wait_ge(sem("diag"), 5 * c + 4)
                    pe.matmul(bE[:], ones[:], d_rk[:], start=True, stop=True).then_inc(sem("fox_rows_ps"), 1)
                    pe.wait_ge(sem("diag"), 5 * c + 5)
                    pe.wait_ge(sem("fvt"), c + 1)
                    pe.matmul(bD[:], ones[:], d_cum[:], start=True, stop=True).then_inc(sem("fox_rows_ps"), 1)

                def tkv():
                    pe.wait_ge(sem("dif"), c + 1)
                    transposes(bB, ck).then_inc(sem("tk_tv_ps"), 1)
                    pe.wait_ge(sem("decays"), 2 * c + 1)
                    transposes(bC, cv).then_inc(sem("tk_tv_ps"), 1)

                def kkqk():
                    pe.wait_ge(sem("decays"), 2 * c + 2)
                    tiles(bA, ck, ck).then_inc(sem("kk_qk_ps"), 1)
                    pe.wait_ge(sem("kv_scaled"), 2 * c + 1)
                    tiles(bB, ck, cq).then_inc(sem("kk_qk_ps"), 1)

                def xt():
                    pe.wait_ge(sem("kv_scaled"), 2 * c + 2)
                    pe.wait_ge(sem("z0"), c + 1)
                    transposes(bC, zi).then_inc(sem("x0_ps"), 1)

                def level_y(l):
                    pe.wait_ge(sem("atm"), 7 * c + l + 1)
                    if l == 1:
                        pe.wait_ge(sem("x0"), c + 1)
                        pe.wait_ge(sem("masked"), 2 * c + 1)
                    else:
                        pe.wait_ge(sem("x_new"), 5 * c + l - 1)
                    tiles(bA, atm[l % 2], xi).then_inc(sem("y_ps"), 1)

                def level_x(l):
                    pe.wait_ge(sem("y"), 6 * c + l)
                    if l == 1:
                        pe.wait_ge(sem("masked"), 2 * c + 2)
                    if l > 1:
                        pe.wait_ge(sem("z_new"), 6 * c + l - 1)
                    if l < LEVELS - 1:
                        tiles(bB, zi, yi).then_inc(sem("xy_ps"), 1)
                    tiles(bC, yi, zi).then_inc(sem("zy_ps"), 1)

                def vk():
                    pe.wait_ge(sem("z_new"), 6 * c + 6)
                    tiles(bA, zi, vp).then_inc(sem("val_kc_ps"), 1)
                    tiles(bB, kp, zi).then_inc(sem("val_kc_ps"), 1)

                def rec(n):
                    c_ = slice(n * P, (n + 1) * P)
                    if n == 0:
                        pe.wait_ge(sem("val"), c + 1)
                        pe.wait_ge(sem("kc"), c + 1)
                        pe.matmul(bC[:, c_], vp[:, c_], att[:, c_], start=True, stop=True)
                        pe.matmul(bB[:, 0:P], kd[:, c_], vp[:, c_], start=True, stop=True).then_inc(sem("s_ps"), 1)
                        return
                    pe.wait_ge(sem("s_new"), 3 * c + n)
                    pe.matmul(bA[:, 0:P], kp[:, c_], st[:], start=True, stop=True).then_inc(sem("vn_ps"), 1)
                    pe.matmul(bC[:, c_], st[:], qdec[:, c_], start=True, stop=False)
                    pe.wait_ge(sem("v_new"), 3 * c + n)
                    mm = pe.matmul(bC[:, c_], vn[:], att[:, c_], start=False, stop=True)
                    if n < NT - 1:
                        pe.matmul(bB[:, 0:P], kd[:, c_], vn[:], start=True, stop=True).then_inc(sem("s_ps"), 1)
                    else:
                        mm.then_inc(sem("o_ps"), 1)

                def osq():
                    pe.wait_ge(sem("o_read"), 2 * c + 1)
                    for n in range(NT):
                        mm = pe.matmul(bA[:, n:n + 1], sq[0][:, n * P:(n + 1) * P], ones[:, 0:1], start=True, stop=True)
                    mm.then_inc(sem("o_norm_ps"), 1)

                def orow():
                    pe.wait_ge(sem("odiag"), c + 1)
                    pe.matmul(bA[:], ones[:], d_b[:], start=True, stop=True).then_inc(sem("o_norm_ps"), 1)

                def logits(i_):
                    w = (i_ + 1) * P
                    if i_ == 0:
                        for name in ("fk", "fq", "cumr"):
                            pe.wait_ge(sem(name), c + 1)
                    else:
                        pe.wait_ge(sem("nmax"), 4 * c + i_)
                    pe.matmul(bD[:, 0:w], fqt[:, i_ * P:w], fkt[:, 0:w], start=True, stop=True).then_inc(sem("l_ps"), 1)

                def probs_t(i_):
                    pe.wait_ge(sem("probs"), 4 * c + i_ + 1)
                    if i_ > 0:
                        pe.wait_ge(sem("pt"), 4 * c + i_)
                    transposes(bE, pr, i_ + 1).then_inc(sem("pt_ps"), 1)

                def outs(i_):
                    pe.wait_ge(sem("pt"), 4 * c + i_ + 1)
                    if i_ == 0:
                        pe.wait_ge(s_taken, 7 * c + 7)
                    for j in range(i_ + 1):
                        mm = pe.matmul(bF[:, i_ * P:(i_ + 1) * P], fvt[:, j * P:(j + 1) * P], pt[:, j * P:(j + 1) * P],
                                       start=j == 0, stop=j == i_)
                    if i_ == NT - 1:
                        mm.then_inc(sem("fo_ps"), 1)

                stages = {"ssq": ssq, "fvt": fvt_, "rows": rows, "frows": frows, "tkv": tkv, "kkqk": kkqk, "xt": xt,
                          "vk": vk, "osq": osq, "orow": orow}
                for l in range(1, LEVELS):
                    stages[f"Y{l}"] = lambda l=l: level_y(l)
                    stages[f"X{l}"] = lambda l=l: level_x(l)
                for n in range(NT):
                    stages[f"r{n}"] = lambda n=n: rec(n)
                    stages[f"S{n}"] = lambda n=n: logits(n)
                    stages[f"T{n}"] = lambda n=n: probs_t(n)
                    stages[f"O{n}"] = lambda n=n: outs(n)
                run(tokens, stages, slab, None)

            head_rounds(pe, head_round)
            after_heads_pe(pe, tiles, transposes)

        @block.scalar
        def _(act):
            step = Steps(act, sem("act_step"))
            for j in range(LEAD):
                split_hi(act, ph_heads, 0, j)
            act.wait_ge(sem("ld_x"), 16)
            act.wait_ge(sem("ld_small"), 80)
            for k in range(KT):
                part_hi(act, 0, k)
            act.wait_ge(sem("setup_dve"), 2)
            step(act.activation(e2[:], e2[:], ACT.Exp))
            act.activation(sp2[:], e2[:], ACT.Ln, bias=1.0).then_inc(sem("setup_act"), 1)
            act.activation(gate_rows[:, 1, :], gate_rows[:, 1, :], ACT.Exp).then_inc(sem("setup_act"), 1)
            act.activation(t8[:], gt[:, :, 8:16].rearrange("p n h -> p h n"), ACT.Tanh, scale=0.5)\
                .then_inc(sem("setup_act"), 1)
            act.wait_ge(sem("setup_dve"), 4)
            act.activation(table[:, :, Q_EGL, :], gtot[:], ACT.Exp).then_inc(sem("setup_act"), 1)
            act.activation(t8[:], table[:, :, Q_GCUM, :], ACT.Exp).then_inc(sem("setup_act"), 1)

            def head_round(tokens, i, c):
                if c is not None:
                    step.rounds(step_base[0], 0, c)

                def slab(j, t):
                    if t == 0:
                        split_hi(act, ph_heads, i, j + LEAD)

                def tanh(x):
                    if x < 3:
                        act.wait_ge(sem("conv"), 3 * c + x + 1)
                    else:
                        act.wait_ge(s_taken, 7 * c + 4)
                    if x >= 2:
                        act.wait_ge(sem("silu"), 4 * c + x - 1)
                    act.activation(th[x % 2][:], (cq, ck, cv, raw_z)[x][:], ACT.Tanh, scale=0.5).then_inc(sem("tanh"), 1)

                def squares(pair):
                    if pair == 0:
                        for x, src in ((0, cq), (1, ck)):
                            act.wait_ge(sem("silu"), 4 * c + x + 1)
                            act.activation(sq[x][:], src[:], ACT.Square).then_inc(sem("sq"), 1)
                    else:
                        act.wait_ge(s_taken, 7 * c + 6)
                        for x, src in ((2, raw_fq), (3, raw_fk)):
                            act.wait_ge(sem("ssq_ps"), 4 * c + x - 1)
                            act.activation(sq[x % 2][:], src[:], ACT.Square).then_inc(sem("sq"), 1)
                        act.activation(fqt[:], raw_fq[:], ACT.Copy, scale=head_gain[:, 1:2]).then_inc(sem("fq"), 1)

                def fvt_():
                    act.wait_ge(sem("fvt_ps"), c + 1)
                    act.copy(fvt[:], bD[:]).then_inc(sem("fvt"), 1)

                def rows():
                    act.wait_ge(sem("row_ps"), 3 * c + 1)
                    act.activation(e_g[:], bB[:], ACT.Exp).then_inc(sem("eg"), 1)

                def dif():
                    act.wait_ge(sem("dif"), c + 1)
                    act.activation(dt_[:], dt_[:], ACT.Exp).then_inc(sem("edif"), 1)

                def frows():
                    act.wait_ge(sem("fox_rows_ps"), 2 * c + 2)
                    act.copy(cumr[:], bD[:]).then_inc(sem("cumr"), 1)

                def xt():
                    act.wait_ge(sem("x0_ps"), c + 1)
                    act.copy(xi[:], bC[:]).then_inc(sem("x0"), 1)

                def level_y(l):
                    act.wait_ge(sem("y_ps"), 6 * c + l)
                    act.copy(yi[:], bA[:]).then_inc(sem("y"), 1)

                def vk():
                    act.wait_ge(sem("val_kc_ps"), 2 * c + 1)
                    act.copy(vp[:], bA[:]).then_inc(sem("val"), 1)

                def osq():
                    act.wait_ge(sem("o_ps"), c + 1)
                    act.activation(sq[0][:], bC[:], ACT.Square).then_inc(sem("o_read"), 1)
                    act.activation(on[:], bC[:], ACT.Copy, scale=head_gain[:, 0:1]).then_inc(sem("o_read"), 1)

                def probs(i_):
                    w = (i_ + 1) * P
                    act.wait_ge(sem("nmax"), 4 * c + i_ + 1)
                    if i_ > 0:
                        act.wait_ge(sem("pt_ps"), 4 * c + i_)
                    act.activation(pr[:, 0:w], sb_[:, 0:w], ACT.Exp, bias=nmax[:, i_:i_ + 1],
                                   accum_out=lsum[:, i_:i_ + 1]).then_inc(sem("exp"), 1)

                def probs_t(i_):
                    w = (i_ + 1) * P
                    act.wait_ge(sem("pt_ps"), 4 * c + i_ + 1)
                    act.copy(pt[:, 0:w], bE[:, 0:w]).then_inc(sem("pt"), 1)

                stages = {"sq0": lambda: squares(0), "sq1": lambda: squares(1), "fvt": fvt_, "rows": rows, "dif": dif,
                          "frows": frows, "xt": xt, "vk": vk, "osq": osq}
                for x in range(4):
                    stages[f"th{x}"] = lambda x=x: tanh(x)
                for l in range(1, LEVELS):
                    stages[f"Y{l}"] = lambda l=l: level_y(l)
                for n in range(NT):
                    stages[f"S{n}"] = lambda n=n: probs(n)
                    stages[f"T{n}"] = lambda n=n: probs_t(n)
                run(tokens, stages, slab, None)

            step_base = [0]
            head_rounds(act, head_round)
            after_heads_act(act)

        @block.vector
        def _(dve):
            step = Steps(dve, sem("dve_step"))
            dve.memset(ones[:], 1.0)
            for n, name in enumerate(("gate_taken", "branch_taken", "merged")):
                dve.memset(rawq[n][:, 0:3], 0.0).then_inc(sem(name), 1)
            dve.wait_ge(sem("ld_small"), 80)
            step(dve.tensor_scalar(head_gain[:, 0:1], head_gain[:, 0:1], 0.5, None, ALU.mult))
            dve.tensor_tensor(w_gates[:], w_gates[:], gains[:, 0, :].unsqueeze(2).to_broadcast([P, KT, 24]),
                              ALU.mult).then_inc(sem("setup_dve"), 1)
            dve.wait_ge(sem("ld_x"), 16)
            for k in range(KT):
                part_lo(dve, 0, k)
            norm_dve(dve, 0)
            norm_dve_row(dve, 0)
            dve.wait_ge(sem("setup_ps"), 1)
            step(dve.tensor_tensor(gt[:], bA[:, 0:96].rearrange("p (n c) -> p n c", n=NT),
                                   r_col[:].unsqueeze(2).to_broadcast([P, NT, 24]), ALU.mult))

            def row(q):
                return gate_rows[:, q, :].unsqueeze(2).to_broadcast([P, HEADS, NT])

            def heads_of(c):
                return gt[:, :, c:c + HEADS].rearrange("p n h -> p h n")

            dve.tensor_tensor(y2[:, 0:HEADS, :], heads_of(0), row(0), ALU.add)
            step(dve.tensor_tensor(y2[:, HEADS:, :], heads_of(16), row(2), ALU.add))
            step(dve.tensor_scalar(y2[:, HEADS:, :], y2[:, HEADS:, :], -1.0, None, ALU.mult))
            dve.scalar_tensor_tensor(out=e2[:], in0=y2[:], scalar=-1.0, in1=y2[:], op0=ALU.mult, op1=ALU.min)\
                .then_inc(sem("setup_dve"), 1)
            dve.wait_ge(sem("setup_act"), 1)
            step(dve.scalar_tensor_tensor(out=sp2[:], in0=y2[:], scalar=0.0, in1=sp2[:], op0=ALU.max, op1=ALU.add))
            dve.wait_ge(sem("setup_act"), 2)
            dve.scalar_tensor_tensor(out=table[:, :, Q_G, :], in0=sp2[:, 0:HEADS, :], scalar=-1.0, in1=row(1),
                                     op0=ALU.mult, op1=ALU.mult).then_inc(sem("setup_dve"), 1)
            step(dve.tensor_scalar(table[:, :, Q_LF, :], sp2[:, HEADS:, :], -1.0, None, ALU.mult))
            dve.wait_ge(sem("setup_act"), 3)
            dve.tensor_scalar(table[:, :, Q_BETA, :], t8[:], 0.5, 0.5, ALU.mult, ALU.add)
            step(dve.memset(table[:, :, Q_LFPREV, 0:1], 0.0))
            for n in range(1, NT):
                step(dve.tensor_tensor(table[:, :, Q_LFPREV, n:n + 1], table[:, :, Q_LFPREV, n - 1:n],
                                       table[:, :, Q_LF, n - 1:n], ALU.add))
            dve.wait_ge(sem("setup_ps"), 2)
            step(dve.tensor_copy(table[:, :, Q_GCUM, :], bB[:, 0:HEADS * NT].rearrange("p (h n) -> p h n", n=NT)))
            dve.tensor_tensor(gtot[:], bC[:, 0:HEADS * NT].rearrange("p (h n) -> p h n", n=NT),
                              table[:, :, Q_GCUM, :], ALU.subtract).then_inc(sem("setup_dve"), 1)
            dve.wait_ge(sem("setup_act"), 5)
            step(dve.tensor_tensor(table[:, :, Q_BEG, :], t8[:], table[:, :, Q_BETA, :], ALU.mult))
            dve.wait_ge(sem("ld_head"), 64)
            dve_start = step.n

            def head_round(tokens, i, c):
                if c is not None:
                    step.rounds(dve_start, DVE_STEPS, c)

                def evac(j):
                    dst = (rawq[0], rawq[1], rawq[2], raw_z, raw_fq, raw_fk, raw_fv)[j]
                    dst = dst[:, 3:3 + T] if j < 3 else dst[:]
                    dve.wait_ge(s_used, ph_heads.index(i, j) + 1)
                    if c is not None and j == 4:
                        dve.wait_ge(sem("fq"), c + 1)
                    if c is not None and j == 6:
                        dve.wait_ge(sem("fvt_ps"), c + 1)
                    dve.tensor_tensor(dst, bank_slab[HEAD_BANK[j]][:], r_row[:], ALU.mult).then_inc(s_taken, 1)

                def conv(x):
                    if x == 0:
                        dve.wait_ge(s_taken, 7 * c + 7)
                        step(dve.tensor_scalar(h_conv[:], conv_w[:, bass.ds(c, 1), :].rearrange("p a w -> p (a w)"),
                                               1.0, None, ALU.mult))
                        step(dve.tensor_scalar(h_small[:].rearrange("p q n -> p (q n)"),
                                               table[:, bass.ds(c, 1), :, :].rearrange("p a q n -> p (a q n)"),
                                               1.0, None, ALU.mult))
                    dst = (cq, ck, cv)[x]
                    step(dve.tensor_scalar(dst[:], rawq[x][:, 0:T], h_conv[:, 4 * x:4 * x + 1], None, ALU.mult))
                    for w in range(1, 4):
                        ins = dve.scalar_tensor_tensor(out=dst[:], in0=rawq[x][:, w:w + T],
                                                       scalar=h_conv[:, 4 * x + w:4 * x + w + 1], in1=dst[:],
                                                       op0=ALU.mult, op1=ALU.add)
                        if w < 3:
                            step(ins)
                        else:
                            ins.then_inc(sem("conv"), 1)

                def silu(x):
                    dve.wait_ge(sem("tanh"), 4 * c + x + 1)
                    src, dst = ((cq, cq), (ck, ck), (cv, cv), (raw_z, sz))[x]
                    dve.scalar_tensor_tensor(out=dst[:], in0=th[x % 2][:], scalar=1.0, in1=src[:], op0=ALU.add,
                                             op1=ALU.mult).then_inc(sem("silu"), 1)

                def cols_():
                    dve.wait_ge(sem("ssq_ps"), 4 * c + 4)
                    dve.tensor_scalar(ssc[:, 0:8], bA[:, 0:8], 4 * EPS, None, ALU.add)
                    dve.tensor_scalar(ssc[:, 8:16], bA[:, 8:16], 1.0 / P, EPS, ALU.mult, ALU.add)\
                        .then_inc(sem("ssc"), 1)
                    dve.wait_ge(sem("rsc"), c + 1)
                    rk = rsc[:, 4:8]
                    dve.tensor_tensor(cols[:, C_BK, :], h_small[:, Q_BETA, :], rk, ALU.mult)
                    dve.tensor_tensor(cols[:, C_KB, :], h_small[:, Q_BEG, :], rk, ALU.mult)
                    dve.tensor_tensor(cols[:, C_KD, :], h_small[:, Q_EGL, :], rk, ALU.mult)
                    dve.tensor_scalar(cols[:, C_RQ, :], rsc[:, 0:4], SCALE, None, ALU.mult)
                    dve.tensor_scalar(cols[:, C_RFQ, :], rsc[:, 8:12], SCALE, None, ALU.mult)
                    dve.tensor_scalar(cols[:, C_VB, :], h_small[:, Q_BETA, :], 0.5, None, ALU.mult)\
                        .then_inc(sem("cols"), 1)
                    dve.wait_ge(sem("cols"), c + 1)

                def dif():
                    dve.wait_ge(sem("eg"), c + 1)
                    step(dve.tensor_tensor(c4(dt_[:]), c4(bB[:]), over_cols(h_small[:, Q_GCUM, :]), ALU.subtract))
                    dve.tensor_scalar(dt_[:], dt_[:], 0.0, None, ALU.min).then_inc(sem("dif"), 1)
                    dve.tensor_scalar(dec[:], e_g[:, P - 1:T:P], 1.0, None, ALU.mult)

                def dt():
                    dve.wait_ge(sem("edif"), c + 1)
                    step(dve.scalar_tensor_tensor(out=c4(dt_[:]), in0=c4(dt_[:]), scalar=1.0, in1=over_tiles(upper[:]),
                                                  op0=ALU.min, op1=ALU.mult))
                    step(dve.tensor_tensor(c4(dt_[:]), c4(dt_[:]), over_cols(rsc[:, 4:8]), ALU.mult))
                    dve.wait_ge(sem("row_ps"), 3 * c + 3)
                    dve.tensor_tensor(bdt[:], bC[:], dt_[:], ALU.mult).then_inc(sem("decays"), 1)
                    dve.tensor_tensor(adt[:], bA[:], dt_[:], ALU.mult)
                    dve.tensor_tensor(e_g[:], bA[:], e_g[:], ALU.mult).then_inc(sem("decays"), 1)
                    dve.wait_ge(sem("decays"), 2 * c + 2)
                    step(dve.tensor_tensor(qdec[:], e_g[:], cq[:], ALU.mult))

                def frows():
                    dve.wait_ge(sem("fox_rows_ps"), 2 * c + 1)
                    dve.scalar_tensor_tensor(out=fkt[:], in0=raw_fk[:], scalar=head_gain[:, 2:3], in1=bE[:],
                                             op0=ALU.mult, op1=ALU.mult).then_inc(sem("fk"), 1)

                def tkv():
                    dve.wait_ge(sem("tk_tv_ps"), 2 * c + 1)
                    dve.tensor_tensor(c4(kp[:]), c4(bB[:]), over_cols(cols[:, C_KB, :]), ALU.mult)
                    dve.tensor_tensor(c4(kd[:]), c4(bB[:]), over_cols(cols[:, C_KD, :]), ALU.mult)\
                        .then_inc(sem("kv_scaled"), 1)
                    dve.wait_ge(sem("tk_tv_ps"), 2 * c + 2)
                    dve.tensor_tensor(c4(vp[:]), c4(bC[:]), over_cols(cols[:, C_VB, :]), ALU.mult)\
                        .then_inc(sem("kv_scaled"), 1)

                def kkqk():
                    dve.wait_ge(sem("kk_qk_ps"), 2 * c + 1)
                    dve.tensor_tensor(a_t[:], bA[:], bdt[:], ALU.mult).then_inc(sem("masked"), 1)
                    dve.wait_ge(sem("kk_qk_ps"), 2 * c + 2)
                    dve.tensor_tensor(att[:], bB[:], adt[:], ALU.mult).then_inc(sem("masked"), 1)

                def z0():
                    dve.wait_ge(sem("atm"), 7 * c + 1)
                    dve.tensor_tensor(c4(zi[:]), over_tiles(ident[:]), c4(atm[0][:]), ALU.subtract)\
                        .then_inc(sem("z0"), 1)

                def level_x(l):
                    if l < LEVELS - 1:
                        dve.wait_ge(sem("xy_ps"), 5 * c + l)
                        dve.tensor_tensor(xi[:], xi[:], bB[:], ALU.subtract).then_inc(sem("x_new"), 1)
                    dve.wait_ge(sem("zy_ps"), 6 * c + l)
                    dve.tensor_tensor(zi[:], zi[:], bC[:], ALU.subtract).then_inc(sem("z_new"), 1)

                def vk():
                    dve.wait_ge(sem("val_kc_ps"), 2 * c + 2)
                    dve.tensor_copy(kp[:], bB[:]).then_inc(sem("kc"), 1)

                def rec(n):
                    if n > 0:
                        dve.wait_ge(sem("vn_ps"), 3 * c + n)
                        dve.tensor_tensor(vn[:], vp[:, n * P:(n + 1) * P], bA[:, 0:P], ALU.subtract)\
                            .then_inc(sem("v_new"), 1)
                    if n < NT - 1:
                        dve.wait_ge(sem("s_ps"), 3 * c + n + 1)
                        if n == 0:
                            dve.wait_ge(sem("val"), c + 1)
                            dve.tensor_copy(st[:], bB[:, 0:P]).then_inc(sem("s_new"), 1)
                        else:
                            dve.scalar_tensor_tensor(out=st[:], in0=st[:], scalar=dec[:, n:n + 1], in1=bB[:, 0:P],
                                                     op0=ALU.mult, op1=ALU.add).then_inc(sem("s_new"), 1)

                def osq():
                    dve.wait_ge(sem("o_norm_ps"), 2 * c + 1)
                    dve.tensor_scalar(osc[:], bA[:, 0:NT], 1.0 / P, EPS, ALU.mult, ALU.add).then_inc(sem("osc"), 1)

                def orow():
                    dve.wait_ge(sem("o_norm_ps"), 2 * c + 2)
                    dve.wait_ge(sem("o_read"), 2 * c + 2)
                    step(dve.tensor_tensor(on[:], on[:], bA[:], ALU.mult))
                    dve.tensor_tensor(br_a[:, bass.ds(c, 1), :].rearrange("p a t -> p (a t)"), on[:], sz[:], ALU.mult)\
                        .then_inc(sem("oa"), 1)

                def logits(i_):
                    w = (i_ + 1) * P
                    dve.wait_ge(sem("l_ps"), 4 * c + i_ + 1)
                    if i_ == 0:
                        dve.wait_ge(sem("cumr"), c + 1)
                    step(dve.scalar_tensor_tensor(out=sb_[:, 0:w], in0=bD[:, 0:w], scalar=cols[:, C_RFQ, i_:i_ + 1],
                                                  in1=cumr[:, 0:w], op0=ALU.mult, op1=ALU.subtract))
                    step(dve.tensor_tensor(sb_[:, i_ * P:w], sb_[:, i_ * P:w], neg_mask[:], ALU.add))
                    dve.tensor_reduce(nmax[:, i_:i_ + 1], sb_[:, 0:w], AX.X, ALU.max, negate=True)\
                        .then_inc(sem("nmax"), 1)
                    dve.wait_ge(sem("exp"), 4 * c + i_ + 1)
                    step(dve.reciprocal(rsum[:, i_:i_ + 1], lsum[:, i_:i_ + 1]))
                    dve.tensor_scalar(pr[:, 0:w], pr[:, 0:w], rsum[:, i_:i_ + 1], None, ALU.mult)\
                        .then_inc(sem("probs"), 1)

                def outs(i_):
                    if i_ == NT - 1:
                        dve.wait_ge(sem("fo_ps"), c + 1)
                        dve.tensor_scalar(br_b[:, bass.ds(c, 1), :].rearrange("p a t -> p (a t)"), bF[:], 1.0, None,
                                          ALU.mult).then_inc(sem("ob"), 1)

                stages = {"cols": cols_, "dif": dif, "dt": dt, "frows": frows, "tkv": tkv, "kkqk": kkqk, "z0": z0,
                          "vk": vk, "osq": osq, "orow": orow}
                for x in range(4):
                    stages[f"sl{x}"] = lambda x=x: silu(x)
                    if x < 3:
                        stages[f"cv{x}"] = lambda x=x: conv(x)
                for l in range(1, LEVELS):
                    stages[f"X{l}"] = lambda l=l: level_x(l)
                for n in range(NT):
                    stages[f"r{n}"] = lambda n=n: rec(n)
                    stages[f"S{n}"] = lambda n=n: logits(n)
                    stages[f"O{n}"] = lambda n=n: outs(n)
                run(tokens, stages, None, evac)
                if c is not None:
                    assert step.n == DVE_STEPS, step.n

            head_rounds(dve, head_round)
            step.straight(dve_start + HEADS * DVE_STEPS)
            after_heads_dve(dve, step)

        @block.gpsimd
        def _(pool):
            pool.memset(mhalf[:], -0.5)
            for j in range(LEAD):
                split_lo(pool, ph_heads, 0, j)
            pool.wait_ge(sem("ld_x"), 16)
            pool.wait_ge(sem("ld_small"), 80)
            for k in range(KT):
                norm_pool_square(pool, 0, k)
            norm_pool_scale(pool, 0)

            def head_round(tokens, i, c):
                def slab(j, t):
                    if t == 0:
                        split_lo(pool, ph_heads, i, j + LEAD)

                def cols_():
                    pool.wait_ge(sem("ssc"), c + 1)
                    pool.tensor_tensor(rsc[:], ssc[:], mhalf[:], ALU.pow).then_inc(sem("rsc"), 1)

                def diag():
                    pool.wait_ge(sem("cols"), c + 1)
                    for dst, mat, col in ((d_g, upper, h_small[:, Q_G, :]), (d_b, ident, cols[:, C_BK, :]),
                                          (d_q, ident, cols[:, C_RQ, :]), (d_rk, ident, rsc[:, 12:16])):
                        pool.tensor_tensor(c4(dst[:]), over_tiles(mat[:]), over_cols(col), ALU.mult)\
                            .then_inc(sem("diag"), 1)
                    pool.tensor_tensor(c4(d_cum[:]), over_tiles(upper[:]), over_cols(h_small[:, Q_LF, :]), ALU.mult)\
                        .then_inc(sem("diag_part"), 1)
                    pool.wait_ge(sem("diag_part"), c + 1)
                    pool.tensor_tensor(c4(d_cum[:]), c4(d_cum[:]), over_cols(h_small[:, Q_LFPREV, :]), ALU.add)\
                        .then_inc(sem("diag"), 1)

                def level(l):
                    if l == 0:
                        pool.wait_ge(sem("masked"), 2 * c + 1)
                    elif l == 2:
                        pool.wait_ge(sem("z0"), c + 1)
                    elif l > 2:
                        pool.wait_ge(sem("y_ps"), 6 * c + l - 2)
                    pool.tensor_tensor(c4(atm[l % 2][:]), c4(a_t[:]), over_tiles(level_mask[:, l, :]), ALU.mult)\
                        .then_inc(sem("atm"), 1)

                def osq():
                    pool.wait_ge(sem("osc"), c + 1)
                    pool.tensor_tensor(ors[:], osc[:], mhalf[:, 0:NT], ALU.pow).then_inc(sem("ors"), 1)
                    pool.wait_ge(sem("ors"), c + 1)
                    pool.tensor_tensor(c4(d_b[:]), over_tiles(ident[:]), over_cols(ors[:]), ALU.mult)\
                        .then_inc(sem("odiag"), 1)

                stages = {"cols": cols_, "diag": diag, "osq": osq, "z0": lambda: (level(0), level(1))}
                for l in range(2, LEVELS):
                    stages[f"Y{l - 1}"] = lambda l=l: level(l)
                run(tokens, stages, slab, None)

            head_rounds(pool, head_round)
            after_heads_pool(pool)

    return nc


def slabs_of(weights):
    order = slab_order()
    out = np.zeros((len(order) + LEAD, P, KT, P), np.float32)
    for n, (name, k0, nk, col) in enumerate(order):
        w = weights[name][k0 * P:(k0 + nk) * P, col:col + P]
        out[n, :, :nk, :] = w.reshape(nk, P, P).transpose(1, 0, 2)
    return out.reshape(len(out), P, KT * P)


def constants():
    r, c = np.arange(P)[:, None], np.arange(P)[None, :]
    masks = [((c // b) % 2 == 1) & ((r // b) % 2 == 0) & (r // (2 * b) == c // (2 * b))
             for b in (2 ** l for l in range(LEVELS))]
    f = np.float32
    t = np.arange(T, dtype=f)

    def rotary(d):
        half = d // 2
        inv = (f(10000.0) ** (-np.arange(half, dtype=f) / f(half))).astype(f)
        ang = (t[None, :] * inv[:, None]).astype(f)
        feature = np.arange(P) % d
        sign = np.where(feature < half, -1.0, 1.0)[:, None].astype(f)
        return np.cos(ang)[feature % half].astype(f), (np.sin(ang)[feature % half] * sign).astype(f)

    cos_r, sin_r = rotary(P)
    cos_a, sin_a = rotary(64)
    log_gamma = np.log1p(-np.exp2(-5.0 - np.arange(RET_HEADS)))
    rel = (c - r)[:, None, :]
    decay_t = np.where(rel >= 0, np.exp(log_gamma[None, :, None] * np.maximum(rel, 0)), 0.0) * P ** -0.5
    q_decay = np.exp(log_gamma[None, :, None] * (np.arange(P)[None, None, :] + 1.0)) * P ** -0.5
    k_decay = np.stack([np.exp(log_gamma[None] * (P - 1.0 - np.arange(P)[:, None])),
                        np.broadcast_to(np.exp(log_gamma * P), (P, RET_HEADS))], 2)
    return {
        "cos_r": cos_r, "sin_r": sin_r, "cos_a": cos_a, "sin_a": sin_a,
        "swap_r": (c == (r + 64) % P).astype(f), "swap_a": (c == (r ^ 32)).astype(f),
        "dup0": (c % 64 == r).astype(f), "dup1": (c % 64 + 64 == r).astype(f),
        "decay_t": decay_t.astype(f), "q_decay": np.broadcast_to(q_decay, (P, RET_HEADS, P)).astype(f),
        "k_decay": k_decay.astype(f),
        "band": np.stack([np.where(c > r, 0.0, -1e30), np.where(c <= r, 0.0, -1e30)], 1).astype(f),
        "ident": np.eye(P, dtype=f),
        "upper": (r <= c).astype(f),
        "neg_mask": np.where(c <= r, 0.0, -1e30).astype(f),
        "level_mask": np.stack(masks, 1).astype(f),
    }


def arrays_of(inp):
    inp = {k: np.asarray(v) for k, v in inp.items()}
    w_in = inp["w_in"][0]
    g0 = 4 * D
    f0 = 4 * D + 16 + 3 * D
    gates = np.concatenate([w_in[:, g0:g0 + 16], w_in[:, f0:f0 + 8]], 1)

    b2 = inp["b_in_2"][0]

    def tiles(v):
        return v.reshape(KT, P).T

    a = {
        "x_t": np.ascontiguousarray(inp["x"][0].T),
        "slabs": slabs_of({k: inp[k][0] for k in (
            "w_in", "w_proj_gdn", "w_proj_fox", "w_out", "w_up", "w_down", "w_in_2", "w_ret_out_2", "w_attn_out_2",
            "w_out_2", "w_ffn_gate_2", "w_ffn_up_2", "w_ffn_down_2")}),
        "gains": np.stack([tiles(inp[k].reshape(-1)) for k in
                           ("norm_mix_g", "norm_mlp_g", "ln1_g_2", "ln2_g_2", "lnf_g_2")], 1),
        "head_gain": np.stack([inp[k][0] for k in ("gdn_norm_g", "fox_q_norm_g", "fox_k_norm_g")], 1),
        "w_gates": gates.reshape(KT, P, 24).transpose(1, 0, 2),
        "gate_rows": np.stack([inp["gdn_dt_bias"][0], inp["gdn_a_log"][0], inp["fox_f_bias"][0]])[None],
        "conv_w": inp["gdn_conv_w"][0].reshape(4, 3, HEADS, P).transpose(3, 2, 1, 0).reshape(P, HEADS, 12),
        **constants(),
        "bias_cols": np.stack([b2[c:c + P] for name, _, _, c in slab_order()
                               if name == "w_in_2" and c < 4352], 1),
        "bias_gate": b2[4352:].reshape(2 * KT, P).T,
        "ret_gain": inp["ret_norm_g_2"][0].reshape(RET_HEADS, 2, P).transpose(2, 0, 1),
        "sink_cols": np.broadcast_to(inp["attn_sinks_2"][0].reshape(RET_HEADS, 4), (P, RET_HEADS, 4)),
    }
    return {k: np.ascontiguousarray(v) for k, v in a.items()}


def kernel(**inputs):
    import concourse.bacc as bacc
    from concourse.bass_utils import run_bass_kernel_spmd

    nc = bacc.Bacc("TRN2", target_bir_lowering=False, num_devices=1)
    arrays = arrays_of(inputs)
    dram = {name: nc.dram_tensor(name, a.shape, mybir.dt.from_np(a.dtype), kind="ExternalInput").ap()
            for name, a in arrays.items()}
    out = nc.dram_tensor("out_t", (D, T), F32, kind="ExternalOutput").ap()
    program(nc, dram, out)
    r = run_bass_kernel_spmd(nc, [arrays], core_ids=[0])
    return np.ascontiguousarray(r.results[0]["out_t"].T)[None]
```

```python
from contextlib import ExitStack

import numpy as np

import concourse.bass as bass
from concourse import mybir
from concourse.alu_op_type import AluOpType as ALU

ACT = mybir.ActivationFunctionType
AX = mybir.AxisListType
F32 = mybir.dt.float32
F32R = mybir.dt.float32r

P = 128
T = 512
NT = T // P
D = 1024
KT = D // P
EPS = 1e-6
HEADS = 8
LEVELS = 7
SCALE = float(P) ** -0.5
SLOTS = 4
DVE_STEPS, LATE_STEPS = 28, 11
LEAD = 2

AHEAD = 2
RET_HEADS = 4
FF2_TILES = 22
KiB = 1024


def slab_order():
    order = []
    q, k, v, z = 0, D, 2 * D, 3 * D
    fq = 4 * D + 16
    fk, fv = fq + D, fq + 2 * D
    gate_a = fq + 3 * D + 8
    gate_b = gate_a + D
    for h in range(HEADS):
        order += [("w_in", 0, KT, base + h * P) for base in (q, k, v, fq, fk, fv, z)]
    for m in range(AHEAD):
        order += [("w_in", 0, KT, gate_a + m * P), ("w_in", 0, KT, gate_b + m * P)]
    for m in range(KT):
        if m >= AHEAD:
            order += [("w_in", 0, KT, gate_a + m * P), ("w_in", 0, KT, gate_b + m * P)]
        order += [("w_proj_gdn", 0, KT, m * P), ("w_proj_fox", 0, KT, m * P)]
    order += [("w_out", 0, KT, m * P) for m in range(KT)]
    for part in range(4):
        order += [("w_up", 0, KT, (8 * part + j) * P) for j in range(8)]
        order += [("w_down", 8 * part, KT, m * P) for m in range(KT)]
    rq, rk, rv, rg, aq, ak, av, ga = 0, 512, 1024, 2048, 3072, 4096, 4224, 4352
    order += [("w_in_2", 0, KT, ak), ("w_in_2", 0, KT, av)]
    for r in range(RET_HEADS):
        order += [("w_in_2", 0, KT, c) for c in (
            rq + r * P, rk + r * P, rv + 2 * r * P, rv + (2 * r + 1) * P,
            aq + 2 * r * P, aq + (2 * r + 1) * P, rg + 2 * r * P, rg + (2 * r + 1) * P)]
    for m in range(KT):
        order += [("w_in_2", 0, KT, ga + m * P), ("w_in_2", 0, KT, ga + D + m * P),
                  ("w_ret_out_2", 0, KT, m * P), ("w_attn_out_2", 0, KT, m * P)]
    order += [("w_out_2", 0, KT, m * P) for m in range(KT)]
    for part in range(3):
        n = min(8, FF2_TILES - 8 * part)
        for j in range(n):
            order += [("w_ffn_gate_2", 0, KT, (8 * part + j) * P), ("w_ffn_up_2", 0, KT, (8 * part + j) * P)]
        order += [("w_ffn_down_2", 8 * part, n, m * P) for m in range(KT)]
    return order




class Phase:

    def __init__(self, n, iters, before=None):
        self.n, self.iters = n, iters
        self.first = before.end if before else 0
        self.uses0 = before.uses_end if before else [0] * SLOTS
        self.last0 = before.last_end if before else [None] * SLOTS
        self.per = [len([j for j in range(n) if j % SLOTS == s]) for s in range(SLOTS)]
        self.end = self.first + n * iters
        self.uses_end = [u + p * iters for u, p in zip(self.uses0, self.per)]
        self.last_end = [self.first + n * (iters - 1) + max(j for j in range(n) if j % SLOTS == s)
                         if p else self.last0[s] for s, p in zip(range(SLOTS), self.per)]

    def slot(self, j):
        return (j % self.n) % SLOTS

    def index(self, i, j):
        return self.first + i * self.n + j

    def landed(self, i, j):
        wrap, j = divmod(j, self.n)
        s = j % SLOTS
        return ((i + wrap) * self.per[s] + (self.uses0[s] + j // SLOTS + 1)) * 16

    def back(self, j):
        wrap, j0 = divmod(j, self.n)
        s = j0 % SLOTS
        dist = []
        if j0 >= SLOTS:
            return SLOTS
        if self.iters > 1 or wrap:
            dist.append(self.n + j0 - max(x for x in range(self.n) if x % SLOTS == s))
        if not wrap and self.last0[s] is not None:
            dist.append(self.first + j0 - self.last0[s])
        return min(dist) if dist else None


def program(nc, dram, out):
    order = slab_order()
    ph_heads = Phase(7, HEADS)
    ph_gates = Phase(2 * AHEAD, 1, ph_heads)
    ph_merge0 = Phase(2 * AHEAD, 1, ph_gates)
    ph_merge1 = Phase(4, KT - AHEAD, ph_merge0)
    ph_out1 = Phase(8, 1, ph_merge1)
    ph_mlp = Phase(16, 4, ph_out1)
    ph_kv = Phase(10, 1, ph_mlp)
    ph_ret = Phase(8, RET_HEADS - 1, ph_kv)
    ph_merge2 = Phase(4, KT, ph_ret)
    ph_out2 = Phase(8, 1, ph_merge2)
    ph_ffn = Phase(24, 2, ph_out2)
    ph_ffn_end = Phase(20, 1, ph_ffn)
    phases = [ph_heads, ph_gates, ph_merge0, ph_merge1, ph_out1, ph_mlp, ph_kv, ph_ret, ph_merge2, ph_out2,
              ph_ffn, ph_ffn_end]
    assert ph_ffn_end.end == len(order)

    with ExitStack() as ctx:
        def at(name, shape, offset, dt=F32):
            n = 4
            for s in shape[1:]:
                n *= s
            assert offset + n <= LIMIT, name
            return nc.alloc_sbuf_tensor_at(name, shape, dt, offset=BASE + offset)

        BASE, LIMIT = 16 * KiB + 256, 207 * KiB
        ctx.enter_context(nc.sbuf_tensor("arena", [P, (128 + LIMIT) // 4], F32))

        class Bump:

            def __init__(self, start, end):
                self.at, self.end = start, end

            def __call__(self, name, shape, dt=F32):
                n = 4
                for s in shape[1:]:
                    n *= s
                t = at(name, shape, self.at, dt)
                self.at += (n + 31) // 32 * 32
                assert self.at <= self.end, (name, self.at, self.end)
                return t

        raw = [at(f"slab_raw{s}", [P, KT, P], s * 4 * KiB) for s in range(SLOTS)]
        w_hi = [at(f"slab_hi{s}", [P, KT, P], (16 + 4 * s) * KiB, F32R) for s in range(SLOTS)]
        w_lo = [at(f"slab_lo{s}", [P, KT, P], (32 + 4 * s) * KiB, F32R) for s in range(SLOTS)]
        u_hi = at("u_hi", [P, KT, T], 48 * KiB, F32R)
        u_lo = at("u_lo", [P, KT, T], 64 * KiB, F32R)
        br_a = at("branch_a", [P, KT, T], 80 * KiB)
        br_b = at("branch_b", [P, KT, T], 96 * KiB)
        m_hi = at("merged_hi", [P, KT, T], 80 * KiB, F32R)
        m_lo = at("merged_lo", [P, KT, T], 96 * KiB, F32R)
        a_hi = at("branch_a_hi", [P, KT, T], 112 * KiB, F32R)
        a_lo = at("branch_a_lo", [P, KT, T], 128 * KiB, F32R)
        b_hi = at("branch_b_hi", [P, KT, T], 144 * KiB, F32R)
        b_lo = at("branch_b_lo", [P, KT, T], 160 * KiB, F32R)
        y_hi = at("hidden_hi", [P, 8, T], 112 * KiB, F32R)
        y_lo = at("hidden_lo", [P, 8, T], 128 * KiB, F32R)
        tmp = [at(f"tmp{n}", [P, T], (144 + 2 * n) * KiB) for n in range(8)]
        mtmp = [at(f"mtmp{n}", [P, T], (192 + 2 * n) * KiB) for n in range(2)]
        h_res = at("residual", [P, KT, T], 176 * KiB)

        small = Bump(196 * KiB, LIMIT)
        ident = small("ident", [P, P])
        ones = small("ones", [P, P])
        mhalf = small("minus_half", [P, 16])
        gains = small("gains", [P, 5, KT])
        sq_sum = small("sq_sum", [P, T])
        r_row = small("r_row", [P, T])
        r_diag = small("r_diag", [P, NT, P])
        ms_col = small("ms_col", [P, NT])
        r_col = small("r_col", [P, NT])
        head_gain = small("head_gain", [P, 3])

        ps = [ctx.enter_context(nc.psum_tensor(f"bank{n}", [P, T], F32)) for n in range(8)]
        bank_slab = ps[0:2]
        bA, bB, bC, bD, bE, bF = ps[2:8]

        sems = {}

        def sem(name):
            if name not in sems:
                sems[name] = ctx.enter_context(nc.semaphore(name))
            return sems[name]

        s_raw = [sem(f"slab_landed{s}") for s in range(SLOTS)]
        s_hi, s_lo, s_used = sem("slab_hi"), sem("slab_lo"), sem("slab_used")
        s_taken = sem("slab_taken")

        def c4(ap):
            return ap.rearrange("p (n c) -> p n c", n=NT)

        def over_cols(ap):
            return ap.unsqueeze(2).to_broadcast([P, NT, P])

        def over_tiles(ap):
            return ap.unsqueeze(1).to_broadcast([P, NT, P])

        def wait_slab(eng, s, ph, i, j):
            back = ph.back(j)
            value = None if back is None else ph.index(i, j) - back + 1
            if value is not None and not (isinstance(value, int) and value <= 0):
                eng.wait_ge(s, value)

        def load_slab(sp, ph, i, j):
            wait_slab(sp, s_lo, ph, i, j)
            s = ph.slot(j)
            src = dram["slabs"][bass.ds(ph.index(i, j), 1), :, :].rearrange("a p n -> (a p) n")
            sp.dma_start(raw[s][:].rearrange("p k c -> p (k c)"), src).then_inc(s_raw[s], 16)

        def split_hi(act, ph, i, j):
            s = ph.slot(j)
            wait_slab(act, s_used, ph, i, j)
            act.wait_ge(s_raw[s], ph.landed(i, j))
            act.copy(w_hi[s][:], raw[s][:]).then_inc(s_hi, 1)

        def split_lo(pool, ph, i, j):
            s = ph.slot(j)
            pool.wait_ge(s_hi, ph.index(i, j) + 1)
            pool.tensor_tensor(w_lo[s][:], raw[s][:], w_hi[s][:].bitcast(F32),
                               ALU.subtract).then_inc(s_lo, 1)

        def slab_products(pe, ph, i, j, bank, x_hi, x_lo, ks=range(KT), n_k=KT):
            s = ph.slot(j)
            if ks[0] == 0:
                pe.wait_ge(s_lo, ph.index(i, j) + 1)
            for k in ks:
                first, last = k == 0, k == n_k - 1
                pe.matmul(bank, w_hi[s][:, k, :], x_hi[:, k, :], start=first, stop=False)
                pe.matmul(bank, w_hi[s][:, k, :], x_lo[:, k, :], start=False, stop=False)
                mm = pe.matmul(bank, w_lo[s][:, k, :], x_hi[:, k, :], start=False, stop=last)
            if ks[-1] == n_k - 1:
                mm.then_inc(s_used, 1)

        Q_G, Q_LF, Q_LFPREV, Q_GCUM, Q_BETA, Q_BEG, Q_EGL = range(7)
        NQ = 7
        head = Bump(112 * KiB, 196 * KiB)
        table = head("table", [P, HEADS, NQ, NT])
        conv_w = head("conv_w", [P, HEADS, 12])
        upper = head("upper", [P, P])
        level_mask = head("level_mask", [P, LEVELS, P])
        neg_mask = head("neg_mask", [P, P])
        h_small = head("h_small", [P, NQ, NT])
        h_conv = head("h_conv", [P, 12])
        raw_z = head("raw_z", [P, T])
        cq, ck, cv, sz = [head(n, [P, T]) for n in ("cq", "ck", "cv", "silu_z")]
        ssc, rsc = head("ssc", [P, 16]), head("rsc", [P, 16])
        cols = head("cols", [P, 6, NT])
        C_BK, C_KB, C_KD, C_RQ, C_RFQ, C_VB = range(6)
        dec = head("chunk_decay", [P, NT])
        d_g = head("diag_g", [P, T])
        d_b, d_q, d_rk, d_cum = [head(f"diag_{n}", [P, T]) for n in ("b", "q", "rk", "cum")]
        e_g, qdec = head("exp_g", [P, T]), head("q_dec", [P, T])
        dt_, bdt, adt = head("decay", [P, T]), head("decay_b", [P, T]), head("decay_q", [P, T])
        a_t, att = d_g, head("attn_t", [P, T])
        kp, kd, vp = head("k_rhs", [P, T]), head("k_dec", [P, T]), head("v_rhs", [P, T])
        atm = [head(f"a_level{n}", [P, T]) for n in range(2)]
        xi, zi, yi = head("inv", [P, T]), head("inv_t", [P, T]), head("level_prod", [P, T])
        th = [bdt, adt, bdt, yi]
        sq = [e_g, d_q, d_rk, d_cum]
        osq_ = atm[1]
        st, vn = head("state", [P, P]), head("v_new", [P, P])
        on = dt_
        fqt, fkt, fvt = [head(f"fox_{n}", [P, T]) for n in ("q", "k", "v")]
        cumr = head("cum_row", [P, T])
        sb_, pr, pt = head("logits", [P, T]), head("probs", [P, T]), head("probs_t", [P, T])
        nmax, lsum, rsum = [head(n, [P, NT]) for n in ("neg_max", "row_sum", "inv_sum")]
        osc, ors = head("osc", [P, NT]), head("ors", [P, NT])
        assert head.at <= 183 * KiB
        head.at = 183 * KiB
        rawq = [head(f"raw_qkv{n}", [P, 3 + T]) for n in range(3)]
        raw_fq, raw_fk, raw_fv = [head(f"raw_{n}", [P, T]) for n in ("fq", "fk", "fv")]
        gates_ahead = [rawq[0][:, 3:3 + T], rawq[1][:, 3:3 + T], rawq[2][:, 3:3 + T], raw_fq[:], raw_fk[:], raw_fv[:]]
        pre = Bump(80 * KiB, 112 * KiB)
        x_sq = [pre(f"x_squares{k}", [P, T]) for k in range(KT)]
        w_gates = pre("w_gates", [P, KT, 24])
        wg_hi, wg_lo = [pre(f"w_gates_{n}", [P, KT, 24], F32R) for n in ("hi", "lo")]
        g_row = pre("gates_row", [P, T])
        gate_rows = pre("gate_rows", [P, 3, HEADS])
        gt = pre("gates_tok", [P, NT, 24])
        y2, sp2, e2 = [pre(f"tok_{n}", [P, 2 * HEADS, NT]) for n in ("y", "softplus", "e")]
        t8, gtot = [pre(f"tok_{n}", [P, HEADS, NT]) for n in ("tanh", "gtot")]

        ORDER = """th3 fq diag s0.0 s0.1 s0.2 sl3 s0.3 fvt s0.4 rows dif s0.5 frows s0.6 s0.7 s1.0 e0 dt s1.1 s1.2
                   s1.3 tkv S0 s1.4 kk s1.5 s1.6 E0 qk z0 s1.7 P0 s2.0 s2.1 s2.2 xt T0 e1 S1 s2.3 Y1 E1 s2.4 O0 X1
                   P1 cv0.0 s2.5 Y2 T1 s2.6 s2.7 cv0.1 X2 S2 s3.0 e2 Y3 E2 cv0.2 s3.1 s3.2 O1 X3 P2 cv0.3 s3.3 Y4
                   s3.4 T2 th0 cv1.0 s3.5 X4 S3 cv1.1 s3.6 Y5 E3 cv1.2 s3.7 O2 X5 P3 s4.0 e3 cv1.3 s4.1 Y6 sl0 th1
                   s4.2 T3 X6 cv2.0 s4.3 s4.4 vk cv2.1 s4.5 O3 sl1 s4.6 r0 s4.7 s5.0 e4 sq0 cv2.2 r1 cv2.3 s5.1 v1
                   s5.2 s5.3 r2 th2 s5.4 v2 s5.5 s5.6 r3 s5.7 v3 sl2 sq1 s6.0 e5 s6.1 s6.2 osq s6.3 s6.4 s6.5 ssq cola
                   s6.6 s6.7 e6 orow colb""".split()
        LATE = {"cv0.0", "cv0.1", "cv0.2", "cv0.3", "cv1.0", "cv1.1", "cv1.2", "cv1.3", "cv2.0", "cv2.1", "cv2.2",
                "cv2.3", "th0", "th1", "th2", "sl0", "sl1", "sl2", "sq0", "sq1", "ssq", "cola", "colb"}

        def is_slab(tok):
            return tok[0] == "s" and tok[1].isdigit()

        def is_evac(tok):
            return tok[0] == "e" and tok[1].isdigit()

        LAST, places, part = [], [n for n, t in enumerate(ORDER) if is_slab(t)], 0
        for n, t in enumerate(ORDER):
            if n in places:
                if (places.index(n) + 1) * 2 * AHEAD * KT // len(places) > part:
                    LAST.append(f"s{part // KT}.{part % KT}")
                    if part % KT == 0 and part:
                        LAST.append(f"e{part // KT - 1}")
                    part += 1
            elif t not in LATE and not is_evac(t):
                LAST.append(t)
        LAST.append(f"e{2 * AHEAD - 1}")
        FIRST = [t for t in ORDER if is_slab(t) or is_evac(t) or t in LATE]
        FIRST.insert(FIRST.index("s1.2"), "gates0")
        FIRST.insert(FIRST.index("s1.7"), "gates0t")
        FIRST.insert(FIRST.index("e1") + 1, "gates1")
        FIRST.insert(FIRST.index("e3") + 1, "gates2")

        def slab_part(tok):
            j, t = tok[1:].split(".")
            return int(j), int(t)

        def run(tokens, stages, slab, evac):
            for tok in tokens:
                if is_slab(tok):
                    if slab:
                        slab(*slab_part(tok))
                elif is_evac(tok):
                    if evac:
                        evac(int(tok[1:]))
                elif tok in stages:
                    stages[tok]()

        HEAD_BANK = [0, 1, 0, 1, 0, 1, 0]

        def head_rounds(eng, per_round):
            per_round(FIRST, 0, None)
            with eng.Fori(1, HEADS) as i:
                per_round(ORDER, i, i - 1)
            per_round(LAST, HEADS, HEADS - 1)

        class Steps:

            def __init__(self, eng, s):
                self.eng, self.sem, self.n, self.base = eng, s, 0, None

            def value(self):
                return self.n if self.base is None else self.base + self.n

            def __call__(self, ins):
                self.n += 1
                ins.then_inc(self.sem, 1)
                self.eng.wait_ge(self.sem, self.value())

            def rounds(self, start, per, c):
                self.base, self.n = start + c * per, 0

            def straight(self, value):
                self.base, self.n = None, value

        def norm_act_square(act, n, m):
            if m >= 3:
                act.wait_ge(sem("norm_sum"), (n - 1) * (KT - 1) + m - 2)
            dst = mtmp[m % 2] if m else sq_sum
            act.activation(dst[:], h_res[:, m, :], ACT.Square).then_inc(sem("norm_sq"), 1)

        def norm_pool_add(pool, n, m):
            if m == 0:
                return
            pool.wait_ge(sem("norm_sq"), (n - 1) * KT + m + 1)
            if m > 1:
                pool.wait_ge(sem("norm_sum"), (n - 1) * (KT - 1) + m - 1)
            pool.tensor_tensor(sq_sum[:], sq_sum[:], mtmp[m % 2][:], ALU.add).then_inc(sem("norm_sum"), 1)

        def part_hi(act, n, m):
            if n > 0:
                act.wait_ge(sem("h_new"), (n - 1) * KT + m + 1)
            act.activation(u_hi[:, m, :], h_res[:, m, :], ACT.Copy, scale=gains[:, n, m:m + 1])\
                .then_inc(sem("u_hi"), 1)

        def part_lo(dve, n, m):
            dve.wait_ge(sem("u_hi"), n * KT + m + 1)
            dve.scalar_tensor_tensor(out=u_lo[:, m, :], in0=h_res[:, m, :], scalar=gains[:, n, m:m + 1],
                                     in1=u_hi[:, m, :].bitcast(F32), op0=ALU.mult, op1=ALU.subtract)\
                .then_inc(sem("u_lo"), 1)

        def residual_add(dve, bank, m, count=True):
            ins = dve.tensor_tensor(h_res[:, m, :], h_res[:, m, :], bank[:], ALU.add)
            ins.then_inc(sem("h_new") if count else sem("h_part"), 1)

        def norm_pool_scale(pool, n):
            pool.wait_ge(sem("norm_ms"), n + 1)
            pool.tensor_tensor(r_col[:], ms_col[:], mhalf[:, 0:NT], ALU.pow).then_inc(sem("norm_pool"), 1)
            pool.wait_ge(sem("norm_pool"), 2 * n + 1)
            pool.tensor_tensor(r_diag[:], over_tiles(ident[:]), over_cols(r_col[:]), ALU.mult)\
                .then_inc(sem("norm_pool"), 1)

        def norm_pe(pe, n):
            if n > 0:
                pe.wait_ge(sem("norm_sum"), n * (KT - 1))
            for t in range(NT):
                mm = pe.matmul(bF[:, t:t + 1], sq_sum[:, t * P:(t + 1) * P], ones[:, 0:1], start=True, stop=True)
            mm.then_inc(sem("norm_ps"), 1)

        def norm_pe_row(pe, n):
            pe.wait_ge(sem("norm_pool"), 2 * n + 2)
            pe.matmul(bF[:], ones[:], r_diag[:].rearrange("p n c -> p (n c)"), start=True, stop=True)\
                .then_inc(sem("norm_ps"), 1)

        def norm_dve(dve, n):
            dve.wait_ge(sem("norm_ps"), 2 * n + 1)
            dve.tensor_scalar(ms_col[:], bF[:, 0:NT], 1.0 / D, EPS, ALU.mult, ALU.add).then_inc(sem("norm_ms"), 1)

        def norm_dve_row(dve, n):
            dve.wait_ge(sem("norm_ps"), 2 * n + 2)
            dve.tensor_copy(r_row[:], bF[:]).then_inc(sem("norm_row"), 1)
            dve.wait_ge(sem("norm_row"), n + 1)

        def products_and_norm(pe, ph, i, j, k, bank, n):
            first = n is not None and isinstance(i, int) and i == 0
            if first and j == 0:
                pe.wait_ge(sem("u_lo"), n * KT + k + 1)
            slab_products(pe, ph, i, j, bank, u_hi, u_lo, ks=(k,))
            if first and (j, k) == (0, KT - 1):
                norm_pe(pe, n)
            if first and (j, k) == (1, KT - 3):
                norm_pe_row(pe, n)

        merge_g = mtmp

        def branches_hi(act, rnd):
            act.wait_ge(sem("branches_done"), rnd + 1)
            for k in range(KT):
                for hi, br in ((a_hi, br_a), (b_hi, br_b)):
                    act.copy(hi[:, k, :], br[:, k, :]).then_inc(sem("br_hi"), 1)

        def branches_lo(dve, rnd):
            for k in range(KT):
                for n, (hi, lo, br) in enumerate(((a_hi, a_lo, br_a), (b_hi, b_lo, br_b))):
                    dve.wait_ge(sem("br_hi"), (rnd * KT + k) * 2 + n + 1)
                    dve.tensor_tensor(lo[:, k, :], br[:, k, :], hi[:, k, :].bitcast(F32), ALU.subtract)\
                        .then_inc(sem("br_lo"), 1)

        def gates_before(rnd, m):
            return 1 + (2 * (m - AHEAD) if rnd == 0 else 2 * (KT - AHEAD + m))

        def merge_tiles(eng, phs, rnd, tile):
            if rnd == 0:
                for m in range(AHEAD):
                    tile(phs[0], 0, (None, None, 2 * m, 2 * m + 1), m, True)
                with eng.Fori(0, KT - AHEAD) as i:
                    tile(phs[1], i, range(4), i + AHEAD, False)
            else:
                with eng.Fori(0, KT) as i:
                    tile(phs[0], i, range(4), i, False)

        def merge_pe(pe, phs, rnd):
            def tile(ph, i, slabs, m, ahead):
                q = rnd * KT + m
                for j in (2, 3) if ahead else range(4):
                    if j < 2:
                        pe.wait_ge(sem("gate_taken"), gates_before(rnd, m))
                        slab_products(pe, ph, i, slabs[j], bank_slab[j][:], u_hi, u_lo)
                        continue
                    first = rnd == 0 and ahead and m == 0
                    if j == 2 and not first:
                        pe.wait_ge(sem("br_lo"), 2 * KT * (rnd + 1))
                    pe.wait_ge(sem("branch_taken"), 2 * q + 1)
                    for k in range(KT):
                        if first:
                            pe.wait_ge(sem("br_lo"), 2 * k + j - 1)
                        slab_products(pe, ph, i, slabs[j], (bA, bB)[j - 2][:], (a_hi, b_hi)[j - 2],
                                      (a_lo, b_lo)[j - 2], ks=(k,))
            merge_tiles(pe, phs, rnd, tile)

        def merge_act(act, phs, rnd):
            branches_hi(act, rnd)

            def tile(ph, i, slabs, m, ahead):
                q = rnd * KT + m
                if ahead:
                    act.wait_ge(s_taken, 7 * HEADS + 2 * m + 2)
                    act.wait_ge(sem("merged"), 3 * q + 1)
                    for j in range(2):
                        act.activation(merge_g[j][:], gates_ahead[2 * m + j], ACT.Tanh, scale=0.5)\
                            .then_inc(sem("gate_tanh"), 1)
                        split_hi(act, ph, i, slabs[2 + j] + LEAD)
                    return
                for j in range(4):
                    split_hi(act, ph, i, slabs[j] + LEAD)
                    if j < 2:
                        act.wait_ge(sem("gate_taken"), gates_before(rnd, m) + j + 1)
                        act.activation(merge_g[j][:], merge_g[j][:], ACT.Tanh, scale=0.5).then_inc(sem("gate_tanh"), 1)
            merge_tiles(act, phs, rnd, tile)

        def merge_pool(pool, phs, rnd):
            def tile(ph, i, slabs, m, ahead):
                for j in slabs:
                    if j is not None:
                        split_lo(pool, ph, i, j + LEAD)
            merge_tiles(pool, phs, rnd, tile)

        def merge_dve(dve, phs, rnd, bias=None):
            def tile(ph, i, slabs, m, ahead):
                q = rnd * KT + m
                if not ahead:
                    dve.wait_ge(sem("merged"), 3 * q + 1)
                for j in range(0 if ahead else 2):
                    dve.wait_ge(s_used, ph.index(i, slabs[j]) + 1)
                    if bias is None:
                        dve.tensor_tensor(merge_g[j][:], bank_slab[j][:], r_row[:], ALU.mult)\
                            .then_inc(sem("gate_taken"), 1)
                    else:
                        dve.tensor_tensor(merge_g[j][:], bank_slab[j][:], r_row[:], ALU.mult)\
                            .then_inc(sem("gate_scaled"), 1)
                        dve.wait_ge(sem("gate_scaled"), 2 * m + j + 1)
                        dve.tensor_scalar(merge_g[j][:], merge_g[j][:], bias[:, bass.ds(m + KT * j, 1)], None, ALU.add)\
                            .then_inc(sem("gate_taken"), 1)
                for j in range(2):
                    dve.wait_ge(s_used, ph.index(i, slabs[2 + j]) + 1)
                    dve.wait_ge(sem("gate_tanh"), 2 * q + j + 1)
                    dve.scalar_tensor_tensor(out=merge_g[j][:], in0=merge_g[j][:], scalar=1.0, in1=(bA, bB)[j][:],
                                             op0=ALU.add, op1=ALU.mult).then_inc(sem("branch_taken"), 1)
                dve.wait_ge(sem("branch_taken"), 2 * q + 3)
                dve.tensor_tensor(merge_g[0][:], merge_g[0][:], merge_g[1][:], ALU.add).then_inc(sem("merged"), 1)
                dve.wait_ge(sem("merged"), 3 * q + 2)
                dst_hi = m_hi[:, bass.ds(m, 1), :].rearrange("p a t -> p (a t)")
                dst_lo = m_lo[:, bass.ds(m, 1), :].rearrange("p a t -> p (a t)")
                dve.tensor_scalar(dst_hi, merge_g[0][:], 0.5, None, ALU.mult).then_inc(sem("merged"), 1)
                dve.wait_ge(sem("merged"), 3 * q + 3)
                dve.scalar_tensor_tensor(out=dst_lo, in0=merge_g[0][:], scalar=0.5, in1=dst_hi.bitcast(F32),
                                         op0=ALU.mult, op1=ALU.subtract).then_inc(sem("merged"), 1)
            merge_tiles(dve, phs, rnd, tile)

        def out_pe(pe, ph, rnd, n):
            for m in range(KT):
                if m == 0:
                    pe.wait_ge(sem("gate_taken"), gates_before(rnd, KT))
                if m >= 2:
                    pe.wait_ge(sem("h_new"), (n - 1) * KT + m - 1)
                for k in range(KT):
                    if m == 0:
                        pe.wait_ge(sem("merged"), 3 * (rnd * KT + k + 1) + 1)
                    slab_products(pe, ph, 0, m, bank_slab[m % 2][:], m_hi, m_lo, ks=(k,))

        def out_act(act, ph, n):
            for m in range(KT):
                split_hi(act, ph, 0, m + LEAD)
                if m >= 1:
                    part_hi(act, n, m - 1)
                    norm_act_square(act, n, m - 1)
            part_hi(act, n, KT - 1)
            norm_act_square(act, n, KT - 1)

        def out_pool(pool, ph, n):
            for m in range(KT):
                split_lo(pool, ph, 0, m + LEAD)
                if m >= 1:
                    norm_pool_add(pool, n, m - 1)
            norm_pool_add(pool, n, KT - 1)
            norm_pool_scale(pool, n)

        def out_dve(dve, ph, n):
            for m in range(KT):
                dve.wait_ge(s_used, ph.index(0, m) + 1)
                if m == 0:
                    dve.wait_ge(sem("ld_x"), 32)
                residual_add(dve, bank_slab[m % 2], m)
                if m >= 1:
                    part_lo(dve, n, m - 1)
            part_lo(dve, n, KT - 1)
            norm_dve(dve, n)
            norm_dve_row(dve, n)

        MLP_PARTS = 4

        def mlp_parts(eng, part):
            part(0)
            with eng.Fori(1, MLP_PARTS - 1) as i:
                part(i)
            part(MLP_PARTS - 1)

        def is_last(i):
            return isinstance(i, int) and i == MLP_PARTS - 1

        def mlp_pe(pe):
            def part(i):
                first = isinstance(i, int) and i == 0
                for j in range(16):
                    if j < 2 and not first:
                        pe.wait_ge(sem("h_part"), 8 * i + j - 1)
                    elif 2 <= j < 10:
                        pe.wait_ge(sem("relu"), 8 * i + j - 1)
                    elif j >= 10:
                        pe.wait_ge(sem("h_new"), KT + j - 9) if is_last(i) else \
                            pe.wait_ge(sem("h_part"), 8 * i + j - 9)
                    if j < 8:
                        if first and j == 0:
                            pe.wait_ge(sem("h_new"), KT)
                        for k in range(KT):
                            products_and_norm(pe, ph_mlp, i, j, k, bank_slab[j % 2][:], 1)
                        continue
                    for k in range(KT):
                        if j == 8:
                            pe.wait_ge(sem("hid_lo"), 8 * i + k + 1)
                        slab_products(pe, ph_mlp, i, j, bank_slab[j % 2][:], y_hi, y_lo, ks=(k,))
            mlp_parts(pe, part)

        def mlp_act(act):
            def part(i):
                for j in range(16):
                    split_hi(act, ph_mlp, i, j + LEAD)
                    if 1 <= j <= 8:
                        hidden(i, j - 1)
                    if isinstance(i, int) and i == MLP_PARTS - 1 and j >= 9:
                        part_hi(act, 2, j - 9)
                        norm_act_square(act, 2, j - 9)

            def hidden(i, t):
                act.wait_ge(sem("relu"), 8 * i + t + 1)
                act.activation(tmp[2 + t % 2][:], tmp[t % 2][:], ACT.Square).then_inc(sem("hid_sq"), 1)
                act.wait_ge(sem("hid_sq"), 8 * i + t + 1)
                act.copy(y_hi[:, t, :], tmp[2 + t % 2][:]).then_inc(sem("hid_hi"), 1)
            mlp_parts(act, part)
            part_hi(act, 2, KT - 1)
            norm_act_square(act, 2, KT - 1)

        def mlp_pool(pool):
            def part(i):
                for j in range(16):
                    split_lo(pool, ph_mlp, i, j + LEAD)
                    if is_last(i) and j >= 9:
                        norm_pool_add(pool, 2, j - 9)
            mlp_parts(pool, part)
            norm_pool_add(pool, 2, KT - 1)
            norm_pool_scale(pool, 2)

        def mlp_dve(dve):
            def part(i):
                for j in range(16):
                    if 1 <= j <= 8:
                        t = j - 1
                        dve.wait_ge(sem("hid_hi"), 8 * i + t + 1)
                        dve.tensor_tensor(y_lo[:, t, :], tmp[2 + t % 2][:], y_hi[:, t, :].bitcast(F32), ALU.subtract)\
                            .then_inc(sem("hid_lo"), 1)
                    dve.wait_ge(s_used, ph_mlp.index(i, j) + 1)
                    if j < 8:
                        if j >= 2:
                            dve.wait_ge(sem("hid_sq"), 8 * i + j - 1)
                        dve.scalar_tensor_tensor(out=tmp[j % 2][:], in0=bank_slab[j % 2][:], scalar=0.0, in1=r_row[:],
                                                 op0=ALU.max, op1=ALU.mult).then_inc(sem("relu"), 1)
                    else:
                        residual_add(dve, bank_slab[j % 2], j - 8, count=is_last(i))
                    if is_last(i) and j >= 9:
                        part_lo(dve, 2, j - 9)
            mlp_parts(dve, part)
            part_lo(dve, 2, KT - 1)
            norm_dve(dve, 2)
            norm_dve_row(dve, 2)

        tab = Bump(152 * KiB, 168 * KiB)
        cos_r, sin_r, cos_a, sin_a = [tab(n, [P, T]) for n in ("cos_ret", "sin_ret", "cos_att", "sin_att")]
        swap_r, swap_a, dup0, dup1 = [tab(n, [P, P]) for n in ("swap_ret", "swap_att", "dup_kv0", "dup_kv1")]
        decay_t = tab("ret_decay_t", [P, RET_HEADS, P])
        q_decay = tab("ret_q_decay", [P, RET_HEADS, P])
        band = tab("band_mask", [P, 2, P])
        small2 = Bump(small.at, LIMIT)
        k_decay = small2("ret_k_decay", [P, RET_HEADS, 2])
        bias_cols = small2("bias_cols", [P, 2 + 8 * RET_HEADS])
        bias_gate = small2("bias_gate", [P, 2 * KT])
        ret_gain = small2("ret_gain", [P, RET_HEADS, 2])
        sink_cols = small2("sink_cols", [P, RET_HEADS, 4])
        hb = small2("round_bias", [P, 8])
        hg, hd, hs = [small2(n, [P, w]) for n, w in (("round_gain", 2), ("round_decay", 2), ("round_sinks", 4))]
        gsc, grs = small2("gn_ms", [P, NT]), small2("gn_rs", [P, NT])
        nm2, ls2, es2, rd2 = [small2(n, [P, NT]) for n in ("att_neg_max", "att_sum", "att_sink", "att_inv")]
        TAB2 = [("cos_r", cos_r), ("sin_r", sin_r), ("cos_a", cos_a), ("sin_a", sin_a), ("swap_r", swap_r),
                ("swap_a", swap_a), ("dup0", dup0), ("dup1", dup1), ("decay_t", decay_t), ("q_decay", q_decay),
                ("band", band), ("k_decay", k_decay), ("bias_cols", bias_cols), ("bias_gate", bias_gate),
                ("ret_gain", ret_gain), ("sink_cols", sink_cols)]
        N_TAB2 = len(TAB2)
        w2 = Bump(112 * KiB, 152 * KiB)
        r_q, r_k = w2("ret_q_raw", [P, T]), w2("ret_k_raw", [P, T])
        r_v = [w2(f"ret_v_raw{n}", [P, T]) for n in range(2)]
        r_g = [w2(f"ret_g_raw{n}", [P, T]) for n in range(2)]
        a_q = [w2(f"att_q_raw{n}", [P, T]) for n in range(2)]
        q_r, k_r = w2("ret_q", [P, T]), w2("ret_k", [P, T])
        kdec2, v_tok = w2("ret_k_dec", [P, T]), w2("ret_v_tok", [P, NT, 2 * P])
        sc_t, q_dec2 = w2("ret_scores_t", [P, T]), w2("ret_q_dec", [P, T])
        y2_at = w2.at
        y_r = [w2(f"ret_y{n}", [P, T]) for n in range(2)]
        k_cur = w2("att_k", [P, T])
        lg = w2("att_logits", [P, NT, 2 * P])
        x2 = Bump(168 * KiB, 176 * KiB)
        v_cur = x2("att_v", [P, NT, 64])
        st2 = [x2(f"ret_state{n}", [P, 2 * P]) for n in range(3)]
        pr2 = [x2("att_probs0", [P, NT, 2 * P]), at("att_probs1", [P, NT, 2 * P], y2_at)]
        kv_dup = at("att_kv_dup", [P, 2, T], 192 * KiB)
        av_tok = small2("att_v_tok", [P, NT, P])
        aq_r, pt2 = [q_r, k_r], v_tok
        gn_sq = [kdec2, q_dec2]
        gn_th = [sc_t[:], pt2[:, 0:2, :].rearrange("p n c -> p (n c)")]

        R_DEST = [r_q, r_k, r_v[0], r_v[1], a_q[0], a_q[1], r_g[0], r_g[1]]
        ORDER2 = """rb s0.0 sw kcur s0.1 s0.2 s0.3 tv rot s0.4 s0.5 s0.6 s0.7 tk sc s1.0 e0 qd s1.1 s1.2 sp0 s1.3 sp1
                    s1.4 sp2 s1.5 s1.6 s1.7 ro s2.0 e1 sa s2.1 y2 s2.2 s2.3 rm rota s2.4 s2.5 yc s2.6 s2.7 s3.0 e2
                    s3.1 L0 s3.2 s3.3 rs s3.4 E0 s3.5 s3.6 s3.7 M0 s4.0 rr e3 yo L1 s4.1 s4.2 T0 E1 s4.3 s4.4 O0 M1
                    s4.5 s4.6 L2 s4.7 s5.0 e4 s5.1 T1 E2 s5.2 s5.3 O1 ev0 M2 s5.4 s5.5 L3 s5.6 s5.7 s6.0 e5 T2 E3
                    s6.1 s6.2 O2 M3 s6.3 s6.4 s6.5 s6.6 s6.7 T3 s7.0 e6 s7.1 s7.2 O3 s7.3 ev1 s7.4 s7.5 s7.6 s7.7
                    e7""".split()
        FINE2 = [t for t in ORDER2 if not is_slab(t) and not is_evac(t)]
        FIRST2 = []
        for j in range(ph_kv.n):
            FIRST2 += [f"s{j}.0"] + ([f"e{j - 1}"] if j else []) + [f"s{j}.{t}" for t in range(1, KT)]
        FIRST2.insert(FIRST2.index("s2.4"), "kva")
        FIRST2.insert(FIRST2.index("s3.6"), "kvb")
        FIRST2.append(f"e{ph_kv.n - 1}")

        def ret_rounds(eng, per_round):
            per_round(FIRST2, ph_kv, 0, None)
            with eng.Fori(0, RET_HEADS - 1) as i:
                per_round(ORDER2, ph_ret, i, i)
            per_round(FINE2, None, None, RET_HEADS - 1)

        L_BANKS = [(bC, bD), (bE, bF), (bE, bF), (bC, bD)]
        O_BANK = [bC, bC, bE, bE]

        def ret_pe(pe, tiles, transposes):
            def per_round(tokens, ph, i, c):
                def slab(j, t):
                    if t == 0:
                        q = ph.index(i, j) - ph_kv.first
                        if not (isinstance(q, int) and q < 2):
                            pe.wait_ge(sem("taken2"), q - 1)
                        else:
                            pe.wait_ge(sem("h_new"), 2 * KT)
                    products_and_norm(pe, ph, i, j, t, bank_slab[j % 2][:], 2 if ph is ph_kv else None)

                def kva():
                    pe.wait_ge(sem("taken2"), 2)
                    pe.wait_ge(sem("ld_tab2"), 16 * N_TAB2)
                    pe.matmul(bA[:], swap_a[:], q_r[:], start=True, stop=True).then_inc(sem("kv_ps"), 1)
                    transposes(bD, k_r).then_inc(sem("kv_ps"), 1)

                def kvb():
                    pe.wait_ge(sem("kv_rot"), 1)
                    pe.matmul(bB[:], dup0[:], sc_t[:], start=True, stop=True)
                    pe.matmul(bC[:], dup1[:], sc_t[:], start=True, stop=True).then_inc(sem("kv_ps"), 1)

                def sw():
                    pe.wait_ge(sem("taken2"), 8 * c + 10)
                    pe.matmul(bA[:], swap_r[:], r_q[:], start=True, stop=True).then_inc(sem("sw_ps"), 1)
                    pe.matmul(bB[:], swap_r[:], r_k[:], start=True, stop=True).then_inc(sem("sw_ps"), 1)

                def tv():
                    transposes(bC, r_v[0]).then_inc(sem("tv2_ps"), 1)
                    transposes(bD, r_v[1]).then_inc(sem("tv2_ps"), 1)

                def tk():
                    pe.wait_ge(sem("rot"), 2 * c + 2)
                    transposes(bA, k_r).then_inc(sem("tk2_ps"), 1)

                def sc():
                    tiles(bB, k_r, q_r).then_inc(sem("sc_ps"), 1)

                def sp(n):
                    if n == 0:
                        pe.wait_ge(sem("kdec2"), c + 1)
                        pe.wait_ge(sem("v_tok"), 2 * c + 2)
                    if n == 2:
                        pe.wait_ge(sem("state2"), 3 * c + 1)
                    pe.matmul((bE, bF, bE)[n][:, 0:2 * P], kdec2[:, n * P:(n + 1) * P], v_tok[:, n, :],
                              start=True, stop=True).then_inc(sem("sp_ps"), 1)

                def ro():
                    pe.wait_ge(sem("sc_t"), c + 1)
                    pe.wait_ge(sem("q_dec2"), c + 1)
                    pe.wait_ge(sem("state2"), 3 * c + 3)
                    for e, bank in enumerate((bC, bD)):
                        cols = slice(e * P, (e + 1) * P)
                        for n in range(NT):
                            q = slice(n * P, (n + 1) * P)
                            mm = pe.matmul(bank[:, q], v_tok[:, n, cols], sc_t[:, q], start=True, stop=n == 0)
                            if n > 0:
                                mm = pe.matmul(bank[:, q], st2[n - 1][:, cols], q_dec2[:, q], start=False, stop=True)
                        mm.then_inc(sem("ro_ps"), 1)

                def rm():
                    pe.wait_ge(sem("ret_y"), 2 * c + 2)
                    pe.matmul(bA[:], ones[:], y_r[0][:], start=True, stop=False)
                    pe.matmul(bA[:], ones[:], y_r[1][:], start=False, stop=True).then_inc(sem("gn_ps"), 1)

                def rs():
                    pe.wait_ge(sem("gn_sq"), 2 * c + 2)
                    for n in range(NT):
                        q = slice(n * P, (n + 1) * P)
                        pe.matmul(bB[:, n:n + 1], gn_sq[0][:, q], ones[:, 0:1], start=True, stop=False)
                        mm = pe.matmul(bB[:, n:n + 1], gn_sq[1][:, q], ones[:, 0:1], start=False, stop=True)
                    mm.then_inc(sem("gn_ps"), 1)

                def rr():
                    pe.wait_ge(sem("gn_scale"), 2 * c + 2)
                    pe.matmul(bA[:], ones[:], r_diag[:].rearrange("p n c -> p (n c)"), start=True, stop=True)\
                        .then_inc(sem("gn_ps"), 1)

                def sa():
                    pe.matmul(bE[:], swap_a[:], a_q[0][:], start=True, stop=True).then_inc(sem("sa_ps"), 1)
                    pe.matmul(bF[:], swap_a[:], a_q[1][:], start=True, stop=True).then_inc(sem("sa_ps"), 1)

                def logits(u):
                    half = slice(64 * (u % 2), 64 * (u % 2) + 64)
                    if u == 0:
                        pe.wait_ge(sem("kv_cur"), c + 1)
                        pe.wait_ge(sem("rot_a"), 2 * c + 1)
                        pe.wait_ge(sem("ret_y"), 2 * c + 2)
                    if u == 1:
                        pe.wait_ge(sem("rot_a"), 2 * c + 2)
                    if u == 2:
                        pe.wait_ge(sem("lg"), 4 * c + 2)
                    if u == 3:
                        pe.wait_ge(sem("att_out"), 2 * c + 1)
                    for b in range(NT):
                        bank, at_ = L_BANKS[u][b // 2], 2 * P * (b % 2)
                        k0 = max(b - 1, 0) * P
                        mm = pe.matmul(bank[:, at_ + (P if b == 0 else 0):at_ + 2 * P],
                                       aq_r[u // 2][half, b * P:(b + 1) * P], k_cur[half, k0:(b + 1) * P],
                                       start=True, stop=True)
                    mm.then_inc(sem("lg_ps"), 1)

                def probs_t(u):
                    pe.wait_ge(sem("probs2"), 4 * c + u + 1)
                    if u == 0:
                        pe.wait_ge(sem("ret_out"), 2 * c + 2)
                    else:
                        pe.wait_ge(sem("pt2"), 2 * (4 * c + u))
                    for b in range(NT):
                        for w in range(1 if b == 0 else 0, 2):
                            mm = pe.transpose((bA, bB)[b // 2][:, (2 * (b % 2) + w) * P:(2 * (b % 2) + w + 1) * P],
                                              pr2[u % 2][:, b, w * P:(w + 1) * P], ident[:])
                        if b % 2:
                            mm.then_inc(sem("pt2_ps"), 1)

                def outs(u):
                    half = slice(64 * (u % 2), 64 * (u % 2) + 64)
                    pe.wait_ge(sem("pt2"), 2 * (4 * c + u + 1))
                    for b in range(NT):
                        for w in range(1 if b == 0 else 0, 2):
                            mm = pe.matmul(O_BANK[u][half, b * P:(b + 1) * P], v_cur[:, b - 1 + w, :],
                                           pt2[:, b, w * P:(w + 1) * P], start=w == 0 or b == 0, stop=w == 1)
                    if u % 2:
                        mm.then_inc(sem("att_ps"), 1)

                stages = {"kva": kva, "kvb": kvb, "sw": sw, "tv": tv, "tk": tk, "sc": sc, "ro": ro, "rm": rm, "rs": rs,
                          "rr": rr, "sa": sa}
                for n in range(3):
                    stages[f"sp{n}"] = lambda n=n: sp(n)
                for u in range(4):
                    stages[f"L{u}"] = lambda u=u: logits(u)
                    stages[f"T{u}"] = lambda u=u: probs_t(u)
                    stages[f"O{u}"] = lambda u=u: outs(u)
                run(tokens, stages, slab, None)
            ret_rounds(pe, per_round)

        def ret_act(act):
            def per_round(tokens, ph, i, c):
                def slab(j, t):
                    if t == 0:
                        split_hi(act, ph, i, j + LEAD)

                def kvb():
                    act.wait_ge(sem("kv_ps"), 2)
                    act.copy(av_tok[:].rearrange("p n d -> p (n d)"), bD[:]).then_inc(sem("kv_act"), 1)
                    act.wait_ge(sem("kv_ps"), 3)
                    act.copy(kv_dup[:, 0, :], bB[:]).then_inc(sem("kv_act"), 1)
                    act.copy(kv_dup[:, 1, :], bC[:]).then_inc(sem("kv_act"), 1)

                def tv():
                    for e, bank in enumerate((bC, bD)):
                        act.wait_ge(sem("tv2_ps"), 2 * c + e + 1)
                        act.copy(v_tok[:, :, e * P:(e + 1) * P], c4(bank[:])).then_inc(sem("v_tok"), 1)

                def tk():
                    act.wait_ge(sem("tk2_ps"), c + 1)
                    act.activation(kdec2[:], bA[:], ACT.Copy, scale=hd[:, 0:1]).then_inc(sem("kdec2"), 1)

                def y2_():
                    for e, bank in enumerate((bC, bD)):
                        act.wait_ge(sem("ro_ps"), 2 * c + e + 1)
                        act.copy(y_r[e][:], bank[:]).then_inc(sem("ret_y"), 1)

                def rs():
                    for e in range(2):
                        act.wait_ge(sem("gn_c"), 2 * c + e + 1)
                        act.activation(gn_sq[e][:], y_r[e][:], ACT.Square).then_inc(sem("gn_sq"), 1)
                    for e in range(2):
                        if e == 1:
                            act.wait_ge(sem("gn_c"), 2 * c + 2)
                        act.activation(gn_th[e], r_g[e][:], ACT.Tanh, scale=0.5).then_inc(sem("gn_tanh"), 1)

                def softmax(u):
                    act.wait_ge(sem("lg_max"), 4 * c + u + 1)
                    if u == 1:
                        act.wait_ge(sem("ret_out"), 2 * c + 2)
                    if u >= 2:
                        act.wait_ge(sem("pt2_ps"), 2 * (4 * c + u - 1))
                    act.activation(es2[:], nm2[:], ACT.Exp, bias=hs[:, u:u + 1])
                    for b in range(NT):
                        ins = act.activation(pr2[u % 2][:, b, :], lg[:, b, :], ACT.Exp, bias=nm2[:, b:b + 1],
                                             accum_out=ls2[:, b:b + 1])
                    ins.then_inc(sem("exp2"), 1)

                def probs_t(u):
                    for h, bank in enumerate((bA, bB)):
                        act.wait_ge(sem("pt2_ps"), 2 * (4 * c + u) + h + 1)
                        lo = P if h == 0 else 0
                        act.copy(pt2[:, 2 * h:2 * h + 2, :].rearrange("p b c -> p (b c)")[:, lo:], bank[:, lo:])\
                            .then_inc(sem("pt2"), 1)

                stages = {"kvb": kvb, "tv": tv, "tk": tk, "y2": y2_, "rs": rs}
                for u in range(4):
                    stages[f"E{u}"] = lambda u=u: softmax(u)
                    stages[f"T{u}"] = lambda u=u: probs_t(u)
                run(tokens, stages, slab, None)
            ret_rounds(act, per_round)

        RET_STEPS = 20

        def ret_dve(dve, step):
            start = [0]

            def dyn(ap):
                return ap.rearrange("p a c -> p (a c)")

            def rotate(bank, src, dst, cos, sin, done):
                step(dve.tensor_tensor(rot_buf[0][:], bank[:], sin[:], ALU.mult))
                step(dve.tensor_tensor(dst[:], src[:], cos[:], ALU.mult))
                dve.tensor_tensor(dst[:], dst[:], rot_buf[0][:], ALU.add).then_inc(sem(done), 1)

            rot_buf = [None]

            def per_round(tokens, ph, i, c):
                if c is not None:
                    step.rounds(start[0], RET_STEPS, c)

                def evac(j):
                    if ph is ph_kv:
                        dst = (q_r, k_r)[j] if j < 2 else R_DEST[j - 2]
                        bias = bias_cols[:, j:j + 1]
                    else:
                        dst, bias = R_DEST[j], hb[:, j:j + 1]
                        if j == 2:
                            dve.wait_ge(sem("tv2_ps"), 2 * c + 2)
                        if j == 6:
                            dve.wait_ge(sem("gn_tanh"), 2 * c + 2)
                    dve.wait_ge(s_used, ph.index(i, j) + 1)
                    dve.tensor_tensor(dst[:], bank_slab[j % 2][:], r_row[:], ALU.mult).then_inc(sem("scaled2"), 1)
                    dve.wait_ge(sem("scaled2"), ph.index(i, j) - ph_kv.first + 1)
                    dve.tensor_scalar(dst[:], dst[:], bias, None, ALU.add).then_inc(sem("taken2"), 1)

                def kva():
                    dve.wait_ge(sem("kv_ps"), 1)
                    dve.wait_ge(sem("taken2"), 2)
                    rot_buf[0] = q_dec2
                    rotate(bA, q_r, sc_t, cos_a, sin_a, "kv_rot")

                def rb():
                    dve.wait_ge(sem("taken2"), 8 * c + 10)
                    if ph is not None:
                        step(dve.tensor_scalar(hb[:], bias_cols[:, bass.ds(8 * i + 10, 8)], 1.0, None, ALU.mult))
                    else:
                        step(dve.tensor_scalar(hb[:], hb[:], 1.0, None, ALU.mult))
                    step(dve.tensor_scalar(hg[:], dyn(ret_gain[:, bass.ds(c, 1), :]), 0.5, None, ALU.mult))
                    step(dve.tensor_scalar(hs[:], dyn(sink_cols[:, bass.ds(c, 1), :]), 1.0, None, ALU.mult))
                    step(dve.tensor_scalar(hd[:], dyn(k_decay[:, bass.ds(c, 1), :]), 1.0, None, ALU.mult))

                def kcur():
                    dve.wait_ge(sem("kv_act"), 3)
                    step(dve.tensor_scalar(k_cur[:], dyn(kv_dup[:, bass.ds(c // 2, 1), :]), 1.0, None, ALU.mult))
                    av = av_tok[:].rearrange("p n (v d) -> p v n d", v=2)[:, bass.ds(c // 2, 1), :, :]
                    dve.tensor_scalar(v_cur[:], av.rearrange("p a n d -> p (a n) d"), 1.0, None, ALU.mult)\
                        .then_inc(sem("kv_cur"), 1)

                def rot():
                    rot_buf[0] = sc_t
                    for n, (bank, src, dst) in enumerate(((bA, r_q, q_r), (bB, r_k, k_r))):
                        dve.wait_ge(sem("sw_ps"), 2 * c + n + 1)
                        if n == 1:
                            dve.wait_ge(sem("rot"), 2 * c + 1)
                        rotate(bank, src, dst, cos_r, sin_r, "rot")

                def sc():
                    dve.wait_ge(sem("sc_ps"), c + 1)
                    dve.wait_ge(sem("rot"), 2 * c + 2)
                    dt = decay_t[:, bass.ds(c, 1), :].to_broadcast([P, NT, P])
                    dve.tensor_tensor(c4(sc_t[:]), c4(bB[:]), dt, ALU.mult).then_inc(sem("sc_t"), 1)

                def qd():
                    qd_ = q_decay[:, bass.ds(c, 1), :].to_broadcast([P, NT, P])
                    dve.tensor_tensor(c4(q_dec2[:]), c4(q_r[:]), qd_, ALU.mult).then_inc(sem("q_dec2"), 1)

                def sp(n):
                    dve.wait_ge(sem("sp_ps"), 3 * c + n + 1)
                    bank = (bE, bF, bE)[n]
                    if n == 0:
                        dve.tensor_copy(st2[0][:], bank[:, 0:2 * P]).then_inc(sem("state2"), 1)
                    else:
                        dve.wait_ge(sem("state2"), 3 * c + n)
                        dve.scalar_tensor_tensor(out=st2[n][:], in0=st2[n - 1][:], scalar=hd[:, 1:2],
                                                 in1=bank[:, 0:2 * P], op0=ALU.mult, op1=ALU.add)\
                            .then_inc(sem("state2"), 1)

                def rota():
                    dve.wait_ge(sem("ro_ps"), 2 * c + 2)
                    rot_buf[0] = sc_t
                    for n in range(2):
                        dve.wait_ge(sem("sa_ps"), 2 * c + n + 1)
                        if n == 1:
                            dve.wait_ge(sem("rot_a"), 2 * c + 1)
                        rotate((bE, bF)[n], a_q[n], aq_r[n], cos_a, sin_a, "rot_a")

                def yc():
                    dve.wait_ge(sem("gn_ps"), 3 * c + 1)
                    dve.wait_ge(sem("rot_a"), 2 * c + 2)
                    for e in range(2):
                        dve.scalar_tensor_tensor(out=y_r[e][:], in0=bA[:], scalar=-1.0 / (2 * P), in1=y_r[e][:],
                                                 op0=ALU.mult, op1=ALU.add).then_inc(sem("gn_c"), 1)

                def rs():
                    dve.wait_ge(sem("gn_ps"), 3 * c + 2)
                    dve.tensor_scalar(gsc[:], bB[:, 0:NT], 1.0 / (2 * P), EPS, ALU.mult, ALU.add)\
                        .then_inc(sem("gn_ms"), 1)
                    for e in range(2):
                        dve.wait_ge(sem("gn_tanh"), 2 * c + e + 1)
                        step(dve.scalar_tensor_tensor(out=gn_th[e], in0=gn_th[e], scalar=1.0, in1=r_g[e][:],
                                                      op0=ALU.add, op1=ALU.mult))

                def yo():
                    dve.wait_ge(sem("gn_ps"), 3 * c + 3)
                    for e in range(2):
                        ins = dve.scalar_tensor_tensor(out=y_r[e][:], in0=y_r[e][:], scalar=hg[:, e:e + 1], in1=bA[:],
                                                       op0=ALU.mult, op1=ALU.mult)
                        if e:
                            ins.then_inc(sem("gn_out"), 1)
                        else:
                            step(ins)
                    dve.wait_ge(sem("gn_out"), c + 1)
                    for e in range(2):
                        dst = br_a[:, bass.ds(2 * c + e, 1), :].rearrange("p a t -> p (a t)")
                        dve.tensor_tensor(dst, y_r[e][:], gn_th[e], ALU.mult).then_inc(sem("ret_out"), 1)

                def logits(u):
                    dve.wait_ge(sem("lg_ps"), 4 * c + u + 1)
                    if u > 0:
                        dve.wait_ge(sem("exp2"), 4 * c + u)
                    flat = lg[:].rearrange("p b c -> p (b c)")
                    bd = band[:].rearrange("p w c -> p (w c)")
                    x_, y_ = L_BANKS[u]
                    for lo, hi, bank in ((P, 2 * P, x_), (2 * P, 4 * P, x_), (4 * P, 6 * P, y_), (6 * P, 8 * P, y_)):
                        ins = dve.scalar_tensor_tensor(out=flat[:, lo:hi], in0=bank[:, lo % 512:lo % 512 + hi - lo],
                                                       scalar=0.125, in1=bd[:, lo % 256:], op0=ALU.mult, op1=ALU.add)
                    ins.then_inc(sem("lg"), 1)
                    dve.wait_ge(sem("lg"), 4 * c + u + 1)
                    step(dve.tensor_reduce(nm2[:], lg[:], AX.X, ALU.max))
                    dve.tensor_scalar(nm2[:], nm2[:], hs[:, u:u + 1], -1.0, ALU.max, ALU.mult)\
                        .then_inc(sem("lg_max"), 1)

                def sums(u):
                    dve.wait_ge(sem("exp2"), 4 * c + u + 1)
                    if u > 0:
                        dve.wait_ge(sem("probs2"), 4 * c + u)
                    dve.tensor_tensor(rd2[:], ls2[:], es2[:], ALU.add).then_inc(sem("att_sum"), 1)
                    dve.wait_ge(sem("att_sum"), 4 * c + u + 1)
                    dve.reciprocal(rd2[:], rd2[:]).then_inc(sem("att_inv"), 1)

                def ev(a_):
                    dve.wait_ge(sem("att_ps"), 2 * c + a_ + 1)
                    dst = br_b[:, bass.ds(2 * c + a_, 1), :].rearrange("p a t -> p (a t)")
                    dve.tensor_scalar(dst, O_BANK[2 * a_][:], 1.0, None, ALU.mult).then_inc(sem("att_out"), 1)

                stages = {"kva": kva, "rb": rb, "kcur": kcur, "rot": rot, "sc": sc, "qd": qd, "rota": rota, "yc": yc,
                          "rs": rs, "yo": yo, "ev0": lambda: ev(0), "ev1": lambda: ev(1)}
                for n in range(3):
                    stages[f"sp{n}"] = lambda n=n: sp(n)
                for u in range(4):
                    stages[f"L{u}"] = lambda u=u: logits(u)
                    stages[f"M{u}"] = lambda u=u: sums(u)
                if c is None:
                    dve.wait_ge(sem("norm_row"), 3)
                    step(dve.memset(lg[:, 0, 0:P], -1e30))
                run(tokens, stages, None, evac)
                if c is None:
                    start[0] = step.value()
                else:
                    assert step.n == RET_STEPS, step.n
            ret_rounds(dve, per_round)
            step.straight(start[0] + RET_HEADS * RET_STEPS)
            dve.wait_ge(sem("ret_out"), 2 * RET_HEADS)
            dve.wait_ge(sem("att_out"), 2 * RET_HEADS)
            dve.tensor_scalar(ms_col[:], ms_col[:], 1.0, None, ALU.mult).then_inc(sem("branches_done"), 1)

        def ret_pool(pool):
            def per_round(tokens, ph, i, c):
                def slab(j, t):
                    if t == 0:
                        split_lo(pool, ph, i, j + LEAD)

                def rs():
                    pool.wait_ge(sem("gn_ms"), c + 1)
                    pool.tensor_tensor(grs[:], gsc[:], mhalf[:, 0:NT], ALU.pow).then_inc(sem("gn_scale"), 1)
                    pool.wait_ge(sem("gn_scale"), 2 * c + 1)
                    pool.tensor_tensor(r_diag[:], over_tiles(ident[:]), over_cols(grs[:]), ALU.mult)\
                        .then_inc(sem("gn_scale"), 1)

                def probs(u):
                    pool.wait_ge(sem("att_inv"), 4 * c + u + 1)
                    pool.tensor_tensor(pr2[u % 2][:], pr2[u % 2][:],
                                       rd2[:].unsqueeze(2).to_broadcast([P, NT, 2 * P]), ALU.mult)\
                        .then_inc(sem("probs2"), 1)
                stages = {"rs": rs}
                for u in range(4):
                    stages[f"M{u}"] = lambda u=u: probs(u)
                run(tokens, stages, slab, None)
            ret_rounds(pool, per_round)

        FFN_PARTS = [(ph_ffn, 0, 8), (ph_ffn, 1, 8), (ph_ffn_end, 0, FF2_TILES - 16)]

        def ffn_part_sem(p, m):
            return (sem("h_new"), 3 * KT + m + 1) if p == 2 else (sem("ffn_part"), 8 * p + m + 1)

        def ffn_pe(pe):
            for p, (ph, i, n) in enumerate(FFN_PARTS):
                for t in range(n):
                    for g in range(2):
                        if p == 0 and t == 0 and g == 0:
                            pe.wait_ge(sem("h_new"), 3 * KT)
                        if t > 0:
                            pe.wait_ge(sem("ffn_scaled"), 2 * (8 * p + t - 1) + g + 1)
                        elif p > 0:
                            pe.wait_ge(*ffn_part_sem(p - 1, 6 + g))
                        for k in range(KT):
                            products_and_norm(pe, ph, i, 2 * t + g, k, bank_slab[g][:], 3 if p == 0 else None)
                for m in range(KT):
                    if m < 2:
                        pe.wait_ge(sem("ffn_scaled"), 2 * (8 * p + n - 1) + m + 1)
                    else:
                        pe.wait_ge(*ffn_part_sem(p, m - 2))
                    for k in range(n):
                        if m == 0:
                            pe.wait_ge(sem("ffn_lo"), 8 * p + k + 1)
                        slab_products(pe, ph, i, 2 * n + m, bank_slab[m % 2][:], y_hi, y_lo, ks=(k,), n_k=n)
            norm_pe(pe, 4)
            norm_pe_row(pe, 4)

        def ffn_act(act):
            def square(m):
                act.wait_ge(sem("h_new"), 3 * KT + m + 1)
                norm_act_square(act, 4, m)

            for p, (ph, i, n) in enumerate(FFN_PARTS):
                for j in range(2 * n + KT):
                    if p < 2 or j + LEAD < 2 * n + KT:
                        split_hi(act, ph, i, j + LEAD)
                    if j % 2 == 0 and j < 2 * n:
                        t = j // 2
                        act.wait_ge(sem("ffn_scaled"), 2 * (8 * p + t) + 1)
                        act.activation(tmp[4 + t % 2][:], tmp[t % 2][:], ACT.Tanh, scale=0.5)\
                            .then_inc(sem("ffn_tanh"), 1)
                    if j % 2 == 1 and 3 <= j <= 2 * n + 1:
                        t = (j - 3) // 2
                        act.wait_ge(sem("ffn_act"), 8 * p + t + 1)
                        act.activation(y_hi[:, t, :], tmp[2 + t % 2][:], ACT.Copy, scale=0.5).then_inc(sem("ffn_hi"), 1)
                    if p == 2 and j > 2 * n:
                        square(j - 2 * n - 1)
            square(KT - 1)

        def ffn_dve(dve):
            for p, (ph, i, n) in enumerate(FFN_PARTS):
                def lo(t):
                    dve.wait_ge(sem("ffn_hi"), 8 * p + t + 1)
                    dve.scalar_tensor_tensor(out=y_lo[:, t, :], in0=tmp[2 + t % 2][:], scalar=0.5,
                                             in1=y_hi[:, t, :].bitcast(F32), op0=ALU.mult, op1=ALU.subtract)\
                        .then_inc(sem("ffn_lo"), 1)
                for t in range(n):
                    g, u, th_ = tmp[t % 2], tmp[2 + t % 2], tmp[4 + t % 2]
                    q = 8 * p + t
                    dve.wait_ge(s_used, ph.index(i, 2 * t) + 1)
                    dve.tensor_tensor(g[:], bank_slab[0][:], r_row[:], ALU.mult).then_inc(sem("ffn_scaled"), 1)
                    if t >= 1:
                        lo(t - 1)
                    dve.wait_ge(sem("ffn_tanh"), q + 1)
                    dve.scalar_tensor_tensor(out=g[:], in0=th_[:], scalar=1.0, in1=g[:], op0=ALU.add, op1=ALU.mult)\
                        .then_inc(sem("ffn_silu"), 1)
                    dve.wait_ge(s_used, ph.index(i, 2 * t + 1) + 1)
                    dve.tensor_tensor(u[:], bank_slab[1][:], r_row[:], ALU.mult).then_inc(sem("ffn_scaled"), 1)
                    dve.wait_ge(sem("ffn_scaled"), 2 * q + 2)
                    dve.wait_ge(sem("ffn_silu"), q + 1)
                    dve.tensor_tensor(u[:], u[:], g[:], ALU.mult).then_inc(sem("ffn_act"), 1)
                lo(n - 1)
                for m in range(KT):
                    dve.wait_ge(s_used, ph.index(i, 2 * n + m) + 1)
                    dve.tensor_tensor(h_res[:, m, :], h_res[:, m, :], bank_slab[m % 2][:], ALU.add)\
                        .then_inc(ffn_part_sem(p, m)[0], 1)
            norm_dve(dve, 4)
            norm_dve_row(dve, 4)
            for m in range(KT):
                dve.scalar_tensor_tensor(out=h_res[:, m, :], in0=h_res[:, m, :], scalar=gains[:, 4, m:m + 1],
                                         in1=r_row[:], op0=ALU.mult, op1=ALU.mult).then_inc(sem("result"), 1)

        def ffn_pool(pool):
            for p, (ph, i, n) in enumerate(FFN_PARTS):
                for j in range(2 * n + KT):
                    if p < 2 or j + LEAD < 2 * n + KT:
                        split_lo(pool, ph, i, j + LEAD)
                    if p == 2 and j > 2 * n:
                        norm_pool_add(pool, 4, j - 2 * n - 1)
            norm_pool_add(pool, 4, KT - 1)
            norm_pool_scale(pool, 4)

        def after_heads_pe(pe, tiles, transposes):
            merge_pe(pe, (ph_merge0, ph_merge1), 0)
            out_pe(pe, ph_out1, 0, 1)
            mlp_pe(pe)
            ret_pe(pe, tiles, transposes)
            merge_pe(pe, (ph_merge2,), 1)
            out_pe(pe, ph_out2, 1, 3)
            ffn_pe(pe)

        def after_heads_act(act):
            merge_act(act, (ph_merge0, ph_merge1), 0)
            out_act(act, ph_out1, 1)
            mlp_act(act)
            ret_act(act)
            merge_act(act, (ph_merge2,), 1)
            out_act(act, ph_out2, 3)
            ffn_act(act)

        def after_heads_pool(pool):
            merge_pool(pool, (ph_merge0, ph_merge1), 0)
            out_pool(pool, ph_out1, 1)
            mlp_pool(pool)
            ret_pool(pool)
            merge_pool(pool, (ph_merge2,), 1)
            out_pool(pool, ph_out2, 3)
            ffn_pool(pool)

        def after_heads_dve(dve, step):
            dve.wait_ge(sem("oa"), HEADS)
            dve.wait_ge(sem("ob"), HEADS)
            dve.tensor_scalar(ms_col[:, 0:1], ms_col[:, 0:1], 1.0, None, ALU.mult).then_inc(sem("branches_done"), 1)
            branches_lo(dve, 0)
            merge_dve(dve, (ph_merge0, ph_merge1), 0)
            out_dve(dve, ph_out1, 1)
            mlp_dve(dve)
            ret_dve(dve, step)
            branches_lo(dve, 1)
            merge_dve(dve, (ph_merge2,), 1, bias_gate)
            out_dve(dve, ph_out2, 3)
            ffn_dve(dve)

        block = ctx.enter_context(nc.Block())

        @block.sync
        def _(sp):
            h_view = dram["x_t"].rearrange("(k p) t -> p k t", p=P)
            for name, dst, src in (
                ("ld_x", h_res[:], h_view),
                ("ld_small", gains[:], dram["gains"]), ("ld_small", head_gain[:], dram["head_gain"]),
                ("ld_small", ident[:], dram["ident"]), ("ld_small", w_gates[:], dram["w_gates"]),
                ("ld_small", gate_rows[:], dram["gate_rows"].to_broadcast([P, 3, HEADS]))):
                sp.dma_start(dst, src).then_inc(sem(name), 16)
            for j in range(ph_heads.n):
                s = ph_heads.slot(j)
                if j == SLOTS:
                    for dst, src in ((upper, "upper"), (conv_w, "conv_w"), (level_mask, "level_mask"),
                                     (neg_mask, "neg_mask")):
                        sp.dma_start(dst[:], dram[src]).then_inc(sem("ld_head"), 16)
                if j >= SLOTS:
                    sp.wait_ge(s_lo, j - SLOTS + 1)
                sp.dma_start(raw[s][:].rearrange("p k c -> p (k c)"), dram["slabs"][j, :, :]).then_inc(s_raw[s], 16)
            for ph in phases:
                if ph is ph_mlp:
                    sp.wait_ge(sem("branch_taken"), 2 * KT + 1)
                    for name, dst in TAB2:
                        sp.dma_start(dst[:], dram[name]).then_inc(sem("ld_tab2"), 16)
                if ph is ph_out1:
                    sp.wait_ge(sem("merged"), 3 * AHEAD + 1)
                    sp.dma_start(h_res[:], h_view).then_inc(sem("ld_x"), 16)
                start = 1 if ph is ph_heads else 0
                if ph.iters - start > 1:
                    with sp.Fori(start, ph.iters) as i:
                        for j in range(ph.n):
                            load_slab(sp, ph, i, j)
                else:
                    for j in range(ph.n):
                        load_slab(sp, ph, start, j)
            for m in range(KT):
                sp.wait_ge(sem("result"), m + 1)
                sp.dma_start(out[m * P:(m + 1) * P, :], h_res[:, m, :]).then_inc(sem("stored"), 16)
            sp.wait_ge(sem("stored"), 16 * KT)

        @block.tensor
        def _(pe):
            pe.wait_ge(sem("setup_dve"), 1)
            norm_pe(pe, 0)

            def tiles(out_, lhs, rhs, start=True, stop=True):
                for n in range(NT):
                    c = slice(n * P, (n + 1) * P)
                    mm = pe.matmul(out_[:, c], lhs[:, c], rhs[:, c], start=start, stop=stop)
                return mm

            def transposes(out_, in_, n=NT):
                for k in range(n):
                    c = slice(k * P, (k + 1) * P)
                    mm = pe.transpose(out_[:, c], in_[:, c], ident[:])
                return mm

            def head_round(tokens, i, c):
                ph, ph_i = (ph_gates, 0) if isinstance(i, int) and i == HEADS else (ph_heads, i)

                def slab(j, t):
                    bank = bank_slab[HEAD_BANK[j]]
                    if t == 0:
                        if i is not None and not (isinstance(i, int) and i == 0 and j < 2):
                            pe.wait_ge(s_taken, ph_heads.index(i, j) - (1 if j == 0 else 2) + 1)
                    if isinstance(i, int) and i == 0 and j == 0:
                        pe.wait_ge(sem("u_lo"), t + 1)
                        if t == 4:
                            norm_pe_row(pe, 0)
                    slab_products(pe, ph, ph_i, j, bank[:], u_hi, u_lo, ks=(t,))

                def ssq():
                    if c is not None:
                        pe.wait_ge(sem("nmax"), 4 * c + 4)
                    for x in range(4):
                        pe.wait_ge(sem("sq"), 4 * i + x + 1)
                        for n in range(NT):
                            mm = pe.matmul(bD[:, 4 * x + n:4 * x + n + 1], sq[x][:, n * P:(n + 1) * P],
                                           ones[:, 0:1], start=True, stop=True)
                    mm.then_inc(sem("ssq_ps"), 1)

                def gates0():
                    pe.wait_ge(sem("gate_w"), 2)
                    for k in range(KT):
                        for w, x in ((wg_hi, u_hi), (wg_hi, u_lo), (wg_lo, u_hi)):
                            mm = pe.matmul(bA[0:24, :], w[:, k, :], x[:, k, :],
                                           start=k == 0 and w is wg_hi and x is u_hi,
                                           stop=k == KT - 1 and w is wg_lo)
                    mm.then_inc(sem("setup_ps"), 1)

                def gates0t():
                    pe.wait_ge(sem("gate_row"), 1)
                    for n in range(NT):
                        mm = pe.transpose(bB[:, 24 * n:24 * n + 24], g_row[0:24, n * P:(n + 1) * P], ident[0:24, 0:24])
                    mm.then_inc(sem("setup_ps"), 1)

                def gates2():
                    pe.wait_ge(sem("setup_dve"), 3)
                    pe.wait_ge(sem("ld_head"), 64)
                    g_all = table[:, :, Q_G, :]
                    pe.matmul(bB[:, 0:HEADS * NT].rearrange("p (h n) -> p h n", n=NT), upper[:], g_all,
                              start=True, stop=True)
                    pe.matmul(bC[:, 0:HEADS * NT].rearrange("p (h n) -> p h n", n=NT), ones[:], g_all,
                              start=True, stop=True).then_inc(sem("setup_ps"), 1)

                def fvt_():
                    pe.wait_ge(s_taken, 7 * c + 6)
                    pe.wait_ge(sem("ssc"), c + 1)
                    transposes(bD, raw_fv).then_inc(sem("fvt_ps"), 1)

                def rows():
                    pe.wait_ge(sem("diag"), 5 * c + 1)
                    pe.matmul(bB[:], ones[:], d_g[:], start=True, stop=True).then_inc(sem("row_ps"), 1)
                    pe.wait_ge(sem("diag"), 5 * c + 2)
                    pe.matmul(bC[:], ones[:], d_b[:], start=True, stop=True).then_inc(sem("row_ps"), 1)
                    pe.wait_ge(sem("diag"), 5 * c + 3)
                    pe.matmul(bA[:], ones[:], d_q[:], start=True, stop=True).then_inc(sem("row_ps"), 1)

                def frows():
                    pe.wait_ge(sem("diag"), 5 * c + 4)
                    pe.matmul(bE[:], ones[:], d_rk[:], start=True, stop=True).then_inc(sem("fox_rows_ps"), 1)
                    pe.wait_ge(sem("diag"), 5 * c + 5)
                    pe.wait_ge(sem("fvt"), c + 1)
                    pe.matmul(bD[:], ones[:], d_cum[:], start=True, stop=True).then_inc(sem("fox_rows_ps"), 1)

                def tkv():
                    pe.wait_ge(sem("dif"), c + 1)
                    transposes(bB, ck).then_inc(sem("tk_tv_ps"), 1)
                    pe.wait_ge(sem("decays"), 2 * c + 1)
                    transposes(bC, cv).then_inc(sem("tk_tv_ps"), 1)

                def kk():
                    pe.wait_ge(sem("decays"), 2 * c + 2)
                    tiles(bA, ck, ck).then_inc(sem("kk_qk_ps"), 1)

                def qk():
                    pe.wait_ge(sem("kv_scaled"), 2 * c + 1)
                    tiles(bB, ck, cq).then_inc(sem("kk_qk_ps"), 1)

                def xt():
                    pe.wait_ge(sem("kv_scaled"), 2 * c + 2)
                    pe.wait_ge(sem("z0"), c + 1)
                    transposes(bC, zi).then_inc(sem("x0_ps"), 1)

                def level_y(l):
                    pe.wait_ge(sem("atm"), 7 * c + l + 1)
                    if l == 1:
                        pe.wait_ge(sem("x0"), c + 1)
                        pe.wait_ge(sem("masked"), 2 * c + 1)
                    else:
                        pe.wait_ge(sem("x_new"), 5 * c + l - 1)
                    tiles(bA, atm[l % 2], xi).then_inc(sem("y_ps"), 1)

                def level_x(l):
                    pe.wait_ge(sem("y"), 6 * c + l)
                    if l == 1:
                        pe.wait_ge(sem("masked"), 2 * c + 2)
                    if l > 1:
                        pe.wait_ge(sem("z_new"), 6 * c + l - 1)
                    if l < LEVELS - 1:
                        tiles(bB, zi, yi).then_inc(sem("xy_ps"), 1)
                    tiles(bC, yi, zi).then_inc(sem("zy_ps"), 1)

                def vk():
                    pe.wait_ge(sem("z_new"), 6 * c + 6)
                    tiles(bA, zi, vp).then_inc(sem("val_kc_ps"), 1)
                    tiles(bB, kp, zi).then_inc(sem("val_kc_ps"), 1)

                def rec(n):
                    c_ = slice(n * P, (n + 1) * P)
                    if n == 0:
                        pe.wait_ge(sem("val"), c + 1)
                        pe.wait_ge(sem("kc"), c + 1)
                        pe.matmul(bC[:, c_], vp[:, c_], att[:, c_], start=True, stop=True)
                        pe.matmul(bB[:, 0:P], kd[:, c_], vp[:, c_], start=True, stop=True).then_inc(sem("s_ps"), 1)
                        return
                    pe.wait_ge(sem("s_new"), 3 * c + n)
                    pe.matmul(bA[:, 0:P], kp[:, c_], st[:], start=True, stop=True).then_inc(sem("vn_ps"), 1)
                    pe.matmul(bC[:, c_], st[:], qdec[:, c_], start=True, stop=False)

                def rec_v(n):
                    c_ = slice(n * P, (n + 1) * P)
                    pe.wait_ge(sem("v_new"), 3 * c + n)
                    mm = pe.matmul(bC[:, c_], vn[:], att[:, c_], start=False, stop=True)
                    if n < NT - 1:
                        pe.matmul(bB[:, 0:P], kd[:, c_], vn[:], start=True, stop=True).then_inc(sem("s_ps"), 1)
                    else:
                        mm.then_inc(sem("o_ps"), 1)

                def osq():
                    pe.wait_ge(sem("o_read"), 2 * c + 1)
                    for n in range(NT):
                        mm = pe.matmul(bA[:, n:n + 1], osq_[:, n * P:(n + 1) * P], ones[:, 0:1], start=True, stop=True)
                    mm.then_inc(sem("o_norm_ps"), 1)

                def orow():
                    pe.wait_ge(sem("odiag"), c + 1)
                    pe.matmul(bA[:], ones[:], d_b[:], start=True, stop=True).then_inc(sem("o_norm_ps"), 1)

                def logits(i_):
                    w = (i_ + 1) * P
                    if i_ == 0:
                        for name in ("fk", "fq", "cumr"):
                            pe.wait_ge(sem(name), c + 1)
                    else:
                        pe.wait_ge(sem("nmax"), 4 * c + i_)
                    pe.matmul(bD[:, 0:w], fqt[:, i_ * P:w], fkt[:, 0:w], start=True, stop=True).then_inc(sem("l_ps"), 1)

                def probs_t(i_):
                    pe.wait_ge(sem("probs"), 4 * c + i_ + 1)
                    if i_ > 0:
                        pe.wait_ge(sem("pt"), 4 * c + i_)
                    transposes(bE, pr, i_ + 1).then_inc(sem("pt_ps"), 1)

                def outs(i_):
                    pe.wait_ge(sem("pt"), 4 * c + i_ + 1)
                    if i_ == 0:
                        pe.wait_ge(s_taken, 7 * c + 7)
                    for j in range(i_ + 1):
                        mm = pe.matmul(bF[:, i_ * P:(i_ + 1) * P], fvt[:, j * P:(j + 1) * P], pt[:, j * P:(j + 1) * P],
                                       start=j == 0, stop=j == i_)
                    if i_ == NT - 1:
                        mm.then_inc(sem("fo_ps"), 1)

                stages = {"gates0": gates0, "gates0t": gates0t, "gates2": gates2, "ssq": ssq, "fvt": fvt_, "rows": rows,
                          "frows": frows, "tkv": tkv, "kk": kk, "qk": qk, "xt": xt, "vk": vk, "osq": osq,
                          "orow": orow}
                for l in range(1, LEVELS):
                    stages[f"Y{l}"] = lambda l=l: level_y(l)
                    stages[f"X{l}"] = lambda l=l: level_x(l)
                for n in range(NT):
                    stages[f"r{n}"] = lambda n=n: rec(n)
                    if n > 0:
                        stages[f"v{n}"] = lambda n=n: rec_v(n)
                    stages[f"S{n}"] = lambda n=n: logits(n)
                    stages[f"T{n}"] = lambda n=n: probs_t(n)
                    stages[f"O{n}"] = lambda n=n: outs(n)
                run(tokens, stages, slab, None)

            head_rounds(pe, head_round)
            after_heads_pe(pe, tiles, transposes)

        @block.scalar
        def _(act):
            act.wait_ge(sem("ld_x"), 16)
            for k in range(KT):
                act.activation(x_sq[k][:], h_res[:, k, :], ACT.Square).then_inc(sem("x_sq"), 1)
            split_hi(act, ph_heads, 0, 0)
            act.wait_ge(sem("ld_small"), 80)
            act.copy(wg_hi[:], w_gates[:]).then_inc(sem("gate_w"), 1)
            for k in range(KT):
                part_hi(act, 0, k)
            split_hi(act, ph_heads, 0, 1)

            def head_round(tokens, i, c):
                ph, ph_i = (ph_gates, 0) if isinstance(i, int) and i == HEADS else (ph_heads, i)

                def slab(j, t):
                    if t == 0:
                        split_hi(act, ph, ph_i, j + LEAD)

                def gates0t():
                    act.wait_ge(sem("setup_ps"), 1)
                    act.copy(g_row[0:24, :], bA[0:24, :]).then_inc(sem("gate_row"), 1)

                def gates1():
                    act.wait_ge(sem("setup_dve"), 2)
                    act.activation(e2[:], e2[:], ACT.Exp).then_inc(sem("act_step"), 1)
                    act.wait_ge(sem("act_step"), 1)
                    act.activation(sp2[:], e2[:], ACT.Ln, bias=1.0).then_inc(sem("setup_act"), 1)
                    act.activation(gate_rows[:, 1, :], gate_rows[:, 1, :], ACT.Exp).then_inc(sem("setup_act"), 1)
                    act.activation(t8[:], gt[:, :, 8:16].rearrange("p n h -> p h n"), ACT.Tanh, scale=0.5)\
                        .then_inc(sem("setup_act"), 1)

                def gates2():
                    act.wait_ge(sem("setup_dve"), 4)
                    act.activation(table[:, :, Q_EGL, :], gtot[:], ACT.Exp).then_inc(sem("setup_act"), 1)
                    act.activation(t8[:], table[:, :, Q_GCUM, :], ACT.Exp).then_inc(sem("setup_act"), 1)

                def tanh(x):
                    if x < 3:
                        act.wait_ge(sem("conv"), 3 * i + x + 1)
                    else:
                        act.wait_ge(s_taken, 7 * c + 7)
                    if x == 2:
                        act.wait_ge(sem("silu"), 4 * i + 1)
                    act.activation(th[x][:], (cq, ck, cv, raw_z)[x][:], ACT.Tanh, scale=0.5)\
                        .then_inc(sem("tanh"), 1)

                def squares(pair):
                    for x in (2 * pair, 2 * pair + 1):
                        if pair == 0:
                            act.wait_ge(sem("silu"), 4 * i + x + 1)
                        else:
                            act.wait_ge(s_taken, 7 * i + 5)
                        act.activation(sq[x][:], (cq, ck, raw_fq, raw_fk)[x][:], ACT.Square).then_inc(sem("sq"), 1)

                def fq_():
                    act.activation(fqt[:], raw_fq[:], ACT.Copy, scale=head_gain[:, 1:2]).then_inc(sem("fq"), 1)

                def fvt_():
                    act.wait_ge(sem("fvt_ps"), c + 1)
                    act.copy(fvt[:], bD[:]).then_inc(sem("fvt"), 1)

                def rows():
                    act.wait_ge(sem("row_ps"), 3 * c + 1)
                    act.activation(e_g[:], bB[:], ACT.Exp).then_inc(sem("eg"), 1)

                def dif():
                    act.wait_ge(sem("dif"), c + 1)
                    act.activation(dt_[:], dt_[:], ACT.Exp).then_inc(sem("edif"), 1)

                def frows():
                    act.wait_ge(sem("fox_rows_ps"), 2 * c + 2)
                    act.copy(cumr[:], bD[:]).then_inc(sem("cumr"), 1)

                def xt():
                    act.wait_ge(sem("x0_ps"), c + 1)
                    act.copy(xi[:], bC[:]).then_inc(sem("x0"), 1)

                def level_y(l):
                    act.wait_ge(sem("y_ps"), 6 * c + l)
                    act.copy(yi[:], bA[:]).then_inc(sem("y"), 1)

                def vk():
                    act.wait_ge(sem("val_kc_ps"), 2 * c + 1)
                    act.copy(vp[:], bA[:]).then_inc(sem("val"), 1)

                def osq():
                    act.wait_ge(sem("o_ps"), c + 1)
                    act.activation(osq_[:], bC[:], ACT.Square).then_inc(sem("o_read"), 1)
                    act.activation(on[:], bC[:], ACT.Copy, scale=head_gain[:, 0:1]).then_inc(sem("o_read"), 1)

                def probs(i_):
                    w = (i_ + 1) * P
                    act.wait_ge(sem("nmax"), 4 * c + i_ + 1)
                    if i_ > 0:
                        act.wait_ge(sem("pt_ps"), 4 * c + i_)
                    act.activation(pr[:, 0:w], sb_[:, 0:w], ACT.Exp, bias=nmax[:, i_:i_ + 1],
                                   accum_out=lsum[:, i_:i_ + 1]).then_inc(sem("exp"), 1)

                def probs_t(i_):
                    w = (i_ + 1) * P
                    act.wait_ge(sem("pt_ps"), 4 * c + i_ + 1)
                    act.copy(pt[:, 0:w], bE[:, 0:w]).then_inc(sem("pt"), 1)

                stages = {"gates0t": gates0t, "gates1": gates1, "gates2": gates2, "sq0": lambda: squares(0),
                          "sq1": lambda: squares(1), "fq": fq_, "fvt": fvt_, "rows": rows, "dif": dif,
                          "frows": frows, "xt": xt, "vk": vk, "osq": osq}
                for x in range(4):
                    stages[f"th{x}"] = lambda x=x: tanh(x)
                for l in range(1, LEVELS):
                    stages[f"Y{l}"] = lambda l=l: level_y(l)
                for n in range(NT):
                    stages[f"E{n}"] = lambda n=n: probs(n)
                    stages[f"T{n}"] = lambda n=n: probs_t(n)
                run(tokens, stages, slab, None)

            head_rounds(act, head_round)
            after_heads_act(act)

        @block.vector
        def _(dve):
            step = Steps(dve, sem("dve_step"))
            dve.memset(ones[:], 1.0)
            dve.wait_ge(sem("ld_small"), 80)
            step(dve.tensor_scalar(head_gain[:, 0:1], head_gain[:, 0:1], 0.5, None, ALU.mult))
            dve.wait_ge(sem("x_sq"), 2)
            dve.tensor_tensor(sq_sum[:], x_sq[0][:], x_sq[1][:], ALU.add).then_inc(sem("dve_step"), 1)
            for k in range(2, KT):
                dve.wait_ge(sem("x_sq"), k + 1)
                dve.wait_ge(sem("dve_step"), step.n + k - 1)
                dve.tensor_tensor(sq_sum[:], sq_sum[:], x_sq[k][:], ALU.add)\
                    .then_inc(sem("dve_step") if k < KT - 1 else sem("setup_dve"), 1)
            step.n += KT - 2
            dve.wait_ge(sem("gate_w"), 1)
            dve.tensor_tensor(wg_lo[:], w_gates[:], wg_hi[:].bitcast(F32), ALU.subtract).then_inc(sem("gate_w"), 1)
            norm_dve(dve, 0)
            for k in range(KT):
                part_lo(dve, 0, k)
            norm_dve_row(dve, 0)
            for n, name in enumerate(("gate_taken", "branch_taken", "merged")):
                dve.memset(rawq[n][:, 0:3], 0.0).then_inc(sem(name), 1)
            round0_end = []

            def head_round(tokens, i, c):
                ph, ph_i = (ph_gates, 0) if isinstance(i, int) and i == HEADS else (ph_heads, i)

                if c is not None:
                    step.rounds(round0_end[0], DVE_STEPS, c)

                def evac(j):
                    dst = (rawq[0], rawq[1], rawq[2], raw_fq, raw_fk, raw_fv, raw_z)[j]
                    dst = dst[:, 3:3 + T] if j < 3 else dst[:]
                    dve.wait_ge(s_used, ph.index(ph_i, j) + 1)
                    if c is not None and j == 3:
                        dve.wait_ge(sem("fq"), c + 1)
                    if c is not None and j == 5:
                        dve.wait_ge(sem("fvt_ps"), c + 1)
                    dve.tensor_tensor(dst, bank_slab[HEAD_BANK[j]][:], r_row[:], ALU.mult).then_inc(s_taken, 1)

                def gates1():
                    dve.wait_ge(sem("setup_ps"), 2)
                    step(dve.tensor_tensor(gt[:], bB[:, 0:96].rearrange("p (n c) -> p n c", n=NT),
                                           r_col[:].unsqueeze(2).to_broadcast([P, NT, 24]), ALU.mult))

                    def row(q):
                        return gate_rows[:, q, :].unsqueeze(2).to_broadcast([P, HEADS, NT])

                    def heads_of(c):
                        return gt[:, :, c:c + HEADS].rearrange("p n h -> p h n")

                    dve.tensor_tensor(y2[:, 0:HEADS, :], heads_of(0), row(0), ALU.add)
                    step(dve.tensor_tensor(y2[:, HEADS:, :], heads_of(16), row(2), ALU.add))
                    step(dve.tensor_scalar(y2[:, HEADS:, :], y2[:, HEADS:, :], -1.0, None, ALU.mult))
                    dve.scalar_tensor_tensor(out=e2[:], in0=y2[:], scalar=-1.0, in1=y2[:], op0=ALU.mult, op1=ALU.min)\
                        .then_inc(sem("setup_dve"), 1)
                    dve.wait_ge(sem("setup_act"), 1)
                    step(dve.scalar_tensor_tensor(out=sp2[:], in0=y2[:], scalar=0.0, in1=sp2[:], op0=ALU.max,
                                                  op1=ALU.add))
                    dve.wait_ge(sem("setup_act"), 2)
                    dve.scalar_tensor_tensor(out=table[:, :, Q_G, :], in0=sp2[:, 0:HEADS, :], scalar=-1.0, in1=row(1),
                                             op0=ALU.mult, op1=ALU.mult).then_inc(sem("setup_dve"), 1)
                    step(dve.tensor_scalar(table[:, :, Q_LF, :], sp2[:, HEADS:, :], -1.0, None, ALU.mult))
                    dve.wait_ge(sem("setup_act"), 3)
                    dve.tensor_scalar(table[:, :, Q_BETA, :], t8[:], 0.5, 0.5, ALU.mult, ALU.add)
                    step(dve.memset(table[:, :, Q_LFPREV, 0:1], 0.0))
                    for n in range(1, NT):
                        step(dve.tensor_tensor(table[:, :, Q_LFPREV, n:n + 1], table[:, :, Q_LFPREV, n - 1:n],
                                               table[:, :, Q_LF, n - 1:n], ALU.add))

                def gates2():
                    dve.wait_ge(sem("setup_ps"), 3)
                    step(dve.tensor_copy(table[:, :, Q_GCUM, :],
                                         bB[:, 0:HEADS * NT].rearrange("p (h n) -> p h n", n=NT)))
                    dve.tensor_tensor(gtot[:], bC[:, 0:HEADS * NT].rearrange("p (h n) -> p h n", n=NT),
                                      table[:, :, Q_GCUM, :], ALU.subtract).then_inc(sem("setup_dve"), 1)
                    dve.wait_ge(sem("setup_act"), 5)
                    step(dve.tensor_tensor(table[:, :, Q_BEG, :], t8[:], table[:, :, Q_BETA, :], ALU.mult))
                    dve.wait_ge(sem("ld_head"), 64)

                def conv(x, w):
                    dst = (cq, ck, cv)[x]
                    if w == 0:
                        dve.wait_ge(s_taken, 7 * i + x + 1)
                        if x == 0:
                            step(dve.tensor_scalar(h_conv[:],
                                                   conv_w[:, bass.ds(i, 1), :].rearrange("p a w -> p (a w)"),
                                                   1.0, None, ALU.mult))
                        step(dve.tensor_scalar(dst[:], rawq[x][:, 0:T], h_conv[:, 4 * x:4 * x + 1], None, ALU.mult))
                        return
                    ins = dve.scalar_tensor_tensor(out=dst[:], in0=rawq[x][:, w:w + T],
                                                   scalar=h_conv[:, 4 * x + w:4 * x + w + 1], in1=dst[:],
                                                   op0=ALU.mult, op1=ALU.add)
                    if w < 3:
                        step(ins)
                    else:
                        ins.then_inc(sem("conv"), 1)

                def silu(x):
                    dve.wait_ge(sem("tanh"), 4 * (c if x == 3 else i) + x + 1)
                    src, dst = ((cq, cq), (ck, ck), (cv, cv), (raw_z, sz))[x]
                    dve.scalar_tensor_tensor(out=dst[:], in0=th[x][:], scalar=1.0, in1=src[:], op0=ALU.add,
                                             op1=ALU.mult).then_inc(sem("silu"), 1)

                def cola():
                    dve.wait_ge(sem("ssq_ps"), i + 1)
                    dve.tensor_scalar(ssc[:, 0:8], bD[:, 0:8], 4 * EPS, None, ALU.add)
                    dve.tensor_scalar(ssc[:, 8:16], bD[:, 8:16], 1.0 / P, EPS, ALU.mult, ALU.add)\
                        .then_inc(sem("ssc"), 1)

                def colb():
                    step(dve.tensor_scalar(h_small[:].rearrange("p q n -> p (q n)"),
                                           table[:, bass.ds(i, 1), :, :].rearrange("p a q n -> p (a q n)"),
                                           1.0, None, ALU.mult))
                    dve.wait_ge(sem("rsc"), i + 1)
                    rk = rsc[:, 4:8]
                    dve.tensor_tensor(cols[:, C_BK, :], h_small[:, Q_BETA, :], rk, ALU.mult)
                    dve.tensor_tensor(cols[:, C_KB, :], h_small[:, Q_BEG, :], rk, ALU.mult)
                    dve.tensor_tensor(cols[:, C_KD, :], h_small[:, Q_EGL, :], rk, ALU.mult)
                    dve.tensor_scalar(cols[:, C_RQ, :], rsc[:, 0:4], SCALE, None, ALU.mult)
                    dve.tensor_scalar(cols[:, C_RFQ, :], rsc[:, 8:12], SCALE, None, ALU.mult)
                    dve.tensor_scalar(cols[:, C_VB, :], h_small[:, Q_BETA, :], 0.5, None, ALU.mult)\
                        .then_inc(sem("cols"), 1)
                    dve.wait_ge(sem("cols"), i + 1)

                def dif():
                    dve.wait_ge(sem("eg"), c + 1)
                    step(dve.tensor_tensor(c4(dt_[:]), c4(bB[:]), over_cols(h_small[:, Q_GCUM, :]), ALU.subtract))
                    dve.tensor_scalar(dt_[:], dt_[:], 0.0, None, ALU.min).then_inc(sem("dif"), 1)
                    dve.tensor_scalar(dec[:], e_g[:, P - 1:T:P], 1.0, None, ALU.mult)

                def dt():
                    dve.wait_ge(sem("edif"), c + 1)
                    step(dve.scalar_tensor_tensor(out=c4(dt_[:]), in0=c4(dt_[:]), scalar=1.0, in1=over_tiles(upper[:]),
                                                  op0=ALU.min, op1=ALU.mult))
                    step(dve.tensor_tensor(c4(dt_[:]), c4(dt_[:]), over_cols(rsc[:, 4:8]), ALU.mult))
                    dve.wait_ge(sem("row_ps"), 3 * c + 3)
                    dve.tensor_tensor(bdt[:], bC[:], dt_[:], ALU.mult).then_inc(sem("decays"), 1)
                    dve.tensor_tensor(adt[:], bA[:], dt_[:], ALU.mult)
                    dve.tensor_tensor(e_g[:], bA[:], e_g[:], ALU.mult).then_inc(sem("decays"), 1)
                    dve.wait_ge(sem("decays"), 2 * c + 2)
                    step(dve.tensor_tensor(qdec[:], e_g[:], cq[:], ALU.mult))

                def frows():
                    dve.wait_ge(sem("fox_rows_ps"), 2 * c + 1)
                    dve.scalar_tensor_tensor(out=fkt[:], in0=raw_fk[:], scalar=head_gain[:, 2:3], in1=bE[:],
                                             op0=ALU.mult, op1=ALU.mult).then_inc(sem("fk"), 1)

                def tkv():
                    dve.wait_ge(sem("tk_tv_ps"), 2 * c + 1)
                    dve.tensor_tensor(c4(kp[:]), c4(bB[:]), over_cols(cols[:, C_KB, :]), ALU.mult)
                    dve.tensor_tensor(c4(kd[:]), c4(bB[:]), over_cols(cols[:, C_KD, :]), ALU.mult)\
                        .then_inc(sem("kv_scaled"), 1)
                    dve.wait_ge(sem("tk_tv_ps"), 2 * c + 2)
                    dve.tensor_tensor(c4(vp[:]), c4(bC[:]), over_cols(cols[:, C_VB, :]), ALU.mult)\
                        .then_inc(sem("kv_scaled"), 1)

                def kk():
                    dve.wait_ge(sem("kk_qk_ps"), 2 * c + 1)
                    dve.tensor_tensor(a_t[:], bA[:], bdt[:], ALU.mult).then_inc(sem("masked"), 1)

                def qk():
                    dve.wait_ge(sem("kk_qk_ps"), 2 * c + 2)
                    dve.tensor_tensor(att[:], bB[:], adt[:], ALU.mult).then_inc(sem("masked"), 1)

                def z0():
                    dve.wait_ge(sem("atm"), 7 * c + 1)
                    dve.tensor_tensor(c4(zi[:]), over_tiles(ident[:]), c4(atm[0][:]), ALU.subtract)\
                        .then_inc(sem("z0"), 1)

                def level_x(l):
                    if l < LEVELS - 1:
                        dve.wait_ge(sem("xy_ps"), 5 * c + l)
                        dve.tensor_tensor(xi[:], xi[:], bB[:], ALU.subtract).then_inc(sem("x_new"), 1)
                    dve.wait_ge(sem("zy_ps"), 6 * c + l)
                    dve.tensor_tensor(zi[:], zi[:], bC[:], ALU.subtract).then_inc(sem("z_new"), 1)

                def vk():
                    dve.wait_ge(sem("val_kc_ps"), 2 * c + 2)
                    dve.tensor_copy(kp[:], bB[:]).then_inc(sem("kc"), 1)

                def rec(n):
                    if n > 0:
                        dve.wait_ge(sem("vn_ps"), 3 * c + n)
                        dve.tensor_tensor(vn[:], vp[:, n * P:(n + 1) * P], bA[:, 0:P], ALU.subtract)\
                            .then_inc(sem("v_new"), 1)
                        return
                    dve.wait_ge(sem("s_ps"), 3 * c + 1)
                    dve.wait_ge(sem("val"), c + 1)
                    dve.tensor_copy(st[:], bB[:, 0:P]).then_inc(sem("s_new"), 1)

                def rec_v(n):
                    dve.wait_ge(sem("s_ps"), 3 * c + n + 1)
                    dve.scalar_tensor_tensor(out=st[:], in0=st[:], scalar=dec[:, n:n + 1], in1=bB[:, 0:P],
                                             op0=ALU.mult, op1=ALU.add).then_inc(sem("s_new"), 1)

                def osq():
                    dve.wait_ge(sem("o_norm_ps"), 2 * c + 1)
                    dve.tensor_scalar(osc[:], bA[:, 0:NT], 1.0 / P, EPS, ALU.mult, ALU.add).then_inc(sem("osc"), 1)

                def orow():
                    dve.wait_ge(sem("o_norm_ps"), 2 * c + 2)
                    dve.wait_ge(sem("o_read"), 2 * c + 2)
                    step(dve.tensor_tensor(on[:], on[:], bA[:], ALU.mult))
                    dve.tensor_tensor(br_a[:, bass.ds(c, 1), :].rearrange("p a t -> p (a t)"), on[:], sz[:], ALU.mult)\
                        .then_inc(sem("oa"), 1)

                def logits(i_):
                    w = (i_ + 1) * P
                    dve.wait_ge(sem("l_ps"), 4 * c + i_ + 1)
                    if i_ == 0:
                        dve.wait_ge(sem("cumr"), c + 1)
                    step(dve.scalar_tensor_tensor(out=sb_[:, 0:w], in0=bD[:, 0:w], scalar=cols[:, C_RFQ, i_:i_ + 1],
                                                  in1=cumr[:, 0:w], op0=ALU.mult, op1=ALU.subtract))
                    step(dve.tensor_tensor(sb_[:, i_ * P:w], sb_[:, i_ * P:w], neg_mask[:], ALU.add))
                    dve.tensor_reduce(nmax[:, i_:i_ + 1], sb_[:, 0:w], AX.X, ALU.max, negate=True)\
                        .then_inc(sem("nmax"), 1)

                def probs(i_):
                    w = (i_ + 1) * P
                    dve.wait_ge(sem("exp"), 4 * c + i_ + 1)
                    step(dve.reciprocal(rsum[:, i_:i_ + 1], lsum[:, i_:i_ + 1]))
                    dve.tensor_scalar(pr[:, 0:w], pr[:, 0:w], rsum[:, i_:i_ + 1], None, ALU.mult)\
                        .then_inc(sem("probs"), 1)

                def outs(i_):
                    if i_ == NT - 1:
                        dve.wait_ge(sem("fo_ps"), c + 1)
                        dve.tensor_scalar(br_b[:, bass.ds(c, 1), :].rearrange("p a t -> p (a t)"), bF[:], 1.0, None,
                                          ALU.mult).then_inc(sem("ob"), 1)

                stages = {"gates1": gates1, "gates2": gates2, "cola": cola, "colb": colb, "dif": dif, "dt": dt,
                          "frows": frows, "tkv": tkv, "kk": kk, "qk": qk, "z0": z0, "vk": vk, "osq": osq,
                          "orow": orow}
                for x in range(4):
                    stages[f"sl{x}"] = lambda x=x: silu(x)
                for x in range(3):
                    for w in range(4):
                        stages[f"cv{x}.{w}"] = lambda x=x, w=w: conv(x, w)
                for l in range(1, LEVELS):
                    stages[f"X{l}"] = lambda l=l: level_x(l)
                for n in range(NT):
                    stages[f"r{n}"] = lambda n=n: rec(n)
                    if 0 < n < NT - 1:
                        stages[f"v{n}"] = lambda n=n: rec_v(n)
                    stages[f"S{n}"] = lambda n=n: logits(n)
                    stages[f"P{n}"] = lambda n=n: probs(n)
                    stages[f"O{n}"] = lambda n=n: outs(n)
                run(tokens, stages, None, evac)
                if c is None:
                    round0_end.append(step.n)
                else:
                    assert step.n == DVE_STEPS - (LATE_STEPS if ph is ph_gates else 0), step.n

            head_rounds(dve, head_round)
            step.straight(round0_end[0] + HEADS * DVE_STEPS - LATE_STEPS)
            after_heads_dve(dve, step)

        @block.gpsimd
        def _(pool):
            pool.memset(mhalf[:], -0.5).then_inc(sem("mhalf"), 1)
            pool.wait_ge(sem("mhalf"), 1)
            for j in range(LEAD):
                split_lo(pool, ph_heads, 0, j)
            pool.wait_ge(sem("ld_small"), 80)
            norm_pool_scale(pool, 0)

            def head_round(tokens, i, c):
                ph, ph_i = (ph_gates, 0) if isinstance(i, int) and i == HEADS else (ph_heads, i)

                def slab(j, t):
                    if t == 0:
                        split_lo(pool, ph, ph_i, j + LEAD)

                def cols_():
                    pool.wait_ge(sem("ssc"), i + 1)
                    pool.tensor_tensor(rsc[:], ssc[:], mhalf[:], ALU.pow).then_inc(sem("rsc"), 1)

                def diag():
                    pool.wait_ge(sem("cols"), c + 1)
                    for dst, mat, col in ((d_g, upper, h_small[:, Q_G, :]), (d_b, ident, cols[:, C_BK, :]),
                                          (d_q, ident, cols[:, C_RQ, :]), (d_rk, ident, rsc[:, 12:16])):
                        pool.tensor_tensor(c4(dst[:]), over_tiles(mat[:]), over_cols(col), ALU.mult)\
                            .then_inc(sem("diag"), 1)
                    pool.tensor_tensor(c4(d_cum[:]), over_tiles(upper[:]), over_cols(h_small[:, Q_LF, :]), ALU.mult)\
                        .then_inc(sem("diag_part"), 1)
                    pool.wait_ge(sem("diag_part"), c + 1)
                    pool.tensor_tensor(c4(d_cum[:]), c4(d_cum[:]), over_cols(h_small[:, Q_LFPREV, :]), ALU.add)\
                        .then_inc(sem("diag"), 1)

                def level(l):
                    if l == 0:
                        pool.wait_ge(sem("masked"), 2 * c + 1)
                    elif l == 2:
                        pool.wait_ge(sem("z0"), c + 1)
                    elif l > 2:
                        pool.wait_ge(sem("y_ps"), 6 * c + l - 2)
                    pool.tensor_tensor(c4(atm[l % 2][:]), c4(a_t[:]), over_tiles(level_mask[:, l, :]), ALU.mult)\
                        .then_inc(sem("atm"), 1)

                def osq():
                    pool.wait_ge(sem("osc"), c + 1)
                    pool.tensor_tensor(ors[:], osc[:], mhalf[:, 0:NT], ALU.pow).then_inc(sem("ors"), 1)
                    pool.wait_ge(sem("ors"), c + 1)
                    pool.tensor_tensor(c4(d_b[:]), over_tiles(ident[:]), over_cols(ors[:]), ALU.mult)\
                        .then_inc(sem("odiag"), 1)

                stages = {"cola": cols_, "diag": diag, "osq": osq, "z0": lambda: (level(0), level(1))}
                for l in range(2, LEVELS):
                    stages[f"Y{l - 1}"] = lambda l=l: level(l)
                run(tokens, stages, slab, None)

            head_rounds(pool, head_round)
            after_heads_pool(pool)

    return nc


def slabs_of(weights):
    order = slab_order()
    out = np.zeros((len(order), P, KT, P), np.float32)
    for n, (name, k0, nk, col) in enumerate(order):
        w = weights[name][k0 * P:(k0 + nk) * P, col:col + P]
        out[n, :, :nk, :] = w.reshape(nk, P, P).transpose(1, 0, 2)
    return out.reshape(len(out), P, KT * P)


def constants():
    r, c = np.arange(P)[:, None], np.arange(P)[None, :]
    masks = [((c // b) % 2 == 1) & ((r // b) % 2 == 0) & (r // (2 * b) == c // (2 * b))
             for b in (2 ** l for l in range(LEVELS))]
    f = np.float32
    t = np.arange(T, dtype=f)

    def rotary(d):
        half = d // 2
        inv = (f(10000.0) ** (-np.arange(half, dtype=f) / f(half))).astype(f)
        ang = (t[None, :] * inv[:, None]).astype(f)
        feature = np.arange(P) % d
        sign = np.where(feature < half, -1.0, 1.0)[:, None].astype(f)
        return np.cos(ang)[feature % half].astype(f), (np.sin(ang)[feature % half] * sign).astype(f)

    cos_r, sin_r = rotary(P)
    cos_a, sin_a = rotary(64)
    log_gamma = np.log1p(-np.exp2(-5.0 - np.arange(RET_HEADS)))
    rel = (c - r)[:, None, :]
    decay_t = np.where(rel >= 0, np.exp(log_gamma[None, :, None] * np.maximum(rel, 0)), 0.0) * P ** -0.5
    q_decay = np.exp(log_gamma[None, :, None] * (np.arange(P)[None, None, :] + 1.0)) * P ** -0.5
    k_decay = np.stack([np.exp(log_gamma[None] * (P - 1.0 - np.arange(P)[:, None])),
                        np.broadcast_to(np.exp(log_gamma * P), (P, RET_HEADS))], 2)
    return {
        "cos_r": cos_r, "sin_r": sin_r, "cos_a": cos_a, "sin_a": sin_a,
        "swap_r": (c == (r + 64) % P).astype(f), "swap_a": (c == (r ^ 32)).astype(f),
        "dup0": (c % 64 == r).astype(f), "dup1": (c % 64 + 64 == r).astype(f),
        "decay_t": decay_t.astype(f), "q_decay": np.broadcast_to(q_decay, (P, RET_HEADS, P)).astype(f),
        "k_decay": k_decay.astype(f),
        "band": np.stack([np.where(c > r, 0.0, -1e30), np.where(c <= r, 0.0, -1e30)], 1).astype(f),
        "ident": np.eye(P, dtype=f),
        "upper": (r <= c).astype(f),
        "neg_mask": np.where(c <= r, 0.0, -1e30).astype(f),
        "level_mask": np.stack(masks, 1).astype(f),
    }


def arrays_of(inp):
    inp = {k: np.asarray(v) for k, v in inp.items()}
    w_in = inp["w_in"][0]
    g0 = 4 * D
    f0 = 4 * D + 16 + 3 * D
    gates = np.concatenate([w_in[:, g0:g0 + 16], w_in[:, f0:f0 + 8]], 1)

    b2 = inp["b_in_2"][0]

    def tiles(v):
        return v.reshape(KT, P).T

    a = {
        "x_t": np.ascontiguousarray(inp["x"][0].T),
        "slabs": slabs_of({k: inp[k][0] for k in (
            "w_in", "w_proj_gdn", "w_proj_fox", "w_out", "w_up", "w_down", "w_in_2", "w_ret_out_2", "w_attn_out_2",
            "w_out_2", "w_ffn_gate_2", "w_ffn_up_2", "w_ffn_down_2")}),
        "gains": np.stack([tiles(inp[k].reshape(-1)) for k in
                           ("norm_mix_g", "norm_mlp_g", "ln1_g_2", "ln2_g_2", "lnf_g_2")], 1),
        "head_gain": np.stack([inp[k][0] for k in ("gdn_norm_g", "fox_q_norm_g", "fox_k_norm_g")], 1),
        "w_gates": gates.reshape(KT, P, 24).transpose(1, 0, 2),
        "gate_rows": np.stack([inp["gdn_dt_bias"][0], inp["gdn_a_log"][0], inp["fox_f_bias"][0]])[None],
        "conv_w": inp["gdn_conv_w"][0].reshape(4, 3, HEADS, P).transpose(3, 2, 1, 0).reshape(P, HEADS, 12),
        **constants(),
        "bias_cols": np.stack([b2[c:c + P] for name, _, _, c in slab_order()
                               if name == "w_in_2" and c < 4352], 1),
        "bias_gate": b2[4352:].reshape(2 * KT, P).T,
        "ret_gain": inp["ret_norm_g_2"][0].reshape(RET_HEADS, 2, P).transpose(2, 0, 1),
        "sink_cols": np.broadcast_to(inp["attn_sinks_2"][0].reshape(RET_HEADS, 4), (P, RET_HEADS, 4)),
    }
    return {k: np.ascontiguousarray(v) for k, v in a.items()}


def kernel(**inputs):
    import concourse.bacc as bacc
    from concourse.bass_utils import run_bass_kernel_spmd

    nc = bacc.Bacc("TRN2", target_bir_lowering=False, num_devices=1)
    arrays = arrays_of(inputs)
    dram = {name: nc.dram_tensor(name, a.shape, mybir.dt.from_np(a.dtype), kind="ExternalInput").ap()
            for name, a in arrays.items()}
    out = nc.dram_tensor("out_t", (D, T), F32, kind="ExternalOutput").ap()
    program(nc, dram, out)
    r = run_bass_kernel_spmd(nc, [arrays], core_ids=[0])
    return np.ascontiguousarray(r.results[0]["out_t"].T)[None]
```
